# Optimizing a Trainium2 kernel written in Bass

```python
import math
import jax, jax.numpy as jnp
from jax import lax
import numpy as np
import jax
import jax.numpy as jnp

D_MODEL = 1024
BATCH = 1
SEQ = 512
DEPTH = 1

CTX_LEN = 256
GRID_W = 64
D_MIX = D_MODEL
D_ATTN = D_MIX // 2
D_CONV = D_MIX - D_ATTN
HEAD_DIM = 64
N_Q_HEADS = D_ATTN // HEAD_DIM
N_KV_HEADS = 2
GROUP = N_Q_HEADS // N_KV_HEADS
ROPE_AXIS_DIM = HEAD_DIM // 2
ROPE_THETA = 10000.0
Q_BLOCK = 128
CONV_WIDTH = 31
CONV_PAD = (CONV_WIDTH - 1) // 2
EPS = 1e-6

Q_LO, Q_HI = 0, D_ATTN
K_LO, K_HI = Q_HI, Q_HI + N_KV_HEADS * HEAD_DIM
V_LO, V_HI = K_HI, K_HI + N_KV_HEADS * HEAD_DIM
ZA_LO, ZA_HI = V_HI, V_HI + D_ATTN
GLU_LO, GLU_HI = ZA_HI, ZA_HI + 2 * D_CONV
ZC_LO, ZC_HI = GLU_HI, GLU_HI + D_CONV
D_IN = ZC_HI


def rms_norm(x, w):
    xf = x.astype(jnp.float32)
    y = xf * lax.rsqrt(jnp.mean(xf * xf, axis=-1, keepdims=True) + EPS)
    return (y * w.astype(jnp.float32)).astype(x.dtype)

def layer_norm(x, w, b):
    xf = x.astype(jnp.float32)
    mu = jnp.mean(xf, axis=-1, keepdims=True)
    var = jnp.mean(jnp.square(xf - mu), axis=-1, keepdims=True)
    y = (xf - mu) * lax.rsqrt(var + EPS)
    return (y * w.astype(jnp.float32) + b.astype(jnp.float32)).astype(x.dtype)

def grid_angles(n_tokens, dtype):
    rows = n_tokens // GRID_W
    row = jnp.repeat(jnp.arange(rows, dtype=jnp.float32), GRID_W)
    col = jnp.tile(jnp.arange(GRID_W, dtype=jnp.float32), rows)
    freqs = ROPE_THETA ** (-jnp.arange(0, ROPE_AXIS_DIM, 2, dtype=jnp.float32) / ROPE_AXIS_DIM)
    ang_r = row[:, None] * freqs[None, :]
    ang_c = col[:, None] * freqs[None, :]
    return (jnp.cos(ang_r).astype(dtype), jnp.sin(ang_r).astype(dtype),
            jnp.cos(ang_c).astype(dtype), jnp.sin(ang_c).astype(dtype))

def rope_axis(x, cos, sin):
    cos = cos[None, :, None, :]
    sin = sin[None, :, None, :]
    x1, x2 = jnp.split(x, 2, axis=-1)
    return jnp.concatenate([x1 * cos - x2 * sin, x1 * sin + x2 * cos], axis=-1)

def rope_2d(x, angles):
    cr, sr, cc, sc = angles
    return jnp.concatenate([rope_axis(x[..., :ROPE_AXIS_DIM], cr, sr),
                            rope_axis(x[..., ROPE_AXIS_DIM:], cc, sc)], axis=-1)

def qk_heads(p, qn_w, kn_w):
    B, S, _ = p.shape
    q = p[..., Q_LO:Q_HI].reshape(B, S, N_Q_HEADS, HEAD_DIM)
    k = p[..., K_LO:K_HI].reshape(B, S, N_KV_HEADS, HEAD_DIM)
    v = p[..., V_LO:V_HI].reshape(B, S, N_KV_HEADS, HEAD_DIM)
    return rms_norm(q, qn_w), rms_norm(k, kn_w), v

def kv_heads(p_kv, kn_w):
    B, S, _ = p_kv.shape
    kv = p_kv.reshape(B, S, 2, N_KV_HEADS, HEAD_DIM)
    return rms_norm(kv[:, :, 0], kn_w), kv[:, :, 1]

def attend_blocked(q, k, v):
    B, S, _, _ = q.shape
    scale = 1.0 / math.sqrt(HEAD_DIM)
    qb = q.reshape(B, S // Q_BLOCK, Q_BLOCK, N_KV_HEADS, GROUP, HEAD_DIM).transpose(1, 0, 2, 3, 4, 5)

    def one_block(qblk):
        s = jnp.einsum('bqkgd,bskd->bkgqs', qblk, k).astype(jnp.float32) * scale
        pr = jax.nn.softmax(s, axis=-1).astype(v.dtype)
        return jnp.einsum('bkgqs,bskd->bqkgd', pr, v)

    o = lax.map(one_block, qb)
    return o.transpose(1, 0, 2, 3, 4, 5).reshape(B, S, D_ATTN)

def attend_dense(q, k, v):
    B, C, _, _ = q.shape
    qg = q.reshape(B, C, N_KV_HEADS, GROUP, HEAD_DIM)
    s = jnp.einsum('bqkgd,bskd->bkgqs', qg, k).astype(jnp.float32) / math.sqrt(HEAD_DIM)
    pr = jax.nn.softmax(s, axis=-1).astype(v.dtype)
    return jnp.einsum('bkgqs,bskd->bqkgd', pr, v).reshape(B, C, D_ATTN)

def conformer_conv(glu_in, conv_w, conv_b, ln_w, ln_b, w_pw, b_pw):
    a, g = jnp.split(glu_in, 2, axis=-1)
    u = a * jax.nn.sigmoid(g)
    y = lax.conv_general_dilated(u, conv_w[:, None, :].astype(u.dtype), window_strides=(1,),
                                 padding=[(CONV_PAD, CONV_PAD)],
                                 dimension_numbers=('NWC', 'WIO', 'NWC'),
                                 feature_group_count=D_CONV) + conv_b
    y = jax.nn.silu(layer_norm(y, ln_w, ln_b))
    return y @ w_pw + b_pw

def first_inputs(seed: int = 0) -> dict:
    key = jax.random.key(seed)
    ks = jax.random.split(key, 20)
    nrm = jax.random.normal
    f32 = jnp.float32
    return {
        "x": nrm(ks[0], (BATCH, SEQ, D_MODEL), f32),
        "c": nrm(ks[1], (BATCH, D_MODEL), f32),
        "ctx": nrm(ks[2], (BATCH, CTX_LEN, D_MODEL), f32),
        "c_ctx": nrm(ks[3], (D_MODEL,), f32),
        "w_mod": nrm(ks[4], (DEPTH, D_MODEL, 3 * D_MODEL), f32) * D_MODEL ** -0.5,
        "b_mod": nrm(ks[5], (DEPTH, 3 * D_MODEL), f32) * 0.02,
        "norm_w": 1.0 + 0.05 * nrm(ks[6], (DEPTH, D_MODEL), f32),
        "w_in": nrm(ks[7], (DEPTH, D_MODEL, D_IN), f32) * D_MODEL ** -0.5,
        "q_norm_w": 1.0 + 0.05 * nrm(ks[8], (DEPTH, HEAD_DIM), f32),
        "k_norm_w": 1.0 + 0.05 * nrm(ks[9], (DEPTH, HEAD_DIM), f32),
        "conv_w": nrm(ks[10], (DEPTH, CONV_WIDTH, D_CONV), f32) * CONV_WIDTH ** -0.5,
        "conv_b": nrm(ks[11], (DEPTH, D_CONV), f32) * 0.02,
        "conv_ln_w": 1.0 + 0.05 * nrm(ks[12], (DEPTH, D_CONV), f32),
        "conv_ln_b": nrm(ks[13], (DEPTH, D_CONV), f32) * 0.02,
        "w_pw": nrm(ks[14], (DEPTH, D_CONV, D_CONV), f32) * D_CONV ** -0.5,
        "b_pw": nrm(ks[15], (DEPTH, D_CONV), f32) * 0.02,
        "w_out": nrm(ks[16], (DEPTH, D_MIX, D_MODEL), f32) * D_MIX ** -0.5,
    }

def first_block(x, c, ctx, c_ctx, w_mod, b_mod, norm_w, w_in, q_norm_w, k_norm_w,
              conv_w, conv_b, conv_ln_w, conv_ln_b, w_pw, b_pw, w_out):
    S = x.shape[1]
    angles = grid_angles(S, x.dtype)
    h, hc = x, ctx
    for l in range(DEPTH):
        mod = jax.nn.silu(c) @ w_mod[l] + b_mod[l]
        shift, scale, gate = jnp.split(mod, 3, axis=-1)
        mod_c = jax.nn.silu(c_ctx) @ w_mod[l] + b_mod[l]
        shift_c, scale_c, gate_c = jnp.split(mod_c, 3, axis=-1)

        u = rms_norm(h, norm_w[l]) * (1.0 + scale[:, None, :]) + shift[:, None, :]
        uc = rms_norm(hc, norm_w[l]) * (1.0 + scale_c) + shift_c

        p = u @ w_in[l]
        q, k, v = qk_heads(p, q_norm_w[l], k_norm_w[l])
        q = rope_2d(q, angles)
        k = rope_2d(k, angles)

        if l == DEPTH - 1:
            k_c, v_c = kv_heads(uc @ w_in[l][:, K_LO:V_HI], k_norm_w[l])
        else:
            pc = uc @ w_in[l]
            q_c, k_c, v_c = qk_heads(pc, q_norm_w[l], k_norm_w[l])
            attn_c = attend_dense(q_c, k_c, v_c) * jax.nn.silu(pc[..., ZA_LO:ZA_HI])
            conv_c = conformer_conv(pc[..., GLU_LO:GLU_HI], conv_w[l], conv_b[l], conv_ln_w[l],
                                    conv_ln_b[l], w_pw[l], b_pw[l]) * jax.nn.silu(pc[..., ZC_LO:ZC_HI])
            out_c = jnp.concatenate([attn_c, conv_c], axis=-1) @ w_out[l]

        k_all = jnp.concatenate([k_c, k], axis=1)
        v_all = jnp.concatenate([v_c, v], axis=1)
        attn = attend_blocked(q, k_all, v_all) * jax.nn.silu(p[..., ZA_LO:ZA_HI])

        conv = conformer_conv(p[..., GLU_LO:GLU_HI], conv_w[l], conv_b[l], conv_ln_w[l],
                              conv_ln_b[l], w_pw[l], b_pw[l]) * jax.nn.silu(p[..., ZC_LO:ZC_HI])

        out = jnp.concatenate([attn, conv], axis=-1) @ w_out[l]
        h = h + gate[:, None, :] * out
        if l < DEPTH - 1:
            hc = hc + gate_c * out_c
    return h


DEPTH_2 = 2

BLOCK_Q = 128
LN_EPS = 1e-5
N_SB_HEADS = D_MODEL // (2 * HEAD_DIM)
N_DSA_HEADS = D_MODEL // (2 * HEAD_DIM)
N_IDX_HEADS = 4
IDX_DIM = 64
DSA_TOPK_MAX = 256
N_DIFF_HEADS = D_MODEL // (2 * HEAD_DIM)
DIFF_DIM = HEAD_DIM
D_FF = ((-(-8 * D_MODEL // 3)) + 255) // 256 * 256
SB_W = N_SB_HEADS * HEAD_DIM
DSA_W = N_DSA_HEADS * HEAD_DIM
EVEN_SPLITS = (SB_W, SB_W, SB_W, DSA_W, HEAD_DIM, HEAD_DIM, N_IDX_HEADS * IDX_DIM, IDX_DIM, N_IDX_HEADS)
EVEN_IN = sum(EVEN_SPLITS)
EVEN_OUT = SB_W + DSA_W
DIFF_W = N_DIFF_HEADS * 2 * DIFF_DIM
N_EVEN = (DEPTH_2 + 1) // 2
N_ODD = DEPTH_2 // 2
ALPHA = (2 * DEPTH_2) ** 0.25
BETA = (8 * DEPTH_2) ** -0.25


F32 = jnp.float32

def layer_norm_2(x, g, b):
    x32 = x.astype(F32)
    mu = jnp.mean(x32, axis=-1, keepdims=True)
    var = jnp.mean(jnp.square(x32 - mu), axis=-1, keepdims=True)
    return ((x32 - mu) * lax.rsqrt(var + LN_EPS) * g.astype(F32) + b.astype(F32)).astype(x.dtype)

def rms_norm_2(x, g):
    x32 = x.astype(F32)
    ms = jnp.mean(jnp.square(x32), axis=-1, keepdims=True)
    return (x32 * lax.rsqrt(ms + LN_EPS) * g.astype(F32)).astype(x.dtype)

def rope_tables(positions, dim):
    inv = ROPE_THETA ** (-jnp.arange(0, dim, 2, dtype=F32) / dim)
    ang = positions.astype(F32)[..., None] * inv
    return jnp.cos(ang)[:, :, None, :], jnp.sin(ang)[:, :, None, :]

def apply_rope(t, cos, sin):
    t32 = t.astype(F32)
    half = t.shape[-1] // 2
    t1, t2 = t32[..., :half], t32[..., half:]
    return jnp.concatenate([t1 * cos - t2 * sin, t2 * cos + t1 * sin], axis=-1).astype(t.dtype)

def to_blocks(t):
    b, s = t.shape[:2]
    return t.reshape((b, s // BLOCK_Q, BLOCK_Q) + t.shape[2:]).swapaxes(0, 1)

def from_blocks(o):
    nb, b, bq = o.shape[:3]
    return o.swapaxes(0, 1).reshape((b, nb * bq) + o.shape[3:])

def stick_breaking_attention(q, k, v):
    s_len, d = q.shape[1], q.shape[-1]
    scale = d ** -0.5
    key_pos = jnp.arange(s_len)

    def block(args):
        qb, start = args
        z = jnp.einsum('bqhd,bshd->bhqs', qb, k, preferred_element_type=F32) * scale
        qpos = start + jnp.arange(BLOCK_Q)
        past = key_pos[None, :] < qpos[:, None]
        log_keep = jnp.where(past, jax.nn.log_sigmoid(-z), 0.0)
        suffix = lax.cumsum(log_keep, axis=3, reverse=True) - log_keep
        w = jnp.where(past, jnp.exp(jax.nn.log_sigmoid(z) + suffix), 0.0)
        return jnp.einsum('bhqs,bshd->bqhd', w.astype(v.dtype), v)

    starts = jnp.arange(s_len // BLOCK_Q) * BLOCK_Q
    return from_blocks(lax.map(block, (to_blocks(q), starts)))

def dsa_attention(q, k, v, q_idx, k_idx, w_idx):
    s_len, d = q.shape[1], q.shape[-1]
    topk = min(DSA_TOPK_MAX, s_len // 4)
    key_pos = jnp.arange(s_len)
    gather = jax.vmap(lambda t, i: t[i])

    def block(args):
        qb, qib, wb, start = args
        qpos = start + jnp.arange(BLOCK_Q)
        causal = key_pos[None, :] <= qpos[:, None]
        logits = jnp.einsum('bqhe,bse->bhqs', qib, k_idx, preferred_element_type=F32) * IDX_DIM ** -0.5
        score = jnp.einsum('bhqs,bqh->bqs', jax.nn.relu(logits), wb.astype(F32))
        score = jnp.where(causal[None], score, -jnp.inf)
        _, sel = lax.top_k(score, topk)
        valid = sel <= qpos[None, :, None]
        kg = gather(k, sel)
        vg = gather(v, sel)
        s = jnp.einsum('bqhd,bqkd->bhqk', qb, kg, preferred_element_type=F32) * d ** -0.5
        s = jnp.where(valid[:, None], s, -jnp.inf)
        p = jax.nn.softmax(s, axis=-1)
        return jnp.einsum('bhqk,bqkd->bqhd', p.astype(vg.dtype), vg)

    starts = jnp.arange(s_len // BLOCK_Q) * BLOCK_Q
    return from_blocks(lax.map(block, (to_blocks(q), to_blocks(q_idx), to_blocks(w_idx), starts)))

def diff_attention(q, k, v, lam):
    s_len, d = q.shape[1], q.shape[-1]
    key_pos = jnp.arange(s_len)

    def block(args):
        qb, start = args
        qpos = start + jnp.arange(BLOCK_Q)
        causal = key_pos[None, :] <= qpos[:, None]
        s = jnp.einsum('bqhcd,bshcd->bhcqs', qb, k, preferred_element_type=F32) * d ** -0.5
        p = jax.nn.softmax(jnp.where(causal, s, -jnp.inf), axis=-1)
        a = p[:, :, 0] - lam * p[:, :, 1]
        return jnp.einsum('bhqs,bshe->bqhe', a.astype(v.dtype), v)

    starts = jnp.arange(s_len // BLOCK_Q) * BLOCK_Q
    return from_blocks(lax.map(block, (to_blocks(q), starts)))

def even_mixer(h, cos, sin, w_in, w_out):
    b, s, _ = h.shape
    idx, acc = [], 0
    for width in EVEN_SPLITS[:-1]:
        acc += width
        idx.append(acc)
    q_sb, k_sb, v_sb, q_dsa, k_dsa, v_dsa, q_ix, k_ix, w_ix = jnp.split(h @ w_in, idx, axis=-1)
    o_sb = stick_breaking_attention(q_sb.reshape(b, s, N_SB_HEADS, HEAD_DIM),
                                    k_sb.reshape(b, s, N_SB_HEADS, HEAD_DIM),
                                    v_sb.reshape(b, s, N_SB_HEADS, HEAD_DIM))
    o_dsa = dsa_attention(apply_rope(q_dsa.reshape(b, s, N_DSA_HEADS, HEAD_DIM), cos, sin),
                          apply_rope(k_dsa[:, :, None], cos, sin)[:, :, 0],
                          v_dsa,
                          apply_rope(q_ix.reshape(b, s, N_IDX_HEADS, IDX_DIM), cos, sin),
                          apply_rope(k_ix[:, :, None], cos, sin)[:, :, 0],
                          w_ix * N_IDX_HEADS ** -0.5)
    o = jnp.concatenate([o_sb.reshape(b, s, SB_W), o_dsa.reshape(b, s, DSA_W)], axis=-1)
    return o @ w_out

def odd_mixer(h, cos, sin, w_in, lam_q1, lam_k1, lam_q2, lam_k2, subln_g, w_out, lambda_init):
    b, s, _ = h.shape
    q, k, v = jnp.split(h @ w_in, 3, axis=-1)
    q = apply_rope(q.reshape(b, s, 2 * N_DIFF_HEADS, DIFF_DIM), cos, sin).reshape(b, s, N_DIFF_HEADS, 2, DIFF_DIM)
    k = apply_rope(k.reshape(b, s, 2 * N_DIFF_HEADS, DIFF_DIM), cos, sin).reshape(b, s, N_DIFF_HEADS, 2, DIFF_DIM)
    v = v.reshape(b, s, N_DIFF_HEADS, 2 * DIFF_DIM)
    lam = (jnp.exp(jnp.sum(lam_q1.astype(F32) * lam_k1.astype(F32)))
           - jnp.exp(jnp.sum(lam_q2.astype(F32) * lam_k2.astype(F32))) + lambda_init)
    o = diff_attention(q, k, v, lam)
    o = rms_norm_2(o, subln_g) * (1.0 - lambda_init)
    return o.reshape(b, s, DIFF_W) @ w_out

def swiglu(h, w_gate, w_up, w_down):
    return (jax.nn.silu(h @ w_gate) * (h @ w_up)) @ w_down

def second_inputs(seed: int = 0) -> dict:
    key = jax.random.key(seed)
    ks = jax.random.split(key, 24)

    def nrm(i, shape, scale):
        return jax.random.normal(ks[i], shape, F32) * scale

    return {
        'x': nrm(0, (BATCH, SEQ, D_MODEL), 1.0),
        'c': nrm(1, (BATCH, D_MODEL), 1.0),
        'positions': jnp.broadcast_to(jnp.arange(SEQ, dtype=jnp.int32), (BATCH, SEQ)),
        'w_mod': nrm(2, (DEPTH_2, D_MODEL, 6 * D_MODEL), 0.1 * D_MODEL ** -0.5),
        'b_mod': nrm(3, (DEPTH_2, 6 * D_MODEL), 0.01),
        'w_in_even': nrm(4, (N_EVEN, D_MODEL, EVEN_IN), D_MODEL ** -0.5),
        'w_out_even': nrm(5, (N_EVEN, EVEN_OUT, D_MODEL), BETA * EVEN_OUT ** -0.5),
        'w_in_odd': nrm(6, (N_ODD, D_MODEL, 3 * DIFF_W), D_MODEL ** -0.5),
        'lam_q1': nrm(7, (N_ODD, DIFF_DIM), 0.1),
        'lam_k1': nrm(8, (N_ODD, DIFF_DIM), 0.1),
        'lam_q2': nrm(9, (N_ODD, DIFF_DIM), 0.1),
        'lam_k2': nrm(10, (N_ODD, DIFF_DIM), 0.1),
        'subln_g': 1.0 + nrm(11, (N_ODD, 2 * DIFF_DIM), 0.02),
        'w_out_odd': nrm(12, (N_ODD, DIFF_W, D_MODEL), BETA * DIFF_W ** -0.5),
        'ln_mix_g': 1.0 + nrm(13, (DEPTH_2, D_MODEL), 0.02),
        'ln_mix_b': nrm(14, (DEPTH_2, D_MODEL), 0.02),
        'w_gate': nrm(15, (DEPTH_2, D_MODEL, D_FF), D_MODEL ** -0.5),
        'w_up': nrm(16, (DEPTH_2, D_MODEL, D_FF), D_MODEL ** -0.5),
        'w_down': nrm(17, (DEPTH_2, D_FF, D_MODEL), BETA * D_FF ** -0.5),
        'ln_ffn_g': 1.0 + nrm(18, (DEPTH_2, D_MODEL), 0.02),
        'ln_ffn_b': nrm(19, (DEPTH_2, D_MODEL), 0.02),
    }

def second_block(x, c, positions, w_mod, b_mod, w_in_even, w_out_even, w_in_odd, lam_q1, lam_k1,
              lam_q2, lam_k2, subln_g, w_out_odd, ln_mix_g, ln_mix_b, w_gate, w_up, w_down,
              ln_ffn_g, ln_ffn_b):
    cos, sin = rope_tables(positions, HEAD_DIM)
    mod = jnp.einsum('bd,ldm->lbm', jax.nn.silu(c), w_mod) + b_mod[:, None, :]
    for i in range(DEPTH_2):
        sh_m, sc_m, g_m, sh_f, sc_f, g_f = [t[:, None, :] for t in jnp.split(mod[i], 6, axis=-1)]
        h = x * (1.0 + sc_m) + sh_m
        if i % 2 == 0:
            y = even_mixer(h, cos, sin, w_in_even[i // 2], w_out_even[i // 2])
        else:
            j = i // 2
            lambda_init = 0.8 - 0.6 * math.exp(-0.3 * i)
            y = odd_mixer(h, cos, sin, w_in_odd[j], lam_q1[j], lam_k1[j], lam_q2[j], lam_k2[j],
                          subln_g[j], w_out_odd[j], lambda_init)
        x = layer_norm_2(ALPHA * x + (1.0 + g_m) * y, ln_mix_g[i], ln_mix_b[i])
        h = x * (1.0 + sc_f) + sh_f
        y = swiglu(h, w_gate[i], w_up[i], w_down[i])
        x = layer_norm_2(ALPHA * x + (1.0 + g_f) * y, ln_ffn_g[i], ln_ffn_b[i])
    return x


def setup_inputs(seed=0):
    out = dict(first_inputs(seed))
    for name, value in second_inputs(seed + 1).items():
        if name != "x":
            out[name + "_2"] = value
    return out


def reference(
    x, c, ctx, c_ctx, w_mod, b_mod, norm_w, w_in, q_norm_w, k_norm_w, conv_w, conv_b, conv_ln_w,
    conv_ln_b, w_pw, b_pw, w_out, c_2, positions_2, w_mod_2, b_mod_2, w_in_even_2, w_out_even_2,
    w_in_odd_2, lam_q1_2, lam_k1_2, lam_q2_2, lam_k2_2, subln_g_2, w_out_odd_2, ln_mix_g_2,
    ln_mix_b_2, w_gate_2, w_up_2, w_down_2, ln_ffn_g_2, ln_ffn_b_2,
):
    x = first_block(
        x, c, ctx, c_ctx, w_mod, b_mod, norm_w, w_in, q_norm_w, k_norm_w, conv_w, conv_b,
        conv_ln_w, conv_ln_b, w_pw, b_pw, w_out,
    )
    return second_block(
        x, c_2, positions_2, w_mod_2, b_mod_2, w_in_even_2, w_out_even_2, w_in_odd_2, lam_q1_2,
        lam_k1_2, lam_q2_2, lam_k2_2, subln_g_2, w_out_odd_2, ln_mix_g_2, ln_mix_b_2, w_gate_2,
        w_up_2, w_down_2, ln_ffn_g_2, ln_ffn_b_2,
    )


_drawn_inputs = setup_inputs


def setup_inputs(seed=0):
    import zlib

    import numpy as np

    out = dict(_drawn_inputs(seed))
    spreads = {}
    factors = {'ctx': 3.462,
     'b_mod': 3.222,
     'norm_w': 3.027,
     'q_norm_w': 8.0,
     'k_norm_w': 8.0,
     'conv_b': 7.337,
     'conv_ln_w': 4.039,
     'conv_ln_b': 8.0,
     'b_pw': 6.151,
     'b_mod_2': 3.605,
     'lam_q1_2': 5.914,
     'lam_k1_2': 4.616,
     'lam_q2_2': 4.326,
     'lam_k2_2': 8.0,
     'subln_g_2': 23.225}
    for name, (base, spread) in spreads.items():
        noise = np.random.default_rng([zlib.crc32(name.encode()), seed]).standard_normal(out[name].shape)
        drawn = base * np.exp(spread * noise) if base else spread * noise
        out[name] = jnp.asarray(drawn.astype(out[name].dtype))
    for name, factor in factors.items():
        out[name] = (out[name] * factor).astype(out[name].dtype)
    return out
```

```python
from contextlib import ExitStack

import numpy as np
import concourse.bass as bass
from concourse import mybir

ALU = mybir.AluOpType
ACT = mybir.ActivationFunctionType
AX = mybir.AxisListType
F32 = mybir.dt.float32
F32R = mybir.dt.float32r
BF16 = mybir.dt.bfloat16
I32 = mybir.dt.int32

P = 128
SEQ, CTX, D = 512, 256, 1024
TT, CT, KT = SEQ // P, CTX // P, D // P
HD = 64
NH, NKV = 8, 2
WCOL = 256
GW = 512
TAPS = 31
PAD = (TAPS - 1) // 2
EPS = 1e-6

VC, VCC, VC2, VBM, VNW, VCB, VLW, VLB, VBP = 0, 8, 16, 24, 48, 56, 60, 64, 68
NV1 = 72
VBM2 = NV1
NV2 = 96
VLMG, VLMB, VLFG, VLFB = 168, 184, 200, 216
NV3 = 64
VCW = NV1 + NV2 + NV3
NCOL = VCW + 4 * TAPS

N_GLU, N_Q, N_KV, N_ZA, N_ZC, N_PW, N_WO = 0, 4, 6, 7, 9, 11, 13
EVEN, FF = 2500, 2816
SBQ, SBK, SBV, DSQ, DSK, DSV, IXQ, IXK, IXW = 0, 512, 1024, 1536, 2048, 2112, 2176, 2432, 2496
EORD = (8, 9, 6, 7, 0, 1, 2, 3, 4, 5)
TOPK = 128
BIG = -1e30
LOWEST = -3.0e38
ALPHA = 4 ** 0.25
LN_EPS = 1e-5
_c1 = 6.28125
_c2 = float(np.floor((2 * np.pi - _c1) * 2 ** 20) / 2 ** 20)
PI2 = (_c1, _c2, float(2 * np.pi - _c1 - _c2))
PI_LOW = 3.1415925
LAMBDA_INIT = 0.8 - 0.6 * float(np.exp(-0.3))
ZOFF = (0, 512, 1024, 896)

U_U, U_UC, U_Y, U_AT, U_CV, U_B2 = 0, 8, 16, 20, 24, 28
U_LN = (36, 44, 52)


def program(nc, t, out):
    ctx = ExitStack()
    with ctx:
        def sb(name, shape, dt=F32):
            return ctx.enter_context(nc.sbuf_tensor(name, shape, dt))

        def sem(name):
            return ctx.enter_context(nc.semaphore(name))

        xT = sb("xT", [P, KT, SEQ])
        uH = sb("uH", [P, KT, SEQ], F32R)
        uL = sb("uL", [P, KT, SEQ], F32R)
        wraw = sb("wraw", [P, 2, KT * WCOL])
        whi = sb("whi", [P, 2, KT * WCOL], F32R)
        wlo = sb("wlo", [P, 2, KT * WCOL], F32R)
        mraw = sb("mraw", [P, 2, 2, GW])
        cols = sb("cols", [P, NCOL])
        cpad = sb("cpad", [P, 2, KT, 32])
        mrow = sb("mrow", [P, P])
        mod1 = sb("mod1", [P, 24, 2])
        mod2 = sb("mod2", [P, 96])
        tmp = sb("tmp", [P, 2, SEQ])
        ident = sb("ident", [P, P])
        identB = sb("identB", [P, P], BF16)
        cmask = sb("cmask", [P, P], BF16)
        onesD = sb("onesD", [P, P])
        ropet = sb("ropet", [P, 2, TT, 32])
        lam = sb("lam", [P, 8])
        fcol = sb("fcol", [P, 4, 4, 8])
        posi = sb("posi", [P, TT], I32)
        ifr = sb("ifr", [P, 32])
        g1p = sb("g1p", [P, 4, 8])
        small = sb("small", [P, 256])
        base = nc.sbuf_base

        ps = ctx.enter_context(nc.psum_tensor("ps", [P, 8, 512], F32))
        acc, X, modp = ps[:, 0:4, :], ps[:, 4:7, :], ps[:, 7, :]

        wT = [[w[:, s, :].rearrange("p (k n) -> p k n", k=KT) for s in range(2)] for w in (wraw, whi, wlo)]
        wT4 = [[w[:, s, 0:4 * WCOL].rearrange("p (k n) -> p k n", k=4) for s in range(2)] for w in (wraw, whi, wlo)]
        pair = [acc[:, 2 * p:2 * p + 2, :].rearrange("p a n -> p (a n)") for p in range(2)]
        fmx, fsum, finv = small[:, 216:224], small[:, 224:232], small[:, 232:240]
        oTp = [X[:, 0, :], X[:, 1, :], X[:, 2, :], modp[:, :]]
        scS = small[:, 0:8]
        scC = small[:, 8:16]
        ssq = small[:, 16:22]
        rstd = small[:, 22:28]
        qss = small[:, 32:76]
        qrs = small[:, 76:120]
        nmx = small[:, 120:152]
        rsum = small[:, 152:184]
        rinv = small[:, 184:216]

        vec_in, x_in, ctx_in, tab_in, out_sem = sem("vec_in"), sem("x_in"), sem("ctx_in"), sem("tab_in"), sem("out_sem")
        w_landed = [sem("w_landed0"), sem("w_landed1")]
        m_landed = [sem("m_landed0"), sem("m_landed1")]
        hi_done, lo_done, chunk_done = sem("hi_done"), sem("lo_done"), sem("chunk_done")
        acc_read = [sem("acc_read0"), sem("acc_read1")]
        consts, vecT, cols_rd, cpad_rd = sem("consts"), sem("vecT"), sem("cols_rd"), sem("cpad_rd")
        tick_done, mrow_rd, modT, mod_rd = sem("tick_done"), sem("mrow_rd"), sem("modT"), sem("mod_rd")
        ssq_rd, rin_rd, rstd_rd, xn_rd, sc_rd = sem("ssq_rd"), sem("rin_rd"), sem("rstd_rd"), sem("xn_rd"), sem("sc_rd")
        xjob, x_read = sem("xjob"), sem("x_read")
        u_tmp, u_hi, u_lo = sem("u_tmp"), sem("u_hi"), sem("u_lo")
        ctx_read, sq_rd, qv_rd, qrs_rd, rope_rd = sem("ctx_read"), sem("sq_rd"), sem("qv_rd"), sem("qrs_rd"), sem("rope_rd")
        qkT, qk_hi, qk_lo, kz_rd = sem("qkT"), sem("qk_hi"), sem("qk_lo"), sem("kz_rd")
        s_rd, mx_rd, p_rd, t_rd, pt_rd, pv_rd, o_rd = [sem(n) for n in ("s_rd", "mx_rd", "p_rd", "t_rd", "pt_rd", "pv_rd", "o_rd")]
        conv_rd, cmean, cd_rd, csq_rd, cvar, crin, crs, ct_rd = [sem(n) for n in (
            "conv_rd", "cmean", "cd_rd", "csq_rd", "cvar", "crin", "crs", "ct_rd")]
        oT = sem("oT")
        ax_rd, ang_rd, sin_rd, odd_in = sem("ax_rd"), sem("ang_rd"), sem("sin_rd"), sem("odd_in")
        rp_rd, zero_rd, ixT, ix_hi, ix_lo, ixs_rd, ixr_rd, ix_acc, msk_rd = [sem(n) for n in (
            "rp_rd", "zero_rd", "ixT", "ix_hi", "ix_lo", "ixs_rd", "ixr_rd", "ix_acc", "msk_rd")]
        jobT, job_hi, job_lo = sem("jobT"), sem("job_hi"), sem("job_lo")
        z_rd, zmin_rd, zexp_rd, zln_rd, sp_rd, arg_rd, wgt_rd, sv_rd, so_rd = [sem(n) for n in (
            "z_rd", "zmin_rd", "zexp_rd", "zln_rd", "sp_rd", "arg_rd", "wgt_rd", "sv_rd", "so_rd")]
        ds_rd, dmx_rd, dp_rd, dt_rd, dpv_rd, do_rd = [sem(n) for n in ("ds_rd", "dmx_rd", "dp_rd", "dt_rd", "dpv_rd", "do_rd")]
        dpt_rd = [sem("dpt_rd0"), sem("dpt_rd1")]
        aoT, ao_hi, ao_lo = sem("aoT"), sem("ao_hi"), sem("ao_lo")
        ln_mean, ln_d, ln_sq, ln_var, ln_rin, ln_rs, ln_t = [sem(n) for n in (
            "ln_mean", "ln_d", "ln_sq", "ln_var", "ln_rin", "ln_rs", "ln_t")]
        silu_rd, h_hi, h_lo = sem("silu_rd"), sem("h_hi"), sem("h_lo")
        lam_rd, fs_rd, fmx_rd, fp_rd, fa_rd, ft_rd, fpv_rd, fo_rd = [sem(n) for n in (
            "lam_rd", "fs_rd", "fmx_rd", "fp_rd", "fa_rd", "ft_rd", "fpv_rd", "fo_rd")]
        fp2_rd, wsc_rd = sem("fp2_rd"), sem("wsc_rd")
        fpt_rd = [sem("fpt_rd0"), sem("fpt_rd1")]
        sln_sq, sln_v, sln_rs, sln_rd, sln_g = sem("sln_sq"), sem("sln_v"), sem("sln_rs"), sem("sln_rd"), sem("sln_g")
        fin_T, fin_rd = sem("fin_T"), sem("fin_rd")
        vch, ach, gch = sem("vector_chain"), sem("scalar_chain"), sem("gpsimd_chain")

        b1 = ExitStack()

        def s1(name, shape, dt=F32):
            return b1.enter_context(nc.sbuf_tensor(name, shape, dt))

        def overlay(specs):
            with ExitStack() as o:
                return [o.enter_context(nc.sbuf_tensor(name, shape, dt)) for name, shape, dt in specs]

        xtok, ctok, xn = overlay([("xtok", [P, TT, D], F32), ("ctok", [P, CT, D], F32), ("xn", [P, TT, D], F32)])
        sq, = overlay([("pad_sq", [P, 8192], F32), ("sq", [P, 2816], F32)])[1:]
        sqt, sqk = sq[:, 0:2048], sq[:, 2048:2816]
        kdup, = overlay([("pad_kd", [P, 8192 + 1536], F32), ("kdup", [P, 6, 2, 2, HD], F32)])[1:]
        sgt, = overlay([("pad_sg", [P, 8192], F32), ("sgt", [P, 2, SEQ], F32)])[1:]
        otok, = overlay([("otok", [P, TT, D], F32)])
        sz = s1("sz", [P, 8, SEQ])
        qH = s1("qH", [P, 4, SEQ], F32R)
        qL = s1("qL", [P, 4, SEQ], F32R)
        ptb = s1("ptb", [P, 2, 768])
        ptT = s1("ptT", [P, 2, 768])
        gt, = overlay([("gt", [P, 4, 256], F32)])
        ucH = s1("ucH", [P, KT, CTX], F32R)
        ucL = s1("ucL", [P, KT, CTX], F32R)
        flatH, flatL = (w[:, :, :].rearrange("p k n -> p (k n)") for w in (ucH, ucL))
        kH, kL = (w[:, :, :].rearrange("p k n -> p (k n)")[:, 0:3072].rearrange("p (e g n) -> p e g n", e=2, g=2)
                  for w in (uH, uL))
        yH, yL = (w.rearrange("p (k n) -> p k n", k=4) for w in (flatH, flatL))
        utp = s1("utp", [P, 4, SEQ + 2 * PAD])
        vr1, cwr = overlay([("vr1", [P, 3, P], F32), ("cwr", [P, 512], F32)])
        cy = s1("cy", [P, 4, SEQ])
        qtok = s1("qtok", [P, TT, 512])
        kvt = s1("kvt", [P, 6, 256])
        qkw = s1("qkw", [P, 2, HD])

        b1.close()

        e2 = ExitStack()

        def s2(name, shape, dt=F32):
            return e2.enter_context(nc.sbuf_tensor(name, shape, dt))

        T0 = s2("T0", [P, TT, EVEN])
        kid = s2("kid", [P, TT, 2, HD])
        kdd = s2("kdd", [P, TT, 2, HD])
        score = s2("score", [P, 3, SEQ])
        work = s2("work", [P, 3, SEQ])
        ptd = s2("ptd", [P, 2, SEQ])
        ge, = overlay([("ge", [P, 4, 256], F32)])
        ptdT = s2("ptdT", [P, 2, SEQ])
        Mk = s2("Mk", [P, 3, SEQ], BF16)
        wsc = s2("wsc", [P, TT, 4])
        smask = s2("smask", [P, P], BF16)
        negtri = s2("negtri", [P, P])
        negone = s2("negone", [P, P])
        m8 = s2("m8", [P, 3, 8])
        cnt = s2("cnt", [P, 3, 2])
        ixr, = overlay([("ixr", [P, 2, SEQ], F32)])
        ixH, ixL, izH, izL = overlay([("pad_iz", [P, 1024], F32)] + [(n, [P, 2, SEQ], F32R) for n in
                                                                     ("ixH", "ixL", "izH", "izL")])[1:]
        zw = s2("zw", [P, 2, 1280])
        spt = s2("spt", [P, 2, 1280])
        e2.close()

        hH, hL = overlay([("hH", [P, 22, SEQ], F32R), ("hL", [P, 22, SEQ], F32R)])

        o2 = ExitStack()

        def s3(name, shape, dt=F32):
            return o2.enter_context(nc.sbuf_tensor(name, shape, dt))

        T1 = s3("T1", [P, TT, 3 * D])
        pdf = s3("pdf", [P, 2, 2, SEQ])
        pdT = s3("pdT", [P, 2, SEQ])
        g1t = s3("g1t", [P, 4, 512])
        g2t = s3("g2t", [P, 4, 512])
        subg = s3("subg", [P, P])
        lv = s3("lv", [P, 4, HD])
        o2.close()

        w_in, w_out, w_pw = t["w_in"][0], t["w_out"][0], t["w_pw"][0]
        k_lo, v_hi, za, glu, zc = 512, 768, 768, 1280, 2304

        def cut(w, c0, n=WCOL):
            return w[:, c0:c0 + n].rearrange("(k p) n -> p k n", p=P)

        sources = []
        for j in range(2):
            sources += [cut(w_in, glu + 512 + WCOL * j), cut(w_in, glu + WCOL * j)]
        sources += [cut(w_in, WCOL * j) for j in range(2)] + [cut(w_in, k_lo)]
        sources += [cut(w_in, za + WCOL * j) for j in range(2)] + [cut(w_in, zc + WCOL * j) for j in range(2)]
        sources += [cut(w_pw, WCOL * j) for j in range(2)]
        sources += [cut(w_out, WCOL * j) for j in range(4)]
        even, odd = t["w_in_even_2"][0], t["w_in_odd_2"][0]
        sources += [cut(even, WCOL * j, min(WCOL, EVEN - WCOL * j)) for j in EORD]
        sources += [cut(t["w_out_even_2"][0], WCOL * j) for j in range(4)]
        N_UP = {0: len(sources), 1: len(sources) + 34 + 16}
        N_DN = {l: N_UP[l] + 22 for l in range(2)}
        N_ODD = N_DN[0] + 12
        A_DN = {0: N_DN[0], 1: N_DN[1] - 8}

        def ffn_sources(l):
            up = []
            for i in range(11):
                up += [cut(t["w_gate_2"][l], WCOL * i), cut(t["w_up_2"][l], WCOL * i)]
            dn = t["w_down_2"][l]
            for j in range(4):
                for c in range(3):
                    k0, k1 = 8 * c, min(8 * c + 8, 22)
                    up.append(dn[k0 * P:k1 * P, WCOL * j:WCOL * j + WCOL].rearrange("(k p) n -> p k n", p=P))
            return up

        sources += ffn_sources(0)
        sources += [cut(odd, WCOL * j) for j in range(12)]
        sources += [cut(t["w_out_odd_2"][0], WCOL * j) for j in range(4)]
        sources += ffn_sources(1)
        assert N_ODD == N_UP[1] - 16 and len(sources) == N_DN[1] + 12
        NC1 = N_WO + 4
        NCH = len(sources)

        def ticks_of(n):
            if n in (N_PW - 1, N_PW):
                return (0, 1, 2, 3) if n == N_PW - 1 else ()
            if n == NC1 - 1 or n >= N_UP[0]:
                return ()
            m = n if n < NC1 else n - 1
            return (2 * (m % 2), 2 * (m % 2) + 1)

        def group_of(n):
            return 4 + n // 2 if n < NC1 else 12 + (n - NC1) // 2

        def use_of(n):
            if n < N_DN[0]:
                return n
            return N_DN[0] + (n - N_DN[0]) // 3 if n < N_ODD else (n - 8 if n < N_DN[1] else A_DN[1] + (n - N_DN[1]) // 3)

        def acc_tile(eng, a, m):
            counted = a // 2 + 1 - (1 if a > N_PW + 1 else 0)
            eng.wait_ge(acc_read[a % 2], 2 * counted - 1 + m)

        def acc_count(a):
            return 2 * (a // 2 + 1 - (1 if a > N_PW + 1 else 0))

        def slot_full(eng, n):
            eng.wait_ge(w_landed[n % 2], 16 * (n // 2 + 1))

        def acc_gone(eng, a):
            counted = a // 2 + 1 - (1 if a > N_PW + 1 else 0)
            eng.wait_ge(acc_read[a % 2], 2 * counted)

        block = ctx.enter_context(nc.Block())

        @block.sync
        def _(sp):
            def load_chunk(n):
                if n >= 2:
                    sp.wait_ge(lo_done, n - 1)
                src = sources[n]
                dst = wT4[0] if N_PW <= n < N_WO else wT[0]
                sp.dma_start(dst[n % 2][:, 0:src.shape[1], 0:src.shape[2]], src).then_inc(w_landed[n % 2], 16)

            def load_tick(g, kp):
                k = 4 * g + kp
                if k >= 2:
                    sp.wait_ge(tick_done, k - 1)
                src = t["w_mod"][0] if g < 6 else t["w_mod_2"][(g - 6) // 12]
                c0 = GW * (g if g < 6 else (g - 6) % 12)
                sp.dma_start(mraw[:, k % 2], src[256 * kp:256 * kp + 256, c0:c0 + GW]
                             .rearrange("(k p) n -> p k n", p=P)).then_inc(m_landed[k % 2], 16)

            row = lambda ap: ap.rearrange("(r f) -> r f", f=P)
            for r, ap in ((VC, t["c"][0]), (VCC, t["c_ctx"]), (VC2, t["c_2"][0]), (VBM, t["b_mod"][0]),
                          (VNW, t["norm_w"][0]), (VCB, t["conv_b"][0]), (VLW, t["conv_ln_w"][0]),
                          (VLB, t["conv_ln_b"][0]), (VBP, t["b_pw"][0])):
                v = row(ap)
                sp.dma_start(vr1[r:r + v.shape[0], 0], v).then_inc(vec_in, 16)
            sp.dma_start(vr1[0:NV2, 1], t["b_mod_2"].rearrange("l (r f) -> (l r) f", f=P)).then_inc(vec_in, 16)
            for r, name in ((0, "ln_mix_g_2"), (16, "ln_mix_b_2"), (32, "ln_ffn_g_2"), (48, "ln_ffn_b_2")):
                sp.dma_start(vr1[r:r + 16, 2], t[name].rearrange("l (r f) -> (l r) f", f=P)).then_inc(vec_in, 16)
            sp.dma_start(cwr[0:TAPS, :], t["conv_w"][0]).then_inc(vec_in, 16)
            for kp in range(2):
                load_tick(0, kp)
            for tt in range(TT):
                sp.dma_start(xtok[:, tt], t["x"][0, tt * P:tt * P + P, :]).then_inc(x_in, 16)
            sp.dma_start(ctok[:, :, :], t["ctx"][0].rearrange("(t p) n -> p t n", p=P)).then_inc(ctx_in, 16)
            for g in range(4):
                for kp in range(2 if g == 0 else 0, 4):
                    load_tick(g, kp)
                if g == 0:
                    sp.dma_start(ropet[:, 0], t["cos1"].rearrange("(t p) n -> p t n", p=P)).then_inc(tab_in, 16)
                    sp.dma_start(ropet[:, 1], t["sin1"].rearrange("(t p) n -> p t n", p=P)).then_inc(tab_in, 16)
                    sp.dma_start(qkw[:, 0], t["q_norm_w"].to_broadcast([P, HD])).then_inc(tab_in, 16)
                    for tt in range(TT):
                        sp.dma_start(posi[:, tt:tt + 1], t["positions_2"][0, tt * P:tt * P + P]
                                     .rearrange("(p o) -> p o", o=1)).then_inc(tab_in, 16)
                    sp.dma_start(ifr[:, :], t["inv2"].to_broadcast([P, 32])).then_inc(tab_in, 16)
                    sp.dma_start(qkw[:, 1], t["k_norm_w"].to_broadcast([P, HD])).then_inc(tab_in, 16)
                if g == 1:
                    load_chunk(0)
                    load_chunk(1)
            for n in range(N_UP[0]):
                load_chunk(n + 2)
                for kp in ticks_of(n):
                    load_tick(group_of(n), kp)

            def up_loads(l):
                def tick_load(i, kp):
                    sp.wait_ge(tick_done, 4 * i + (4 * 19 + kp - 1))
                    sp.dma_start(mraw[:, kp % 2], t["w_mod_2"][1][256 * kp:256 * kp + 256, bass.ds(i * GW + GW, GW)]
                                 .rearrange("(k p) n -> p k n", p=P)).then_inc(m_landed[kp % 2], 16)

                with sp.Fori(0, 10) as i:
                    for e, w in ((0, "w_gate_2"), (1, "w_up_2")):
                        p = (N_UP[l] + e) % 2
                        sp.wait_ge(lo_done, 2 * i + (N_UP[l] + e + 1))
                        sp.dma_start(wT[0][p], t[w][l][:, bass.ds(i * WCOL + WCOL, WCOL)]
                                     .rearrange("(k p) n -> p k n", p=P)).then_inc(w_landed[p], 16)
                        if l == 0:
                            for kp in (2 * e, 2 * e + 1):
                                tick_load(i, kp)
                for e in range(2):
                    load_chunk(N_DN[l] + e)
                    if l == 0:
                        for kp in (2 * e, 2 * e + 1):
                            load_tick(29, kp)

            up_loads(0)
            for n in range(N_DN[0], N_UP[1]):
                load_chunk(n + 2)
                if n == N_ODD:
                    sp.wait_ge(chunk_done, N_ODD)
                    sp.dma_start(subg[:, :], t["subln_g_2"].to_broadcast([P, P])).then_inc(odd_in, 16)
                    for k, name in enumerate(("lam_q1_2", "lam_k1_2", "lam_q2_2", "lam_k2_2")):
                        sp.dma_start(lv[:, k], t[name].to_broadcast([P, HD])).then_inc(odd_in, 16)
            up_loads(1)
            for n in range(N_DN[1], NCH - 2):
                load_chunk(n + 2)
            for tt in range(TT):
                sp.wait_ge(fin_rd, tt + 1)
                sp.dma_start(out[0, tt * P:tt * P + P, :], otok[:, tt]).then_inc(out_sem, 16)
            sp.wait_ge(out_sem, 16 * TT)

        @block.gpsimd
        def _(pool):
            g = nc.gpsimd
            n = [0]

            def link(ins):
                n[0] += 1
                ins.then_inc(gch, 1)
                pool.wait_ge(gch, n[0])

            g.memset(onesD[:], 1.0 / D)
            g.memset(cpad[:], 0.0)
            g.memset(utp[:], 0.0)
            link(g.memset(ident[:], 0.0))
            g.affine_select(out=ident[:], in_=ident[:], compare_op=ALU.not_equal, fill=1.0, base=0,
                            pattern=[[-1, P]], channel_multiplier=1).then_inc(consts, 1)
            g.memset(identB[:], 0.0)
            link(g.memset(cmask[:], 0.0))
            g.affine_select(out=identB[:], in_=identB[:], compare_op=ALU.not_equal, fill=1.0, base=0,
                            pattern=[[-1, P]], channel_multiplier=1).then_inc(consts, 1)
            g.affine_select(out=cmask[:], in_=cmask[:], compare_op=ALU.is_ge, fill=BIG, base=0,
                            pattern=[[-1, P]], channel_multiplier=1).then_inc(consts, 1)

            pool.wait_ge(tab_in, 144)
            pool.wait_ge(qrs_rd, 1)
            qv = qtok[:, :, :].rearrange("p t (h d) -> p t h d", d=HD)
            kv = kvt[:, :, 0:P].rearrange("p t (h d) -> p t h d", d=HD)
            for tt in range(TT):
                link(g.tensor_tensor(qv[:, tt], qv[:, tt],
                                     qrs[:, tt * NH:tt * NH + NH].unsqueeze(2).to_broadcast([P, NH, HD]), ALU.mult))
                link(g.tensor_tensor(qv[:, tt], qv[:, tt],
                                     qkw[:, 0:1, :].to_broadcast([P, NH, HD]), ALU.mult))
            for tt in range(6):
                link(g.tensor_tensor(kv[:, tt], kv[:, tt],
                                     qrs[:, 32 + 2 * tt:34 + 2 * tt].unsqueeze(2).to_broadcast([P, 2, HD]), ALU.mult))
                link(g.tensor_tensor(kv[:, tt], kv[:, tt],
                                     qkw[:, 1:2, :].to_broadcast([P, 2, HD]), ALU.mult))
            for tt in range(TT):
                for heads, src, dsts in ((2, kvt[:, 2 + tt, 0:P], [0, 1]), (NH, qtok[:, tt], None)):
                    v = src.rearrange("p (h a z f) -> p h a z f", a=2, z=2, f=16)
                    one, two = v[:, :, :, 0, :], v[:, :, :, 1, :]
                    w = heads * 32
                    tm = [gt[:, i, 0:w].rearrange("p (h a f) -> p h a f", a=2, f=16) for i in range(4)]
                    cs, sn = [ropet[:, i, tt].rearrange("p (o a f) -> p o a f", o=1, a=2)
                              .to_broadcast([P, heads, 2, 16]) for i in range(2)]
                    link(g.tensor_tensor(tm[0], one, cs, ALU.mult))
                    link(g.tensor_tensor(tm[1], two, sn, ALU.mult))
                    link(g.tensor_tensor(tm[2], one, sn, ALU.mult))
                    link(g.tensor_tensor(tm[3], two, cs, ALU.mult))
                    if dsts is None:
                        link(g.tensor_tensor(one, tm[0], tm[1], ALU.subtract))
                        link(g.tensor_tensor(two, tm[2], tm[3], ALU.add))
                    else:
                        for e in dsts:
                            d = kdup[:, 2 + tt, :, e, :].rearrange("p h (a z f) -> p h a z f", a=2, z=2)
                            link(g.tensor_tensor(d[:, :, :, 0, :], tm[0], tm[1], ALU.subtract))
                            link(g.tensor_tensor(d[:, :, :, 1, :], tm[2], tm[3], ALU.add))
            for c in range(CT):
                for e in range(2):
                    last = g.tensor_copy(kdup[:, c, :, e, :], kv[:, c])
                    if c < CT - 1 or e == 0:
                        link(last)
            last.then_inc(rope_rd, 1)
            pool.wait_ge(chunk_done, N_PW)
            pool.wait_ge(rope_rd, 1)
            for i in range(4):
                half = slice(HD, P) if i % 2 == 0 else slice(0, HD)
                g.memset((kH, kL)[i // 2][half, i % 2].bitcast(F32), 0.0).then_inc(kz_rd, 1)
                pool.wait_ge(kz_rd, i + 1)

            def turn_heads(src, heads, tm_, tt, out2=None):
                v = src.rearrange("p (h z f) -> p h z f", z=2, f=32)
                one, two = v[:, :, 0, :], v[:, :, 1, :]
                tm = [tm_[:, i, 0:heads * 32].rearrange("p (h f) -> p h f", f=32) for i in range(4)]
                cs, sn = [ropet[:, i, tt:tt + 1].to_broadcast([P, heads, 32]) for i in range(2)]
                link(g.tensor_tensor(tm[0], one, cs, ALU.mult))
                link(g.tensor_tensor(tm[1], two, sn, ALU.mult))
                link(g.tensor_tensor(tm[2], one, sn, ALU.mult))
                link(g.tensor_tensor(tm[3], two, cs, ALU.mult))
                for o1, o2_ in ([(one, two)] if out2 is None else [(out2[:, e, 0:32].unsqueeze(1), out2[:, e, 32:64].unsqueeze(1)) for e in range(2)]):
                    link(g.tensor_tensor(o1, tm[0], tm[1], ALU.subtract))
                    link(g.tensor_tensor(o2_, tm[2], tm[3], ALU.add))

            pool.wait_ge(sin_rd, 2)
            acc_gone(pool, NC1)
            acc_gone(pool, NC1 + 1)
            for tt in range(TT):
                turn_heads(T0[:, tt, IXQ:IXK], 4, ge, tt)
                turn_heads(T0[:, tt, IXK:IXW], 1, ge, tt, kid[:, tt])
                turn_heads(T0[:, tt, DSK:DSV], 1, ge, tt, kdd[:, tt])
            for i in range(4):
                half, e = (slice(HD, P), 0) if i % 2 == 0 else (slice(0, HD), 1)
                link(g.memset((izH, izL)[i // 2][half, e].bitcast(F32), 0.0))
            link(g.memset(negtri[:], -1.0))
            g.affine_select(out=negtri[:], in_=negtri[:], compare_op=ALU.is_ge, fill=0.0, base=0,
                            pattern=[[-1, P]], channel_multiplier=1)
            g.memset(negone[:], -1.0)
            link(g.memset(smask[:], 0.0))
            g.affine_select(out=smask[:], in_=smask[:], compare_op=ALU.is_gt, fill=BIG, base=0,
                            pattern=[[1, P]], channel_multiplier=-1).then_inc(rp_rd, 1)
            pool.wait_ge(rp_rd, 1)
            acc_gone(pool, NC1 + 2)
            acc_gone(pool, NC1 + 3)
            for tt in range(TT):
                turn_heads(T0[:, tt, DSQ:DSK], NH, ge, tt)

            def zero_keys(n, count):
                pool.wait_ge(chunk_done, n)
                for i in range(8):
                    w, sl, e = (uH, uL)[i // 4], (i // 2) % 2, i % 2
                    half = slice(HD, P) if e == 0 else slice(0, HD)
                    g.memset(w[half, 4 * sl + 1 + e].bitcast(F32), 0.0).then_inc(zero_rd, 1)
                    pool.wait_ge(zero_rd, count + i + 1)

            zero_keys(NC1 + 10, 0)
            for part in range(2):
                for c in range(4):
                    acc_gone(pool, use_of(N_ODD + 4 * part + c))
                for tt in range(TT):
                    turn_heads(T1[:, tt, part * D:part * D + D], 16, (g1t, g2t)[part], tt)
            zero_keys(N_ODD + 12, 8)

        @block.tensor
        def _(pe):
            mm, tr = nc.tensor.matmul, nc.tensor.transpose

            pe.wait_ge(vec_in, 16 * 15)
            pe.wait_ge(consts, 1)
            tr(X[:, 0, 0:NV1], vr1[0:NV1, 0], ident[0:NV1, 0:NV1])
            tr(X[:, 0, NV1:NV1 + NV2], vr1[0:NV2, 1], ident[0:NV2, 0:NV2])
            tr(X[:, 0, NV1 + NV2:VCW], vr1[0:NV3, 2], ident[0:NV3, 0:NV3])
            for j in range(4):
                last = tr(X[:, 0, VCW + TAPS * j:VCW + TAPS * j + TAPS], cwr[0:TAPS, j * P:j * P + P],
                          ident[0:TAPS, 0:TAPS])
            last.then_inc(vecT, 1)
            pe.wait_ge(cpad_rd, 1)

            def tick(g, kp):
                k = 4 * g + kp
                pe.wait_ge(m_landed[k % 2], 16 * (k // 2 + 1))
                if kp == 0 and g >= 1:
                    pe.wait_ge(mod_rd, g)
                c = 0 if g < 6 else 1
                for kk in range(2):
                    for j in range(4):
                        last = mm(modp[32 * j:32 * j + 32, 0:P], cpad[:, c, 2 * kp + kk, :],
                                  mraw[:, k % 2, kk, j * P:j * P + P],
                                  start=(kp == 0 and kk == 0), stop=(kp == 3 and kk == 1))
                last.then_inc(tick_done, 1)

            def turn_group(g):
                pe.wait_ge(mrow_rd, g + 1)
                tr(modp[:, P:2 * P], mrow[:], ident[:]).then_inc(modT, 1)

            for g in range(4):
                for kp in range(4):
                    tick(g, kp)
                turn_group(g)

            pe.wait_ge(x_in, 64)
            pe.wait_ge(cols_rd, 1)
            for f in range(24):
                i = f % 8
                if f == 8:
                    pe.wait_ge(xn_rd, 4)
                if f == 16:
                    pe.wait_ge(xn_rd, 6)
                if f >= 11:
                    pe.wait_ge(u_tmp, f - 10)
                elif f >= 3:
                    pe.wait_ge(x_read, f - 2)
                src = xtok if f < 8 else (xn if f < 16 else ctok)
                for tt in range(TT if f < 16 else CT):
                    s = src[:, tt, i * P:i * P + P]
                    last = tr(X[:, f % 3, tt * P:tt * P + P], s, ident[:])
                last.then_inc(xjob, 1)

            def product(n, a, nk, u0, xh, xl, w_hi, w_lo, turn=None, k0=0, first=True, done=True):
                pe.wait_ge(lo_done, n + 1)
                if a - 2 in (N_PW, N_PW + 1):
                    pe.wait_ge(u_tmp, U_CV + 2 * (a - 2 - N_PW) + 2)
                elif a >= 2 and first:
                    acc_gone(pe, a - 2)
                for m in range(2):
                    o = acc[:, 2 * (a % 2) + m, :]
                    if m == 1 and turn is not None:
                        turn_group(turn)
                    for k in range(nk):
                        if u0 is not None and m == 0:
                            pe.wait_ge(u_lo, u0 + k + 1)
                        h, l = w_hi[n % 2][:, k, m * P:m * P + P], w_lo[n % 2][:, k, m * P:m * P + P]
                        mm(o, h, xh[:, k0 + k], start=(first and k == 0), stop=False)
                        mm(o, h, xl[:, k0 + k], start=False, stop=False)
                        last = mm(o, l, xh[:, k0 + k], start=False, stop=(done and k == nk - 1))
                last.then_inc(chunk_done, 1)

            def by_token(o, n, nt, xh, xl, ncol=WCOL, turn=None):
                for tt in range(nt):
                    if tt == 1 and turn is not None:
                        turn_group(turn)
                    for k in range(KT):
                        h, l = whi_v[n % 2][:, k, 0:ncol], wlo_v[n % 2][:, k, 0:ncol]
                        oo = o[:, tt * WCOL:tt * WCOL + ncol]
                        xs = slice(tt * P, tt * P + P)
                        mm(oo, xh[:, k, xs], h, start=(k == 0), stop=False)
                        mm(oo, xh[:, k, xs], l, start=False, stop=False)
                        last = mm(oo, xl[:, k, xs], h, start=False, stop=(k == KT - 1))
                return last

            whi_v, wlo_v = wT[1], wT[2]
            for n in range(N_PW):
                turn = 3 + n // 2 if n and n % 2 == 0 else None
                if N_Q <= n < N_ZA:
                    pe.wait_ge(lo_done, n + 1)
                    acc_gone(pe, n - 2)
                    if n == N_KV:
                        pe.wait_ge(u_lo, U_UC + 8)
                        pe.wait_ge(u_tmp, 16)
                        by_token(X[:, 0, :], n, CT, ucH, ucL)
                    by_token(pair[n % 2], n, TT, uH, uL, turn=turn).then_inc(chunk_done, 1)
                else:
                    product(n, n, KT, U_U if n == 0 else None, uH, uL, wT[1], wT[2], turn)
                for kp in ticks_of(n):
                    tick(group_of(n), kp)

            pe.wait_ge(rope_rd, 1)
            pe.wait_ge(ctx_read, 1)
            for j in range(6):
                if j >= 1:
                    pe.wait_ge(qk_lo, j if j < 5 else 5)
                if j < 4:
                    for tt in range(TT):
                        last = tr(X[:, j % 2, tt * P:tt * P + P], qtok[:, tt, j * P:j * P + P], ident[:])
                else:
                    for c in range(6):
                        last = tr(X[:, c // 4, (c % 4) * P:(c % 4) * P + P],
                                  kdup[:, c, j - 4].rearrange("p e d -> p (e d)"), ident[:])
                last.then_inc(qkT, 1)

            pe.wait_ge(qk_lo, 6)
            pe.wait_ge(kz_rd, 4)
            acc_gone(pe, N_PW - 1)
            acc_gone(pe, N_PW - 2)

            def scores(i):
                h, qt = i // 4, i % 4
                if i >= 2:
                    pe.wait_ge(p_rd, i - 1)
                ql = slice(qt * P, qt * P + P)
                for c0, c1 in ((0, 512), (512, 768)):
                    o = pair[i % 2][:, c0:c1]
                    q_h, q_l = qH[:, h // 2, ql], qL[:, h // 2, ql]
                    k_h, k_l = kH[:, h % 2, h // 4, c0:c1], kL[:, h % 2, h // 4, c0:c1]
                    mm(o, q_h, k_h, start=True, stop=False)
                    mm(o, q_h, k_l, start=False, stop=False)
                    last = mm(o, q_l, k_h, start=False, stop=True)
                last.then_inc(s_rd, 1)

            def turn(i):
                pe.wait_ge(p_rd, i + 1)
                if i >= 1:
                    pe.wait_ge(pt_rd, 2 * i)
                for c in range(6):
                    last = tr(X[:, c // 4, (c % 4) * P:(c % 4) * P + P], ptb[:, i % 2, c * P:c * P + P], ident[:])
                last.then_inc(t_rd, 1)

            def values(i):
                h, qt = i // 4, i % 4
                o = X[:, 2, :] if h % 2 == 0 else modp[:, :]
                pe.wait_ge(pt_rd, 2 * i + 2)
                if qt == 0 and h >= 2:
                    pe.wait_ge(o_rd, h - 1)
                v0 = P + HD * (h // 4)
                for c in range(6):
                    last = mm(o[:, 256 + qt * HD:256 + qt * HD + HD], ptT[:, i % 2, c * P:c * P + P],
                              kvt[:, c, v0:v0 + HD], start=(c == 0), stop=(c == 5))
                last.then_inc(pv_rd, 1)

            NS = 4 * NH
            pe.wait_ge(mrow_rd, 10)
            scores(0)
            for i in range(NS):
                if i + 1 < NS:
                    scores(i + 1)
                if i >= 1:
                    values(i - 1)
                turn(i)
            values(NS - 1)

            pe.wait_ge(conv_rd, 4)
            for j in range(4):
                last = mm(acc[:, 0, :], onesD[:], cy[:, j], start=(j == 0), stop=(j == 3))
            last.then_inc(cmean, 1)
            pe.wait_ge(o_rd, NH)
            for j in range(4):
                for tt in range(TT):
                    last = tr(oTp[j][:, tt * P:tt * P + P], qtok[:, tt, j * P:j * P + P], ident[:])
                last.then_inc(oT, 1)
            for j in range(4):
                pe.wait_ge(csq_rd, j + 1)
                last = mm(acc[:, 1, :], onesD[:], sgt[:, j % 2], start=(j == 0), stop=(j == 3))
                last.then_inc(cvar, 1)
            for n in range(N_PW, NC1):
                turn = 3 + n // 2 if n % 2 == 0 else None
                if n == N_PW + 1:
                    pe.wait_ge(u_tmp, U_AT + 4)
                if n < N_WO:
                    product(n, n, 4, U_Y if n == N_PW else None, yH, yL, wT4[1], wT4[2], turn)
                else:
                    product(n, n, KT, U_AT if n == N_WO else None, uH, uL, wT[1], wT[2], turn)
                for kp in ticks_of(n):
                    tick(group_of(n), kp)

            for e in range(10):
                n = NC1 + e
                turn = group_of(n) - 1 if e % 2 == 0 and e else None
                pe.wait_ge(lo_done, n + 1)
                acc_gone(pe, n - 2)
                if e == 0:
                    pe.wait_ge(u_lo, U_B2 + 8)
                by_token(pair[n % 2], n, TT, uH, uL, min(WCOL, EVEN - WCOL * EORD[e]), turn=turn).then_inc(chunk_done, 1)
                for kp in ticks_of(n):
                    tick(group_of(n), kp)
                if e == 2:
                    pe.wait_ge(rp_rd, 1)
                    for j in range(3):
                        for tt in range(TT):
                            src = T0[:, tt, IXQ + j * P:IXQ + j * P + P] if j < 2 else \
                                kid[:, tt].rearrange("p e d -> p (e d)")
                            last = tr(X[:, j, tt * P:tt * P + P], src, ident[:])
                        last.then_inc(ixT, 1)
                if e == 3:
                    pe.wait_ge(ix_lo, 3)
                    for i in range(12):
                        q, h = i // 4 + 1, i % 4
                        if i >= 3:
                            pe.wait_ge(ixr_rd, i - 2)
                        o, w = X[:, i % 3, 0:(q + 1) * P], slice(0, (q + 1) * P)
                        q_h, q_l = ixH[:, h // 2, q * P:q * P + P], ixL[:, h // 2, q * P:q * P + P]
                        mm(o, q_h, izH[:, h % 2, w], start=True, stop=False)
                        mm(o, q_h, izL[:, h % 2, w], start=False, stop=False)
                        mm(o, q_l, izH[:, h % 2, w], start=False, stop=True).then_inc(ixs_rd, 1)

            def head_pair(k, q_of, k_of, wait_lo):
                for e, src in enumerate((q_of, k_of)):
                    j = 2 * k + e
                    if j >= 1:
                        pe.wait_ge(job_lo, j)
                    for tt in range(TT):
                        last = tr(ps[:, 7, tt * P:tt * P + P], src(tt), ident[:])
                    last.then_inc(jobT, 1)

            def sb_pair(p):
                head_pair(p, lambda tt: T0[:, tt, SBQ + p * P:SBQ + p * P + P],
                          lambda tt: T0[:, tt, SBK + p * P:SBK + p * P + P], None)

            def region(h):
                return ps[:, 3 * (h % 2):3 * (h % 2) + 3, :].rearrange("p b n -> p (b n)")

            def sb_scores(h):
                z, sl, e = region(h), 4 * ((h // 2) % 2), h % 2
                pe.wait_ge(job_lo, 2 * (h // 2) + 2)
                if h >= 2:
                    pe.wait_ge(wgt_rd, h - 1)
                for kt in range(4):
                    w = SEQ - kt * P
                    o = z[:, ZOFF[kt]:ZOFF[kt] + w]
                    ks, qs = slice(kt * P, kt * P + P), slice(kt * P, SEQ)
                    mm(o, uH[:, sl + 1 + e, ks], uH[:, sl, qs], start=(kt != 3), stop=False, skip_group_check=True)
                    mm(o, uH[:, sl + 1 + e, ks], uL[:, sl, qs], start=False, stop=False, skip_group_check=True)
                    mm(o, uL[:, sl + 1 + e, ks], uH[:, sl, qs], start=False, stop=False, skip_group_check=True)
                    last = mm(o[:, 0:P], identB[:], smask[:], start=False, stop=True, skip_group_check=True)
                last.then_inc(z_rd, 1)

            def sb_suffix(h):
                z, s_ = region(h), spt[:, h % 2]
                pe.wait_ge(sp_rd, h + 1)
                for kt in range(4):
                    for k2 in range(kt, 4):
                        w = SEQ - k2 * P
                        o0 = ZOFF[kt] + (k2 - kt) * P
                        last = mm(z[:, o0:o0 + w], negtri[:] if k2 == kt else negone[:], s_[:, ZOFF[k2]:ZOFF[k2] + w],
                                  start=False, stop=True, skip_group_check=True)
                last.then_inc(arg_rd, 1)

            def sb_values(h):
                pe.wait_ge(wgt_rd, h + 1)
                if h >= 1:
                    pe.wait_ge(so_rd, h)
                for q in range(TT):
                    for kt in range(q + 1):
                        o0 = ZOFF[kt] + (q - kt) * P
                        last = mm(ps[:, 6, q * HD:q * HD + HD], zw[:, h % 2, o0:o0 + P],
                                  T0[:, kt, SBV + h * HD:SBV + h * HD + HD], start=(kt == 0), stop=(kt == q))
                last.then_inc(sv_rd, 1)

            acc_gone(pe, NC1 + 9)
            acc_gone(pe, NC1 + 8)
            pe.wait_ge(mrow_rd, group_of(NC1 + 8) + 1)
            sb_pair(0)
            pe.wait_ge(zero_rd, 8)
            sb_scores(0)
            for h in range(NH):
                if h % 2 == 0 and h // 2 + 1 < 4:
                    sb_pair(h // 2 + 1)
                if h + 1 < NH:
                    sb_scores(h + 1)
                if h >= 1:
                    sb_values(h - 1)
                sb_suffix(h)
            sb_values(NH - 1)

            def dsa_pair(p):
                jobs = ([lambda tt: kdd[:, tt].rearrange("p e d -> p (e d)")] if p == 0 else []) + \
                       [lambda tt: T0[:, tt, DSQ + p * P:DSQ + p * P + P]]
                for e, src in enumerate(jobs):
                    j = 8 + (e if p == 0 else 1 + p)
                    pe.wait_ge(job_lo, j)
                    if j == 8:
                        pe.wait_ge(wgt_rd, NH)
                    for tt in range(TT):
                        last = tr(ps[:, 3, tt * P:tt * P + P], src(tt), ident[:])
                    last.then_inc(jobT, 1)

            def dsa_scores(i):
                h, q = i // 4, i % 4
                w = (q + 1) * P
                if i % 8 == 0:
                    pe.wait_ge(job_lo, 8 + 2 + h // 2)
                if i >= 3:
                    pe.wait_ge(dp_rd, i - 2)
                o, sl = ps[:, i % 3, 0:w], 4 * ((h // 2) % 2)
                q_h, q_l = uH[:, sl, q * P:q * P + P], uL[:, sl, q * P:q * P + P]
                k_h, k_l = uH[:, 1 + h % 2, 0:w], uL[:, 1 + h % 2, 0:w]
                mm(o, q_h, k_h, start=True, stop=False)
                mm(o, q_h, k_l, start=False, stop=False)
                mm(o, q_l, k_h, start=False, stop=False)
                mm(o, identB[:], cmask[:] if q == 0 else Mk[:, q - 1, 0:w], start=False, stop=True).then_inc(ds_rd, 1)

            def dsa_turn(i):
                q = i % 4
                pe.wait_ge(dp_rd, i + 1)
                if i >= 2:
                    pe.wait_ge(dpt_rd[i % 2], i // 2)
                for c in range(q + 1):
                    last = tr(ps[:, 4 + i % 2, c * P:c * P + P], ptd[:, i % 2, c * P:c * P + P], ident[:])
                last.then_inc(dt_rd, 1)

            def dsa_values(i):
                h, q = i // 4, i % 4
                pe.wait_ge(dpt_rd[i % 2], i // 2 + 1)
                if q == 0 and h >= 2:
                    pe.wait_ge(do_rd, h - 1)
                for c in range(q + 1):
                    last = mm(ps[:, 6 + h % 2, q * HD:q * HD + HD], ptdT[:, i % 2, c * P:c * P + P],
                              T0[:, c, DSV:DSV + HD], start=(c == 0), stop=(c == q))
                last.then_inc(dpv_rd, 1)

            pe.wait_ge(so_rd, NH)
            pe.wait_ge(msk_rd, 3)
            dsa_pair(0)
            dsa_scores(0)
            for i in range(NS):
                if i % 8 == 2 and i // 8 + 1 < 4:
                    dsa_pair(i // 8 + 1)
                if i + 1 < NS:
                    dsa_scores(i + 1)
                if i >= 1:
                    dsa_values(i - 1)
                dsa_turn(i)
            dsa_values(NS - 1)

            def mixer_out(l, src):
                for k in range(KT):
                    if k >= 3:
                        pe.wait_ge(ao_lo, 8 * l + k - 2)
                    for tt in range(TT):
                        last = tr(X[:, k % 3, tt * P:tt * P + P], src[:, tt, k * P:k * P + P], ident[:])
                    last.then_inc(aoT, 1)

            def mean(L, a, j):
                for m in range(2):
                    acc_tile(pe, a, m)
                    x = 2 * j + m
                    last = mm(X[:, 0, :], onesD[:], xT[:, x], start=(x == 0), stop=(x == 7))
                return last

            def out_product(L, l, n0):
                for j in range(4):
                    n = n0 + j
                    turn = group_of(n) - 1 if l == 0 and j % 2 == 0 else None
                    product(n, use_of(n), KT, None, uH, uL, wT[1], wT[2], turn)
                    if l == 0:
                        for kp in ticks_of(n):
                            tick(group_of(n), kp)
                    if j:
                        mean(L, use_of(n) - 1, j - 1)
                mean(L, use_of(n0 + 3), 3).then_inc(ln_mean, 1)

            def variance(L):
                for x in range(8):
                    pe.wait_ge(ln_sq, 8 * L + x + 1)
                    mm(X[:, 1, :], onesD[:], tmp[:, x % 2], start=(x == 0), stop=(x == 7)).then_inc(ln_var, 1)

            pe.wait_ge(do_rd, NH)
            mixer_out(0, T0)
            pe.wait_ge(ao_lo, 8)
            out_product(0, 0, NC1 + 10)
            variance(0)

            def feed_forward(l):
                n0, a0 = N_UP[l], use_of(N_UP[l])
                with pe.Fori(0, 11) as i:
                    for e in range(2):
                        p = (n0 + e) % 2
                        pa = (a0 + e) % 2
                        pe.wait_ge(lo_done, 2 * i + (n0 + e + 1))
                        pe.wait_ge(acc_read[pa], 2 * i + acc_count(a0 + e - 2))
                        for m in range(2):
                            if m == 1 and e == 0 and l == 0:
                                pe.wait_ge(mrow_rd, i + 19)
                                tr(modp[:, P:2 * P], mrow[:], ident[:]).then_inc(modT, 1)
                            o = acc[:, 2 * pa + m, :]
                            for k in range(KT):
                                if e == 0 and m == 0:
                                    pe.wait_ge(u_lo, U_LN[2 * l] + k + 1)
                                h_, l_ = wT[1][p][:, k, m * P:m * P + P], wT[2][p][:, k, m * P:m * P + P]
                                mm(o, h_, uH[:, k], start=(k == 0), stop=False)
                                mm(o, h_, uL[:, k], start=False, stop=False)
                                last = mm(o, l_, uH[:, k], start=False, stop=(k == KT - 1))
                        last.then_inc(chunk_done, 1)
                        if l == 0:
                            for kp in (2 * e, 2 * e + 1):
                                pe.wait_ge(m_landed[kp % 2], 32 * i + 16 * (2 * 19 + kp // 2 + 1))
                                if kp == 0:
                                    pe.wait_ge(mod_rd, i + 19)
                                for kk in range(2):
                                    for j in range(4):
                                        last = mm(modp[32 * j:32 * j + 32, 0:P], cpad[:, 1, 2 * kp + kk, :],
                                                  mraw[:, kp % 2, kk, j * P:j * P + P],
                                                  start=(kp == 0 and kk == 0), stop=(kp == 3 and kk == 1))
                                last.then_inc(tick_done, 1)
                if l == 0:
                    turn_group(29)
                for j in range(4):
                    a = A_DN[l] + j
                    for c in range(3):
                        n = N_DN[l] + 3 * j + c
                        if j == 0:
                            pe.wait_ge(h_lo, 11 * l + min(11, 4 * c + 4) + 1)
                        product(n, a, min(8, 22 - 8 * c), None, hH, hL, wT[1], wT[2], None, 8 * c, c == 0, c == 2)
                    if j:
                        mean(2 * l + 1, a - 1, j - 1)
                mean(2 * l + 1, A_DN[l] + 3, 3).then_inc(ln_mean, 1)
                variance(2 * l + 1)

            feed_forward(0)

            for e in range(12):
                n = N_ODD + e
                pe.wait_ge(lo_done, n + 1)
                acc_gone(pe, use_of(n) - 2)
                if e == 0:
                    pe.wait_ge(u_lo, U_LN[1] + 8)
                by_token(pair[use_of(n) % 2], n, TT, uH, uL).then_inc(chunk_done, 1)

            def diff_pair(h):
                for e in range(2):
                    j = 13 + 2 * h + e
                    pe.wait_ge(job_lo, j)
                    for tt in range(TT):
                        last = tr(ps[:, 7, tt * P:tt * P + P], T1[:, tt, e * D + h * P:e * D + h * P + P], ident[:])
                    last.then_inc(jobT, 1)

            def diff_scores(i):
                h, q = i // 4, i % 4
                w = (q + 1) * P
                sl = 4 * (h % 2)
                if q == 0:
                    pe.wait_ge(job_lo, 13 + 2 * h + 2)
                if i >= 2:
                    pe.wait_ge(fp_rd, i - 1)
                q_h, q_l = uH[:, sl, q * P:q * P + P], uL[:, sl, q * P:q * P + P]
                for c in range(2):
                    o = ps[:, 2 * (i % 2) + c, 0:w]
                    k_h, k_l = uH[:, sl + 1 + c, 0:w], uL[:, sl + 1 + c, 0:w]
                    mm(o, q_h, k_h, start=True, stop=False)
                    mm(o, q_h, k_l, start=False, stop=False)
                    mm(o, q_l, k_h, start=False, stop=False)
                    last = mm(o[:, q * P:w], identB[:], cmask[:], start=False, stop=True)
                last.then_inc(fs_rd, 1)

            def diff_turn(i):
                pe.wait_ge(fa_rd, i + 1)
                if i >= 2:
                    pe.wait_ge(fpt_rd[i % 2], i // 2)
                for c in range(i % 4 + 1):
                    last = tr(ps[:, 4 + i % 2, c * P:c * P + P], pdf[:, i % 2, 0, c * P:c * P + P], ident[:])
                last.then_inc(ft_rd, 1)

            def diff_values(i):
                h, q = i // 4, i % 4
                pe.wait_ge(fpt_rd[i % 2], i // 2 + 1)
                if q == 0 and h >= 1:
                    pe.wait_ge(fo_rd, h)
                for c in range(q + 1):
                    last = mm(ps[:, 6, q * P:q * P + P], pdT[:, i % 2, c * P:c * P + P],
                              T1[:, c, 2 * D + h * P:2 * D + h * P + P], start=(c == 0), stop=(c == q))
                last.then_inc(fpv_rd, 1)

            acc_gone(pe, use_of(N_ODD + 11))
            acc_gone(pe, use_of(N_ODD + 10))
            pe.wait_ge(zero_rd, 16)
            pe.wait_ge(mod_rd, 30)
            diff_pair(0)
            diff_scores(0)
            for i in range(NS):
                if i % 4 == 2 and i // 4 + 1 < NH:
                    diff_pair(i // 4 + 1)
                if i + 1 < NS:
                    diff_scores(i + 1)
                if i >= 1:
                    diff_values(i - 1)
                diff_turn(i)
            diff_values(NS - 1)
            pe.wait_ge(sln_g, 4)
            mixer_out(1, T1)
            pe.wait_ge(ao_lo, 16)
            out_product(2, 1, N_ODD + 12)
            variance(2)
            feed_forward(1)

            pe.wait_ge(ax_rd, 40)
            for tt in range(TT):
                if tt >= 2:
                    pe.wait_ge(fin_rd, tt - 1)
                for k in range(KT):
                    last = tr(pair[tt % 2][:, k * P:k * P + P], xT[:, k, tt * P:tt * P + P], ident[:])
                last.then_inc(fin_T, 1)

        @block.scalar
        def _(act):
            A = nc.scalar.activation
            n_ = [0]

            def link(ins):
                n_[0] += 1
                ins.then_inc(ach, 1)
                act.wait_ge(ach, n_[0])

            act.wait_ge(vecT, 1)
            A(cols[:], X[:, 0, 0:NCOL], ACT.Copy).then_inc(cols_rd, 1)
            act.wait_ge(cols_rd, 1)
            act.wait_ge(consts, 1)
            A(cpad[:, 0, :, 0], cols[:, VC:VC + 8], ACT.Silu)
            A(cpad[:, 0, :, 1], cols[:, VCC:VCC + 8], ACT.Silu)
            A(cpad[:, 1, :, 0], cols[:, VC2:VC2 + 8], ACT.Silu).then_inc(cpad_rd, 1)

            def split_high(n):
                slot_full(act, n)
                if n >= 2:
                    act.wait_ge(chunk_done, n - 1)
                A(whi[:, n % 2, :], wraw[:, n % 2, :], ACT.Copy).then_inc(hi_done, 1)

            def copy_group(g):
                act.wait_ge(tick_done, 4 * g + 4)
                if g >= 1:
                    act.wait_ge(modT, g)
                A(mrow[:], modp[:, 0:P], ACT.Copy).then_inc(mrow_rd, 1)

            def high(i, dst):
                act.wait_ge(u_tmp, i + 1)
                A(dst, tmp[:, i % 2, 0:dst.shape[-1]], ACT.Copy).then_inc(u_hi, 1)

            act.wait_ge(x_in, 64)
            act.wait_ge(ctx_in, 16)
            for tt in range(6):
                src = xtok[:, tt] if tt < 4 else ctok[:, tt - 4]
                if tt >= 4:
                    act.wait_ge(ssq_rd, tt - 3)
                A(xn[:, tt % 4], src, ACT.Square, accum_out=ssq[:, tt:tt + 1]).then_inc(ssq_rd, 1)
            copy_group(0)
            act.wait_ge(ssq_rd, 6)
            act.wait_ge(rin_rd, 1)
            A(rstd, rstd, ACT.Sqrt).then_inc(rstd_rd, 1)
            act.wait_ge(rstd_rd, 1)
            for tt in range(6):
                src = xtok[:, tt] if tt < 4 else ctok[:, tt - 4]
                A(xn[:, tt] if tt < 4 else ctok[:, tt - 4], src, ACT.Copy, scale=rstd[:, tt:tt + 1]).then_inc(xn_rd, 1)
            for g in range(1, 3):
                copy_group(g)
            split_high(0)
            copy_group(3)
            split_high(1)
            for f in range(8):
                act.wait_ge(xjob, f + 1)
                A(xT[:, f], X[:, f % 3, :], ACT.Copy).then_inc(x_read, 1)
            for i in range(8):
                high(U_U + i, uH[:, i])
            for i in range(8):
                high(U_UC + i, ucH[:, i])

            for n in range(N_PW):
                act.wait_ge(chunk_done, n + 1)
                if n in (0, 2):
                    if n == 2:
                        acc_gone(act, 1)
                    A(sgt[:], acc[:, 2 * (n % 2):2 * (n % 2) + 2, :], ACT.Sigmoid).then_inc(acc_read[n % 2], 2)
                elif N_Q <= n < N_KV:
                    c0 = WCOL * (n - N_Q)
                    A(qtok[:, 0:2, c0:c0 + WCOL], pair[n % 2][:, 0:512].rearrange("p (t n) -> p t n", t=2),
                      ACT.Copy).then_inc(acc_read[n % 2], 1)
                elif n == N_KV:
                    A(kvt[:, 2:4, :], pair[n % 2][:, 0:512].rearrange("p (t n) -> p t n", t=2),
                      ACT.Copy).then_inc(acc_read[n % 2], 1)
                    A(kvt[:, 0:2, :], X[:, 0, :].rearrange("p (t n) -> p t n", t=2), ACT.Copy).then_inc(ctx_read, 1)
                    acc_gone(act, N_KV)
                    acc_gone(act, N_KV - 1)
                    act.wait_ge(ctx_read, 1)
                    A(sqt, qtok[:, :, :].rearrange("p t n -> p (t n)"), ACT.Square).then_inc(sq_rd, 1)
                    A(sqk.rearrange("p (t n) -> p t n", t=6), kvt[:, :, 0:P], ACT.Square).then_inc(sq_rd, 1)
                elif n >= N_ZA:
                    if n == N_ZA:
                        act.wait_ge(qv_rd, 1)
                        A(qrs, qss, ACT.Sqrt).then_inc(qrs_rd, 1)
                    m = 2 * (n - N_ZA)
                    A(sz[:, m:m + 2, :], acc[:, 2 * (n % 2):2 * (n % 2) + 2, :], ACT.Silu)\
                        .then_inc(acc_read[n % 2], 2)
                split_high(n + 2)
                if 3 in ticks_of(n):
                    copy_group(group_of(n))

            act.wait_ge(chunk_done, N_PW)
            for j in range(6):
                act.wait_ge(qkT, j + 1)
                if j < 4:
                    A(qH[:, j], X[:, j % 2, :], ACT.Copy).then_inc(qk_hi, 1)
                else:
                    src = X[:, 0:2, :].rearrange("p a n -> p (a n)")[:, 0:768]
                    A(kH[0:HD, 0, j - 4], src[0:HD], ACT.Copy)
                    A(kH[HD:P, 1, j - 4], src[HD:P], ACT.Copy).then_inc(qk_hi, 1)

            NS = 4 * NH

            def exps(i):
                act.wait_ge(mx_rd, i + 1)
                if i >= 2:
                    act.wait_ge(t_rd, i - 1)
                A(ptb[:, i % 2, :], pair[i % 2][:, 0:768], ACT.Exp, bias=nmx[:, i:i + 1],
                  accum_out=rsum[:, i:i + 1]).then_inc(p_rd, 1)

            def move(i):
                act.wait_ge(t_rd, i + 1)
                if i >= 2:
                    act.wait_ge(pv_rd, i - 1)
                A(ptT[:, i % 2, 512:768], X[:, 1, 0:256], ACT.Copy).then_inc(pt_rd, 1)

            exps(0)
            for i in range(NS):
                if i + 1 < NS:
                    exps(i + 1)
                move(i)

            for j in range(4):
                act.wait_ge(cd_rd, j + 1)
                if j >= 2:
                    act.wait_ge(cvar, j - 1)
                A(sgt[:, j % 2], cy[:, j], ACT.Square).then_inc(csq_rd, 1)
            act.wait_ge(crin, 1)
            A(utp[:, 0, 0:SEQ], utp[:, 0, 0:SEQ], ACT.Sqrt).then_inc(crs, 1)
            for j in range(4):
                i = U_Y + j
                act.wait_ge(ct_rd, j + 1)
                act.wait_ge(u_lo, i - 1)
                A(tmp[:, i % 2], cy[:, j], ACT.Silu, bias=cols[:, VLB + j:VLB + j + 1],
                  scale=cols[:, VLW + j:VLW + j + 1]).then_inc(u_tmp, 1)
                high(i, yH[:, j])
            for j in range(4):
                high(U_AT + j, uH[:, j])
            for n in range(N_PW, NC1):
                act.wait_ge(chunk_done, n + 1)
                if n < N_WO:
                    for m in range(2):
                        j = 2 * (n - N_PW) + m
                        high(U_CV + j, uH[:, 4 + j])
                split_high(n + 2)
                if 3 in ticks_of(n):
                    copy_group(group_of(n))
            act.wait_ge(ang_rd, 1)
            A(ropet[:, 0].rearrange("p t f -> p (t f)"), ropet[:, 0].rearrange("p t f -> p (t f)"), ACT.Sin).then_inc(sin_rd, 1)
            A(ropet[:, 1].rearrange("p t f -> p (t f)"), ropet[:, 1].rearrange("p t f -> p (t f)"), ACT.Sin).then_inc(sin_rd, 1)
            for i in range(8):
                high(U_B2 + i, uH[:, i])
                A(xT[:, i], xT[:, i], ACT.Copy, scale=ALPHA).then_inc(ax_rd, 1)
            for e in range(10):
                n = NC1 + e
                c0 = WCOL * EORD[e]
                w = min(WCOL, EVEN - c0)
                act.wait_ge(chunk_done, n + 1)
                A(T0[:, 0:2, c0:c0 + w], pair[n % 2][:, 0:512].rearrange("p (t n) -> p t n", t=2)[:, :, 0:w],
                  ACT.Copy).then_inc(acc_read[n % 2], 1)
                split_high(n + 2)
                if 3 in ticks_of(n):
                    copy_group(group_of(n))
                if e == 2:
                    for j in range(3):
                        act.wait_ge(ixT, j + 1)
                        if j < 2:
                            A(ixH[:, j], X[:, j, :], ACT.Copy, scale=0.125).then_inc(ix_hi, 1)
                        else:
                            A(izH[0:HD, 0], X[0:HD, j, :], ACT.Copy)
                            A(izH[HD:P, 1], X[HD:P, j, :], ACT.Copy).then_inc(ix_hi, 1)
                if e == 3:
                    for i in range(12):
                        w = (i // 4 + 2) * P
                        act.wait_ge(ixs_rd, i + 1)
                        if i >= 2:
                            act.wait_ge(ix_acc, i - 1)
                        A(ixr[:, i % 2, 0:w], X[:, i % 3, 0:w], ACT.Relu).then_inc(ixr_rd, 1)

            def job_high(j, sl, bank, keys):
                act.wait_ge(jobT, j + 1)
                if keys:
                    A(uH[0:HD, sl + 1], ps[0:HD, bank, :], ACT.Copy)
                    A(uH[HD:P, sl + 2], ps[HD:P, bank, :], ACT.Copy).then_inc(job_hi, 1)
                else:
                    A(uH[:, sl], ps[:, bank, :], ACT.Copy, scale=0.125).then_inc(job_hi, 1)

            def sb_high(p):
                if p == 0:
                    act.wait_ge(chunk_done, NC1 + 10)
                if p >= 2:
                    act.wait_ge(z_rd, 2 * p - 2)
                job_high(2 * p, 4 * (p % 2), 7, False)
                job_high(2 * p + 1, 4 * (p % 2), 7, True)

            nc.scalar.preload_act_table_set("natural_log_exp_and_others")

            def sb_softplus(h):
                w = zw[:, h % 2]
                act.wait_ge(zmin_rd, h + 1)
                A(w, w, ACT.Exp).then_inc(zexp_rd, 1)
                act.wait_ge(zexp_rd, h + 1)
                A(w, w, ACT.Ln, bias=1.0).then_inc(zln_rd, 1)

            def region(h):
                return ps[:, 3 * (h % 2):3 * (h % 2) + 3, :].rearrange("p b n -> p (b n)")[:, 0:1280]

            sb_high(0)
            sb_softplus(0)
            for h in range(NH):
                if h % 2 == 0 and h // 2 + 1 < 4:
                    sb_high(h // 2 + 1)
                if h + 1 < NH:
                    sb_softplus(h + 1)
                act.wait_ge(arg_rd, h + 1)
                A(zw[:, h % 2], region(h), ACT.Exp).then_inc(wgt_rd, 1)

            def dsa_high(p):
                if p == 0:
                    act.wait_ge(z_rd, NH)
                    job_high(8, 0, 3, True)
                    job_high(9, 0, 3, False)
                else:
                    if p >= 2:
                        act.wait_ge(ds_rd, 8 * p - 8)
                    job_high(9 + p, 4 * (p % 2), 3, False)

            def dsa_exps(i):
                w = (i % 4 + 1) * P
                act.wait_ge(dmx_rd, i + 1)
                if i >= 2:
                    act.wait_ge(dt_rd, i - 1)
                A(ptd[:, i % 2, 0:w], ps[:, i % 3, 0:w], ACT.Exp, bias=nmx[:, i:i + 1],
                  accum_out=rsum[:, i:i + 1]).then_inc(dp_rd, 1)

            def dsa_move(i):
                w = (i % 4 + 1) * P
                act.wait_ge(dt_rd, i + 1)
                if i >= 2:
                    act.wait_ge(dpv_rd, i - 1)
                A(ptdT[:, i % 2, 0:w], ps[:, 4 + i % 2, 0:w], ACT.Copy).then_inc(dpt_rd[i % 2], 1)

            dsa_high(0)
            dsa_exps(0)
            for i in range(NS):
                if i % 8 == 2 and i // 8 + 1 < 4:
                    dsa_high(i // 8 + 1)
                if i + 1 < NS:
                    dsa_exps(i + 1)
                if i % 2:
                    dsa_move(i)

            def mixer_high(l):
                for k in range(KT):
                    act.wait_ge(aoT, 8 * l + k + 1)
                    A(uH[:, k], X[:, k % 3, :], ACT.Copy).then_inc(ao_hi, 1)

            def out_steps(l, n0):
                for j in range(4):
                    act.wait_ge(chunk_done, n0 + j + 1)
                    split_high(n0 + j + 2)
                    if l == 0 and 3 in ticks_of(n0 + j):
                        copy_group(group_of(n0 + j))

            def norm(L):
                for x in range(8):
                    act.wait_ge(ln_d, 8 * L + x + 1)
                    if x >= 2:
                        act.wait_ge(ln_var, 8 * L + x - 1)
                    A(tmp[:, x % 2], xT[:, x], ACT.Square).then_inc(ln_sq, 1)
                act.wait_ge(ln_rin, L + 1)
                A(X[:, 2, :], X[:, 2, :], ACT.Sqrt).then_inc(ln_rs, 1)
                for x in range(8):
                    if L < 3:
                        high(U_LN[L] + x, uH[:, x])
                    else:
                        act.wait_ge(ln_t, 8 * L + x + 1)
                    A(xT[:, x], xT[:, x], ACT.Identity, bias=fcol[:, L, 3, x:x + 1],
                      scale=fcol[:, L, 2, x:x + 1]).then_inc(ax_rd, 1)

            act.wait_ge(ds_rd, NS)
            mixer_high(0)
            out_steps(0, NC1 + 10)
            norm(0)

            def feed_forward(l):
                n0, a0 = N_UP[l], use_of(N_UP[l])
                with act.Fori(0, 11) as i:
                    act.wait_ge(chunk_done, 2 * i + (n0 + 1))
                    act.wait_ge(h_lo, i + (11 * l + 1))
                    A(tmp[:, :, :], acc[:, 2 * (a0 % 2):2 * (a0 % 2) + 2, :], ACT.Silu).then_inc(acc_read[a0 % 2], 2)
                    p = n0 % 2
                    act.wait_ge(w_landed[p], 16 * i + 16 * ((n0 + 2) // 2 + 1))
                    A(whi[:, p, :], wraw[:, p, :], ACT.Copy).then_inc(hi_done, 1)
                    act.wait_ge(chunk_done, 2 * i + (n0 + 2))
                    p = 1 - p
                    act.wait_ge(w_landed[p], 16 * i + 16 * ((n0 + 3) // 2 + 1))
                    A(whi[:, p, :], wraw[:, p, :], ACT.Copy).then_inc(hi_done, 1)
                    act.wait_ge(acc_read[(a0 + 1) % 2], 2 * i + acc_count(a0 + 1))
                    A(hH[:, :, :].rearrange("p k n -> p (k n)")[:, bass.ds(i * 1024, 1024)],
                      tmp[:, :, :].rearrange("p k n -> p (k n)"), ACT.Copy).then_inc(h_hi, 1)
                    if l == 0:
                        act.wait_ge(tick_done, 4 * i + 80)
                        act.wait_ge(modT, i + 19)
                        A(mrow[:], modp[:, 0:P], ACT.Copy).then_inc(mrow_rd, 1)
                for n in range(N_DN[l], N_DN[l] + 12):
                    act.wait_ge(chunk_done, n + 1)
                    if n + 2 < NCH:
                        split_high(n + 2)
                norm(2 * l + 1)

            feed_forward(0)

            for e in range(12):
                n = N_ODD + e
                a = use_of(n)
                act.wait_ge(chunk_done, n + 1)
                A(T1[:, 0:2, WCOL * e:WCOL * e + WCOL], pair[a % 2][:, 0:512].rearrange("p (t n) -> p t n", t=2),
                  ACT.Copy).then_inc(acc_read[a % 2], 1)
                split_high(n + 2)

            act.wait_ge(lam_rd, 1)
            A(lam[:, 0:2], lam[:, 0:2], ACT.Exp).then_inc(lam_rd, 1)

            def diff_high(h):
                if h >= 2:
                    act.wait_ge(fs_rd, 4 * h - 4)
                job_high(13 + 2 * h, 4 * (h % 2), 7, False)
                job_high(14 + 2 * h, 4 * (h % 2), 7, True)

            def diff_exps(i):
                w = (i % 4 + 1) * P
                act.wait_ge(fmx_rd, i + 1)
                if i >= 2:
                    act.wait_ge(ft_rd, i - 1)
                for c in range(2):
                    A(pdf[:, i % 2, c, 0:w], ps[:, 2 * (i % 2) + c, 0:w], ACT.Exp, bias=fmx[:, 2 * (i % 4) + c:2 * (i % 4) + c + 1],
                      accum_out=fsum[:, 2 * (i % 4) + c:2 * (i % 4) + c + 1]).then_inc(fp2_rd if c == 0 else fp_rd, 1)

            def diff_move(i):
                w = (i % 4 + 1) * P
                act.wait_ge(ft_rd, i + 1)
                if i >= 2:
                    act.wait_ge(fpv_rd, i - 1)
                A(pdT[:, i % 2, 0:w], ps[:, 4 + i % 2, 0:w], ACT.Copy).then_inc(fpt_rd[i % 2], 1)

            def diff_out(h):
                act.wait_ge(fpv_rd, 4 * h + 4)
                A(T1[:, :, h * P:h * P + P], ps[:, 6, :].rearrange("p (t n) -> p t n", t=4), ACT.Copy).then_inc(fo_rd, 1)

            diff_high(0)
            diff_exps(0)
            for i in range(NS):
                if i % 4 == 2 and i // 4 + 1 < NH:
                    diff_high(i // 4 + 1)
                if i + 1 < NS:
                    diff_exps(i + 1)
                diff_move(i)
                if i >= 4 and i % 4 == 0:
                    diff_out(i // 4 - 1)
            diff_out(NH - 1)
            act.wait_ge(fo_rd, NH)
            for tt in range(TT):
                A(T1[:, tt, D:2 * D], T1[:, tt, 0:D], ACT.Square).then_inc(sln_sq, 1)
            act.wait_ge(sln_v, 1)
            A(nmx, nmx, ACT.Sqrt).then_inc(sln_rs, 1)
            mixer_high(1)
            out_steps(1, N_ODD + 12)
            norm(2)
            feed_forward(1)

            for tt in range(TT):
                act.wait_ge(fin_T, tt + 1)
                A(otok[:, tt], pair[tt % 2], ACT.Copy).then_inc(fin_rd, 1)

        @block.vector
        def _(dve):
            V = nc.vector
            n_ = [0]

            def link(ins):
                n_[0] += 1
                ins.then_inc(vch, 1)
                dve.wait_ge(vch, n_[0])

            def split_low(n):
                dve.wait_ge(hi_done, n + 1)
                V.tensor_tensor(wlo[:, n % 2, :], wraw[:, n % 2, :], whi[:, n % 2, :].bitcast(F32),
                                ALU.subtract).then_inc(lo_done, 1)

            def group_columns(g):
                dve.wait_ge(modT, g + 1)
                if g < 6:
                    o, b = mod1[:, 4 * g:4 * g + 4, :], cols[:, VBM + 4 * g:VBM + 4 * g + 4]
                    src = modp[:, P:2 * P].rearrange("p (j r) -> p j r", r=32)[:, :, 0:2]
                    V.tensor_tensor(o, src, b.unsqueeze(2).to_broadcast([P, 4, 2]), ALU.add).then_inc(mod_rd, 1)
                else:
                    b = 4 * (g - 6)
                    src = modp[:, P:2 * P].rearrange("p (j r) -> p j r", r=32)[:, :, 0]
                    V.tensor_tensor(mod2[:, b:b + 4], src, cols[:, VBM2 + b:VBM2 + b + 4], ALU.add).then_inc(mod_rd, 1)

            def low(i, dst, hi):
                dve.wait_ge(u_hi, i + 1)
                V.tensor_tensor(dst, tmp[:, i % 2, 0:dst.shape[-1]], hi.bitcast(F32), ALU.subtract).then_inc(u_lo, 1)

            dve.wait_ge(ssq_rd, 6)
            link(V.tensor_scalar(rstd, ssq, 1.0 / D, EPS, ALU.mult, ALU.add))
            V.reciprocal(rstd, rstd).then_inc(rin_rd, 1)
            dve.wait_ge(cols_rd, 1)
            for g in range(2):
                group_columns(g)
            for g in range(2, 4):
                group_columns(g)
            dve.wait_ge(mod_rd, 4)
            for c, dst in ((0, scS), (1, scC)):
                V.scalar_tensor_tensor(dst, mod1[:, 8:16, c], 1.0, cols[:, VNW:VNW + 8], ALU.add, ALU.mult)\
                    .then_inc(sc_rd, 1)
            split_low(0)
            split_low(1)
            dve.wait_ge(sc_rd, 2)
            for i in range(16):
                f, c, w = i + 8, i // 8, SEQ if i < 8 else CTX
                dve.wait_ge(xjob, f + 1)
                if i >= 2:
                    dve.wait_ge(u_lo, i - 1)
                V.tensor_scalar(tmp[:, i % 2, 0:w], X[:, f % 3, 0:w], (scS, scC)[c][:, i % 8:i % 8 + 1],
                                mod1[:, i % 8, c:c + 1], ALU.mult, ALU.add).then_inc(u_tmp, 1)
                if i >= 1:
                    j = i - 1
                    low(j, (uL if j < 8 else ucL)[:, j % 8], (uH if j < 8 else ucH)[:, j % 8])
            low(15, ucL[:, 7], ucH[:, 7])

            def tap(q):
                j, k = q // TAPS, q % TAPS
                w = cols[:, VCW + q:VCW + q + 1]
                if k == 0:
                    link(V.tensor_scalar(cy[:, j], utp[:, j, 0:SEQ], w, cols[:, VCB + j:VCB + j + 1], ALU.mult, ALU.add))
                elif k < TAPS - 1:
                    link(V.scalar_tensor_tensor(cy[:, j], utp[:, j, k:k + SEQ], w, cy[:, j], ALU.mult, ALU.add))
                else:
                    V.scalar_tensor_tensor(cy[:, j], utp[:, j, k:k + SEQ], w, cy[:, j], ALU.mult, ALU.add)\
                        .then_inc(conv_rd, 1)

            TG = 12
            for n in range(N_PW):
                if n in (1, 3):
                    j = n // 2
                    dve.wait_ge(chunk_done, n + 1)
                    acc_gone(dve, n - 1)
                    V.tensor_tensor(utp[:, 2 * j:2 * j + 2, PAD:PAD + SEQ], acc[:, 2 * (n % 2):2 * (n % 2) + 2, :],
                                    sgt[:], ALU.mult).then_inc(acc_read[n % 2], 2)
                elif N_Q <= n < N_KV:
                    c0 = WCOL * (n - N_Q)
                    dve.wait_ge(chunk_done, n + 1)
                    V.tensor_copy(qtok[:, 2:4, c0:c0 + WCOL], pair[n % 2][:, 512:1024].rearrange("p (t n) -> p t n", t=2))\
                        .then_inc(acc_read[n % 2], 1)
                elif n == N_KV:
                    dve.wait_ge(chunk_done, n + 1)
                    V.tensor_copy(kvt[:, 4:6, :], pair[n % 2][:, 512:1024].rearrange("p (t n) -> p t n", t=2))\
                        .then_inc(acc_read[n % 2], 1)
                    dve.wait_ge(sq_rd, 2)
                    V.tensor_reduce(qss[:, 0:32], sqt.rearrange("p (h d) -> p h d", d=HD), AX.X, ALU.add)
                    link(V.tensor_reduce(qss[:, 32:44], sqk.rearrange("p (h d) -> p h d", d=HD), AX.X, ALU.add))
                    dve.wait_ge(tab_in, 144)
                    link(V.tensor_scalar(qss, qss, 1.0 / HD, EPS, ALU.mult, ALU.add))
                    link(V.tensor_scalar(qkw[:, 0], qkw[:, 0], HD ** -0.5, None, ALU.mult))
                    V.reciprocal(qss, qss).then_inc(qv_rd, 1)
                if n >= 2 and n % 2 == 0:
                    group_columns(3 + n // 2)
                split_low(n + 2)
                if n >= N_Q:
                    if n == N_Q:
                        acc_gone(dve, 3)
                        acc_gone(dve, 1)
                    for q in range(TG * (n - N_Q), TG * (n - N_Q) + TG):
                        tap(q)

            for j in range(6):
                dve.wait_ge(qk_hi, j + 1)
                if j < 4:
                    V.tensor_tensor(qL[:, j], X[:, j % 2, :], qH[:, j].bitcast(F32), ALU.subtract).then_inc(qk_lo, 1)
                else:
                    src = X[:, 0:2, :].rearrange("p a n -> p (a n)")[:, 0:768]
                    V.tensor_tensor(kL[0:HD, 0, j - 4], src[0:HD], kH[0:HD, 0, j - 4].bitcast(F32), ALU.subtract)
                    V.tensor_tensor(kL[HD:P, 1, j - 4], src[HD:P], kH[HD:P, 1, j - 4].bitcast(F32),
                                    ALU.subtract).then_inc(qk_lo, 1)

            NS = 4 * NH

            def maxima(i):
                dve.wait_ge(s_rd, i + 1)
                V.tensor_reduce(nmx[:, i:i + 1], pair[i % 2][:, 0:768], AX.X, ALU.max, negate=True).then_inc(mx_rd, 1)

            def move(i):
                dve.wait_ge(t_rd, i + 1)
                if i >= 2:
                    dve.wait_ge(pv_rd, i - 1)
                V.tensor_copy(ptT[:, i % 2, 0:512], X[:, 0, :]).then_inc(pt_rd, 1)

            def head_out(h):
                dve.wait_ge(pv_rd, 4 * h + 4)
                o = X[:, 2, :] if h % 2 == 0 else modp[:, :]
                link(V.reciprocal(rinv[:, 4 * h:4 * h + 4], rsum[:, 4 * h:4 * h + 4]))
                V.tensor_tensor(qtok[:, :, h * HD:h * HD + HD], o[:, 256:512].rearrange("p (t d) -> p t d", t=4),
                                rinv[:, 4 * h:4 * h + 4].unsqueeze(2).to_broadcast([P, 4, HD]),
                                ALU.mult).then_inc(o_rd, 1)

            q = TG * (N_PW - N_Q)
            maxima(0)
            for i in range(NS):
                if i + 1 < NS:
                    maxima(i + 1)
                move(i)
                if i >= 4 and i % 4 == 1:
                    head_out(i // 4 - 1)
                for _ in range(2 if i % 4 == 0 else 1):
                    if q < 4 * TAPS:
                        tap(q)
                        q += 1
            head_out(NH - 1)

            dve.wait_ge(cmean, 1)
            for j in range(4):
                V.scalar_tensor_tensor(cy[:, j], acc[:, 0, :], -2.0, cy[:, j], ALU.mult, ALU.add).then_inc(cd_rd, 1)
            vr = utp[:, 0, 0:SEQ]
            dve.wait_ge(cvar, 4)
            link(V.tensor_scalar(vr, acc[:, 1, :], 2.0, EPS, ALU.mult, ALU.add))
            V.reciprocal(vr, vr).then_inc(crin, 1)
            dve.wait_ge(crs, 1)
            for j in range(4):
                V.tensor_tensor(cy[:, j], cy[:, j], vr, ALU.mult).then_inc(ct_rd, 1)
            for j in range(4):
                low(U_Y + j, yL[:, j], yH[:, j])
            for j in range(4):
                i = U_AT + j
                dve.wait_ge(oT, j + 1)
                dve.wait_ge(u_lo, i - 1)
                V.tensor_tensor(tmp[:, i % 2], oTp[j], sz[:, j], ALU.mult).then_inc(u_tmp, 1)
                low(i, uL[:, j], uH[:, j])
            for n in range(N_PW, NC1):
                dve.wait_ge(chunk_done, n + 1)
                if n < N_WO:
                    for m in range(2):
                        j = 2 * (n - N_PW) + m
                        i = U_CV + j
                        dve.wait_ge(u_lo, i - 1)
                        V.scalar_tensor_tensor(tmp[:, i % 2], acc[:, 2 * (n % 2) + m, :], cols[:, VBP + j:VBP + j + 1],
                                               sz[:, 4 + j], ALU.add, ALU.mult).then_inc(u_tmp, 1)
                        low(i, uL[:, 4 + j], uH[:, 4 + j])
                else:
                    for m in range(2):
                        j = 2 * (n - N_WO) + m
                        V.scalar_tensor_tensor(xT[:, j], acc[:, 2 * (n % 2) + m, :], mod1[:, 16 + j, 0:1],
                                               xT[:, j], ALU.mult, ALU.add).then_inc(acc_read[n % 2], 1)
                if n >= 2 and n % 2 == 0:
                    group_columns(3 + n // 2)
                split_low(n + 2)

            posf = small[:, 0:4]
            dve.wait_ge(rope_rd, 1)
            dve.wait_ge(chunk_done, NC1)
            link(V.tensor_copy(posf, posi[:, :]))
            ang, kk, red = [score[:, i, 0:P] for i in range(3)]
            link(V.tensor_tensor(ang.rearrange("p (t f) -> p t f", f=32), posf.unsqueeze(2).to_broadcast([P, TT, 32]),
                                 ifr[:, :].unsqueeze(1).to_broadcast([P, TT, 32]), ALU.mult))
            ROUND = 12582912.0
            for i, (turn, shift) in enumerate(((0.25, float(np.pi / 2)), (0.0, 0.0))):
                link(V.tensor_scalar(kk, ang, float(1 / (2 * np.pi)), turn, ALU.mult, ALU.add))
                link(V.tensor_scalar(kk, kk, ROUND, None, ALU.add))
                link(V.tensor_scalar(kk, kk, -ROUND, None, ALU.add))
                link(V.scalar_tensor_tensor(red, kk, -PI2[0], ang, ALU.mult, ALU.add))
                link(V.scalar_tensor_tensor(red, kk, -PI2[1], red, ALU.mult, ALU.add))
                link(V.scalar_tensor_tensor(red, kk, -PI2[2], red, ALU.mult, ALU.add))
                link(V.tensor_scalar(red, red, shift, PI_LOW, ALU.add, ALU.min))
                last = V.tensor_scalar(ropet[:, i].rearrange("p t f -> p (t f)"), red, -PI_LOW, None, ALU.max)
                if i == 0:
                    link(last)
            last.then_inc(ang_rd, 1)

            def mod(l, k):
                return mod2[:, 48 * l + 8 * k:48 * l + 8 * k + 8]

            dve.wait_ge(mod_rd, 10)
            link(V.tensor_scalar(scS, mod(0, 1), 1.0, None, ALU.add))
            acc_gone(dve, NC1 - 2)
            acc_gone(dve, NC1 - 1)

            def scaled(i, x, sc, sh):
                dve.wait_ge(u_lo, i - 1)
                V.tensor_scalar(tmp[:, i % 2], xT[:, x], sc[:, x:x + 1], sh[:, x:x + 1], ALU.mult, ALU.add).then_inc(u_tmp, 1)

            for x in range(8):
                scaled(U_B2 + x, x, scS, mod(0, 0))
                if x:
                    low(U_B2 + x - 1, uL[:, x - 1], uH[:, x - 1])
            low(U_B2 + 7, uL[:, 7], uH[:, 7])

            def topk(r_):
                q, k = r_ // 16, r_ % 16
                w = (q + 2) * P
                src = score if k == 0 else work
                link(V.max(m8[:, q], src[:, q, 0:w]))
                if k < 15:
                    link(V.match_replace(work[:, q, 0:w], m8[:, q], src[:, q, 0:w], LOWEST))
                else:
                    select(q)

            def select(q):
                w = (q + 2) * P
                tau, sc_, gt_, eq, cum = m8[:, q, 7:8], score[:, q, 0:w], work[:, q, 0:w], ptd[:, 0, 0:w], ptd[:, 1, 0:w]
                link(V.tensor_scalar(gt_, sc_, tau, 0.0, ALU.is_gt, ALU.add, accum_out=cnt[:, q, 0:1]))
                link(V.tensor_scalar(cnt[:, q, 1:2], cnt[:, q, 0:1], -1.0, float(TOPK), ALU.mult, ALU.add))
                link(V.tensor_scalar(eq, sc_, tau, None, ALU.is_equal))
                link(V.tensor_tensor_scan(cum, eq, eq, 0.0, ALU.add, ALU.max))
                link(V.scalar_tensor_tensor(cum, cum, cnt[:, q, 1:2], eq, ALU.is_le, ALU.mult))
                link(V.tensor_tensor(gt_, gt_, cum, ALU.add))
                V.tensor_scalar(Mk[:, q, 0:w], gt_, -BIG, BIG, ALU.mult, ALU.add).then_inc(msk_rd, 1)

            for e in range(10):
                n = NC1 + e
                c0 = WCOL * EORD[e]
                w = min(WCOL, EVEN - c0)
                dve.wait_ge(chunk_done, n + 1)
                V.tensor_copy(T0[:, 2:4, c0:c0 + w], pair[n % 2][:, 512:1024].rearrange("p (t n) -> p t n", t=2)[:, :, 0:w])\
                    .then_inc(acc_read[n % 2], 1)
                if e >= 2 and e % 2 == 0:
                    group_columns(group_of(n) - 1)
                split_low(n + 2)
                if e == 1:
                    acc_gone(dve, n)
                    V.tensor_scalar(wsc[:, :, :], T0[:, :, IXW:IXW + 4], 0.5, None, ALU.mult).then_inc(wsc_rd, 1)
                if e == 2:
                    for j in range(3):
                        dve.wait_ge(ix_hi, j + 1)
                        if j < 2:
                            V.scalar_tensor_tensor(ixL[:, j], X[:, j, :], 0.125, ixH[:, j].bitcast(F32),
                                                   ALU.mult, ALU.subtract).then_inc(ix_lo, 1)
                        else:
                            V.tensor_tensor(izL[0:HD, 0], X[0:HD, j, :], izH[0:HD, 0].bitcast(F32), ALU.subtract)
                            V.tensor_tensor(izL[HD:P, 1], X[HD:P, j, :], izH[HD:P, 1].bitcast(F32),
                                            ALU.subtract).then_inc(ix_lo, 1)
                if e == 3:
                    dve.wait_ge(wsc_rd, 1)
                    for i in range(12):
                        q, h = i // 4, i % 4
                        w = (q + 2) * P
                        dve.wait_ge(ixr_rd, i + 1)
                        if i:
                            dve.wait_ge(ix_acc, i)
                        sc_, wc = score[:, q, 0:w], wsc[:, q + 1, h:h + 1]
                        if h == 0:
                            V.tensor_scalar(sc_, ixr[:, i % 2, 0:w], wc, None, ALU.mult).then_inc(ix_acc, 1)
                        else:
                            V.scalar_tensor_tensor(sc_, ixr[:, i % 2, 0:w], wc, sc_, ALU.mult, ALU.add).then_inc(ix_acc, 1)
                    dve.wait_ge(ix_acc, 12)
                    for q in range(3):
                        d = score[:, q, (q + 1) * P:(q + 2) * P]
                        link(V.tensor_tensor(d, d, cmask[:], ALU.add))
                if e >= 4:
                    for r_ in range(8 * (e - 4), 8 * (e - 4) + 8):
                        topk(r_)

            def job_low(j, sl, bank, keys):
                dve.wait_ge(job_hi, j + 1)
                if keys:
                    V.tensor_tensor(uL[0:HD, sl + 1], ps[0:HD, bank, :], uH[0:HD, sl + 1].bitcast(F32), ALU.subtract)
                    V.tensor_tensor(uL[HD:P, sl + 2], ps[HD:P, bank, :], uH[HD:P, sl + 2].bitcast(F32),
                                    ALU.subtract).then_inc(job_lo, 1)
                else:
                    V.scalar_tensor_tensor(uL[:, sl], ps[:, bank, :], 0.125, uH[:, sl].bitcast(F32),
                                           ALU.mult, ALU.subtract).then_inc(job_lo, 1)

            def sb_low(p):
                job_low(2 * p, 4 * (p % 2), 7, False)
                job_low(2 * p + 1, 4 * (p % 2), 7, True)

            def region(h):
                return ps[:, 3 * (h % 2):3 * (h % 2) + 3, :].rearrange("p b n -> p (b n)")[:, 0:1280]

            def sb_min(h):
                dve.wait_ge(z_rd, h + 1)
                if h >= 2:
                    dve.wait_ge(sv_rd, h - 1)
                V.tensor_scalar(zw[:, h % 2], region(h), 40.0, None, ALU.min).then_inc(zmin_rd, 1)

            def sb_max(h):
                dve.wait_ge(zln_rd, h + 1)
                if h >= 2:
                    dve.wait_ge(arg_rd, h - 1)
                V.tensor_tensor(spt[:, h % 2], region(h), zw[:, h % 2], ALU.max).then_inc(sp_rd, 1)

            def sb_out(h):
                dve.wait_ge(sv_rd, h + 1)
                V.tensor_copy(T0[:, :, h * HD:h * HD + HD], ps[:, 6, 0:256].rearrange("p (t d) -> p t d", t=4))\
                    .then_inc(so_rd, 1)

            sb_low(0)
            sb_min(0)
            for h in range(NH):
                if h % 2 == 0 and h // 2 + 1 < 4:
                    sb_low(h // 2 + 1)
                if h + 1 < NH:
                    sb_min(h + 1)
                sb_max(h)
                if h >= 1:
                    sb_out(h - 1)
            sb_out(NH - 1)

            def dsa_low(p):
                if p == 0:
                    job_low(8, 0, 3, True)
                    job_low(9, 0, 3, False)
                else:
                    job_low(9 + p, 4 * (p % 2), 3, False)

            def dsa_max(i):
                w = (i % 4 + 1) * P
                dve.wait_ge(ds_rd, i + 1)
                V.tensor_reduce(nmx[:, i:i + 1], ps[:, i % 3, 0:w], AX.X, ALU.max, negate=True).then_inc(dmx_rd, 1)

            def dsa_move(i):
                w = (i % 4 + 1) * P
                dve.wait_ge(dt_rd, i + 1)
                if i >= 2:
                    dve.wait_ge(dpv_rd, i - 1)
                V.tensor_copy(ptdT[:, i % 2, 0:w], ps[:, 4 + i % 2, 0:w]).then_inc(dpt_rd[i % 2], 1)

            def dsa_out(h):
                dve.wait_ge(dpv_rd, 4 * h + 4)
                link(V.reciprocal(rinv[:, 4 * h:4 * h + 4], rsum[:, 4 * h:4 * h + 4]))
                V.tensor_tensor(T0[:, :, 512 + h * HD:512 + h * HD + HD],
                                ps[:, 6 + h % 2, 0:256].rearrange("p (t d) -> p t d", t=4),
                                rinv[:, 4 * h:4 * h + 4].unsqueeze(2).to_broadcast([P, 4, HD]), ALU.mult).then_inc(do_rd, 1)

            dsa_low(0)
            dsa_max(0)
            for i in range(NS):
                if i % 8 == 2 and i // 8 + 1 < 4:
                    dsa_low(i // 8 + 1)
                if i + 1 < NS:
                    dsa_max(i + 1)
                if i % 2 == 0:
                    dsa_move(i)
                if i >= 4 and i % 4 == 1:
                    dsa_out(i // 4 - 1)
            dsa_out(NH - 1)

            def mixer_low(l):
                for k in range(KT):
                    dve.wait_ge(ao_hi, 8 * l + k + 1)
                    V.tensor_tensor(uL[:, k], X[:, k % 3, :], uH[:, k].bitcast(F32), ALU.subtract).then_inc(ao_lo, 1)

            def fold(L):
                l = L // 2
                gain = cols[:, (VLMG, VLFG)[L % 2] + 8 * l:(VLMG, VLFG)[L % 2] + 8 * l + 8]
                bias = cols[:, (VLMB, VLFB)[L % 2] + 8 * l:(VLMB, VLFB)[L % 2] + 8 * l + 8]
                f = [fcol[:, L, i] for i in range(4)]
                if L < 3:
                    sc_, sh = (mod(l, 4), mod(l, 3)) if L % 2 == 0 else (mod(1, 1), mod(1, 0))
                    link(V.scalar_tensor_tensor(f[0], sc_, 1.0, gain, ALU.add, ALU.mult))
                    link(V.scalar_tensor_tensor(f[1], sc_, 1.0, bias, ALU.add, ALU.mult))
                    link(V.tensor_tensor(f[1], f[1], sh, ALU.add))
                a = ALPHA if L < 3 else 1.0
                link(V.tensor_scalar(f[2], gain, a, None, ALU.mult))
                link(V.tensor_scalar(f[3], bias, a, None, ALU.mult))

            def add_out(L, n, j, a):
                dve.wait_ge(chunk_done, n + 1)
                for m in range(2):
                    x = 2 * j + m
                    V.scalar_tensor_tensor(xT[:, x], acc[:, 2 * (a % 2) + m, :], g1p[:, L, x:x + 1], xT[:, x],
                                           ALU.mult, ALU.add).then_inc(acc_read[a % 2], 1)

            def out_steps(L, l, n0):
                dve.wait_ge(ax_rd, 8 * (L + 1))
                link(V.tensor_scalar(g1p[:, L], mod(l, 2), 1.0, None, ALU.add))
                for j in range(4):
                    n = n0 + j
                    add_out(L, n, j, use_of(n))
                    if l == 0 and j % 2 == 0:
                        group_columns(group_of(n) - 1)
                    split_low(n + 2)

            def norm(L, a):
                acc_gone(dve, a)
                acc_gone(dve, a - 1)
                dve.wait_ge(ln_mean, L + 1)
                for x in range(8):
                    V.tensor_tensor(xT[:, x], xT[:, x], X[:, 0, :], ALU.subtract).then_inc(ln_d, 1)
                fold(L)
                dve.wait_ge(ln_var, 8 * L + 8)
                link(V.tensor_scalar(X[:, 2, :], X[:, 1, :], LN_EPS, None, ALU.add))
                V.reciprocal(X[:, 2, :], X[:, 2, :]).then_inc(ln_rin, 1)
                dve.wait_ge(ln_rs, L + 1)
                for x in range(8):
                    V.tensor_tensor(xT[:, x], xT[:, x], X[:, 2, :], ALU.mult).then_inc(ln_t, 1)
                    if L < 3:
                        dve.wait_ge(ln_t, 8 * L + x + 1)
                        i = U_LN[L] + x
                        scaled(i, x, fcol[:, L, 0], fcol[:, L, 1])
                        if x:
                            low(i - 1, uL[:, x - 1], uH[:, x - 1])
                if L < 3:
                    low(U_LN[L] + 7, uL[:, 7], uH[:, 7])

            mixer_low(0)
            dve.wait_ge(mod_rd, 12)
            out_steps(0, 0, NC1 + 10)
            dve.wait_ge(mod_rd, 16)
            norm(0, use_of(NC1 + 13))

            def feed_forward(l):
                n0, a0 = N_UP[l], use_of(N_UP[l])
                L = 2 * l + 1
                if l == 0:
                    dve.wait_ge(mod_rd, 18)
                    V.tensor_scalar(g1p[:, 1], mod(0, 5), 1.0, None, ALU.add).then_inc(h_lo, 1)
                with dve.Fori(0, 11) as i:
                    if l == 0:
                        dve.wait_ge(modT, i + 19)
                        V.tensor_tensor(mod2[:, bass.ds(4 * i + 48, 4)], modp[:, P:2 * P].rearrange("p (j r) -> p j r", r=32)[:, :, 0],
                                        cols[:, bass.ds(4 * i + (VBM2 + 48), 4)], ALU.add).then_inc(mod_rd, 1)
                    p = n0 % 2
                    dve.wait_ge(hi_done, 2 * i + (n0 + 3))
                    V.tensor_tensor(wlo[:, p, :], wraw[:, p, :], whi[:, p, :].bitcast(F32), ALU.subtract).then_inc(lo_done, 1)
                    p = 1 - p
                    dve.wait_ge(chunk_done, 2 * i + (n0 + 2))
                    dve.wait_ge(acc_read[a0 % 2], 2 * i + acc_count(a0))
                    V.tensor_tensor(tmp[:, :, :], tmp[:, :, :], acc[:, 2 * ((a0 + 1) % 2):2 * ((a0 + 1) % 2) + 2, :],
                                    ALU.mult).then_inc(acc_read[(a0 + 1) % 2], 2)
                    dve.wait_ge(hi_done, 2 * i + (n0 + 4))
                    V.tensor_tensor(wlo[:, p, :], wraw[:, p, :], whi[:, p, :].bitcast(F32), ALU.subtract).then_inc(lo_done, 1)
                    dve.wait_ge(h_hi, i + (11 * l + 1))
                    fl = [w[:, :, :].rearrange("p k n -> p (k n)")[:, bass.ds(i * 1024, 1024)] for w in (hL, hH)]
                    V.tensor_tensor(fl[0], tmp[:, :, :].rearrange("p k n -> p (k n)"), fl[1].bitcast(F32),
                                    ALU.subtract).then_inc(h_lo, 1)
                if l == 0:
                    group_columns(29)
                if l == 0:
                    dve.wait_ge(h_lo, 1)
                else:
                    link(V.tensor_scalar(g1p[:, L], mod(l, 5), 1.0, None, ALU.add))
                dve.wait_ge(ax_rd, 8 * (L + 1))
                for j in range(4):
                    for c in range(3):
                        n = N_DN[l] + 3 * j + c
                        if c == 2:
                            add_out(L, n, j, A_DN[l] + j)
                        if n + 2 < NCH:
                            split_low(n + 2)
                dve.wait_ge(mod_rd, 30)
                norm(L, A_DN[l] + 3)

            feed_forward(0)

            for e in range(12):
                n = N_ODD + e
                a = use_of(n)
                dve.wait_ge(chunk_done, n + 1)
                V.tensor_copy(T1[:, 2:4, WCOL * e:WCOL * e + WCOL], pair[a % 2][:, 512:1024].rearrange("p (t n) -> p t n", t=2))\
                    .then_inc(acc_read[a % 2], 1)
                split_low(n + 2)

            dve.wait_ge(odd_in, 80)
            pr = lv[:, 0:4:2, :]
            link(V.tensor_tensor(pr, pr, lv[:, 1:4:2, :], ALU.mult))
            V.tensor_reduce(lam[:, 0:2], pr, AX.X, ALU.add).then_inc(lam_rd, 1)
            dve.wait_ge(lam_rd, 2)
            link(V.tensor_tensor(lam[:, 2:3], lam[:, 1:2], lam[:, 0:1], ALU.subtract))
            link(V.tensor_scalar(lam[:, 3:4], lam[:, 2:3], -LAMBDA_INIT, None, ALU.add))

            def diff_low(h):
                job_low(13 + 2 * h, 4 * (h % 2), 7, False)
                job_low(14 + 2 * h, 4 * (h % 2), 7, True)

            def diff_max(i):
                w = (i % 4 + 1) * P
                dve.wait_ge(fs_rd, i + 1)
                if i >= 4:
                    dve.wait_ge(fp_rd, i - 3)
                V.tensor_reduce(fmx[:, 2 * (i % 4):2 * (i % 4) + 2], ps[:, 2 * (i % 2):2 * (i % 2) + 2, 0:w], AX.X, ALU.max,
                                negate=True).then_inc(fmx_rd, 1)

            def diff_combine(i):
                w = (i % 4 + 1) * P
                c0 = 2 * (i % 4)
                dve.wait_ge(fp_rd, i + 1)
                dve.wait_ge(fp2_rd, i + 1)
                link(V.reciprocal(finv[:, c0:c0 + 2], fsum[:, c0:c0 + 2]))
                link(V.tensor_tensor(finv[:, c0 + 1:c0 + 2], finv[:, c0 + 1:c0 + 2], lam[:, 3:4], ALU.mult))
                p0, p1 = pdf[:, i % 2, 0, 0:w], pdf[:, i % 2, 1, 0:w]
                link(V.tensor_scalar(p1, p1, finv[:, c0 + 1:c0 + 2], None, ALU.mult))
                V.scalar_tensor_tensor(p0, p0, finv[:, c0:c0 + 1], p1, ALU.mult, ALU.add).then_inc(fa_rd, 1)

            diff_low(0)
            diff_max(0)
            for i in range(NS):
                if i % 4 == 2 and i // 4 + 1 < NH:
                    diff_low(i // 4 + 1)
                if i + 1 < NS:
                    diff_max(i + 1)
                diff_combine(i)

            dve.wait_ge(sln_sq, 4)
            ms = nmx.rearrange("p (t h) -> p t h", t=4)
            for tt in range(TT):
                last = V.tensor_reduce(ms[:, tt], T1[:, tt, D:2 * D].rearrange("p (h d) -> p h d", d=P), AX.X, ALU.add)
                link(last)
            link(V.tensor_scalar(nmx, nmx, 1.0 / P, LN_EPS, ALU.mult, ALU.add))
            link(V.tensor_scalar(subg[:, :], subg[:, :], 1.0 - LAMBDA_INIT, None, ALU.mult))
            V.reciprocal(nmx, nmx).then_inc(sln_v, 1)
            dve.wait_ge(sln_rs, 1)
            for tt in range(TT):
                o = T1[:, tt, 0:D].rearrange("p (h d) -> p h d", d=P)
                link(V.tensor_tensor(o, o, ms[:, tt].unsqueeze(2).to_broadcast([P, NH, P]), ALU.mult))
                V.tensor_tensor(o, o, subg[:, :].unsqueeze(1).to_broadcast([P, NH, P]), ALU.mult).then_inc(sln_g, 1)
            mixer_low(1)
            out_steps(2, 1, N_ODD + 12)
            norm(2, use_of(N_ODD + 15))
            feed_forward(1)


_INS = ["x", "c", "ctx", "c_ctx", "w_mod", "b_mod", "norm_w", "w_in", "q_norm_w", "k_norm_w", "conv_w", "conv_b",
        "conv_ln_w", "conv_ln_b", "w_pw", "b_pw", "w_out", "c_2", "positions_2", "w_mod_2", "b_mod_2",
        "w_in_even_2", "w_out_even_2", "w_in_odd_2", "lam_q1_2", "lam_k1_2", "lam_q2_2", "lam_k2_2", "subln_g_2",
        "w_out_odd_2", "ln_mix_g_2", "ln_mix_b_2", "w_gate_2", "w_up_2", "w_down_2", "ln_ffn_g_2", "ln_ffn_b_2"]


def shape_tables():
    tok = np.arange(SEQ, dtype=np.float32)
    freqs = (np.float32(10000.0) ** (-np.arange(0, 32, 2, dtype=np.float32) / np.float32(32))).astype(np.float32)
    r = np.floor(tok / 64).astype(np.float32)[:, None] * freqs[None]
    c = (tok % 64).astype(np.float32)[:, None] * freqs[None]
    ang = np.concatenate([r, c], axis=1)
    inv2 = (np.float32(10000.0) ** (-np.arange(0, 64, 2, dtype=np.float32) / np.float32(64))).astype(np.float32)
    return {"inv2": inv2[None], "cos1": np.cos(ang).astype(np.float32), "sin1": np.sin(ang).astype(np.float32)}


def kernel(**inputs):
    import numpy as _np
    import concourse.bacc as _bacc
    from concourse import mybir as _mybir
    from concourse.bass_utils import run_bass_kernel_spmd as _run

    nc = _bacc.Bacc("TRN2", target_bir_lowering=False, num_devices=1)
    arrays, t = {}, {}
    given = {name: _np.ascontiguousarray(inputs[name]) for name in _INS}
    given.update(shape_tables())
    for name, a in given.items():
        arrays[f"in_{name}_dram"] = a
        t[name] = nc.dram_tensor(f"in_{name}_dram", a.shape, _mybir.dt.from_np(a.dtype), kind="ExternalInput").ap()
    out = nc.dram_tensor("out_0_dram", (1, SEQ, D), _mybir.dt.float32, kind="ExternalOutput").ap()
    program(nc, t, out)
    r = _run(nc, [arrays], core_ids=[0])
    return r.results[0]["out_0_dram"]
```

```python
from contextlib import ExitStack

import numpy as np
import concourse.bass as bass
from concourse import mybir

ALU = mybir.AluOpType
ACT = mybir.ActivationFunctionType
AX = mybir.AxisListType
F32 = mybir.dt.float32
F32R = mybir.dt.float32r
BF16 = mybir.dt.bfloat16
I32 = mybir.dt.int32

P = 128
SEQ, CTX, D = 512, 256, 1024
TT, CT, KT = SEQ // P, CTX // P, D // P
HD = 64
NH, NKV = 8, 2
WCOL = 256
GW = 512
TAPS = 31
TURNS = {2: 12, 3: 13, 4: 14, 5: 15, 9: 16, 11: 17}
TICK_LOADS = {e: [(12 + e, (0, 1, 2, 3))] for e in range(4)}
TICK_LOADS.update({4: [(16, (0, 1))], 5: [(16, (2, 3))], 8: [(17, (0, 1))], 10: [(17, (2, 3)), (18, (0, 1))], 12: [(18, (2, 3))]})
G_DVE = range(12, 16)
CTX_TILES = {0: range(16, 19), 1: range(19, 22), 2: range(22, 24)}
G_POOL = 10
PAD = (TAPS - 1) // 2
EPS = 1e-6

VC, VCC, VC2, VBM, VNW, VCB, VLW, VLB, VBP = 0, 8, 16, 24, 48, 56, 60, 64, 68
NV1 = 72
VBM2 = NV1
NV2 = 96
VLMG, VLMB, VLFG, VLFB = 168, 184, 200, 216
NV3 = 64
VCW = NV1 + NV2 + NV3
NCOL = VCW + 4 * TAPS

N_GLU, N_Q, N_KV, N_ZA, N_ZC, N_PW, N_WO = 0, 4, 6, 7, 9, 11, 13
EVEN, FF = 2500, 2816
SBQ, SBK, SBV, DSQ, DSK, DSV, IXQ, IXK, IXW = 0, 512, 1024, 1536, 2048, 2112, 2176, 2432, 2496
EORD = (8, 9, 6, 7, 0, 1, 2, 3, 4, 5)
TOPK = 128
LOG_EXP = "natural_log_exp_and_others"
BIG = -1e30
LOWEST = -3.0e38
ALPHA = 4 ** 0.25
LN_EPS = 1e-5
_c1 = 6.28125
_c2 = float(np.floor((2 * np.pi - _c1) * 2 ** 20) / 2 ** 20)
PI2 = (_c1, _c2, float(2 * np.pi - _c1 - _c2))
PI_LOW = 3.1415925
LAMBDA_INIT = 0.8 - 0.6 * float(np.exp(-0.3))
ZOFF = (0, 512, 1024, 896)

U_U, U_UC, U_Y, U_AT, U_CV, U_B2 = 0, 8, 16, 20, 24, 28
U_LN = (36, 44, 52)


def program(nc, t, out):
    ctx = ExitStack()
    with ctx:
        def sb(name, shape, dt=F32):
            return ctx.enter_context(nc.sbuf_tensor(name, shape, dt))

        def sem(name):
            return ctx.enter_context(nc.semaphore(name))

        xT = sb("xT", [P, KT, SEQ])
        uH = sb("uH", [P, KT, SEQ], F32R)
        uL = sb("uL", [P, KT, SEQ], F32R)
        wraw = sb("wraw", [P, 2, KT * WCOL])
        whi = sb("whi", [P, 2, KT * WCOL], F32R)
        wlo = sb("wlo", [P, 2, KT * WCOL], F32R)
        mraw = sb("mraw", [P, 2, 2, GW])
        cols = sb("cols", [P, NCOL])
        cpad = sb("cpad", [P, KT, 32])
        msum = sb("msum", [P, GW])
        mrow = msum[:, 0:P]
        qkw = msum[:, P:2 * P].rearrange("p (e d) -> p e d", e=2)
        mod1 = sb("mod1", [P, 24, 2])
        mod2 = sb("mod2", [P, 96])
        tmp = sb("tmp", [P, 2, SEQ])
        ident = sb("ident", [P, P])
        identB = sb("identB", [P, P], BF16)
        cmask = sb("cmask", [P, P], BF16)
        onesD = sb("onesD", [P, P])
        ropet = sb("ropet", [P, 2, TT, 32])
        lam = sb("lam", [P, 8])
        fcol = sb("fcol", [P, 4, 4, 8])
        posi = sb("posi", [P, TT], I32)
        ifr = sb("ifr", [P, 32])
        g1p = sb("g1p", [P, 4, 8])
        small = sb("small", [P, 256])
        base = nc.sbuf_base

        ps = ctx.enter_context(nc.psum_tensor("ps", [P, 8, 512], F32))
        acc, X, modp = ps[:, 0:4, :], ps[:, 4:7, :], ps[:, 7, :]

        wT = [[w[:, s, :].rearrange("p (k n) -> p k n", k=KT) for s in range(2)] for w in (wraw, whi, wlo)]
        wT4 = [[w[:, s, 0:4 * WCOL].rearrange("p (k n) -> p k n", k=4) for s in range(2)] for w in (wraw, whi, wlo)]
        pair = [acc[:, 2 * p:2 * p + 2, :].rearrange("p a n -> p (a n)") for p in range(2)]
        fmx, fsum, finv = small[:, 216:224], small[:, 224:232], small[:, 232:240]
        oTp = [X[:, 0, :], X[:, 1, :], X[:, 2, :], modp[:, :]]
        scS = small[:, 0:8]
        scC = small[:, 8:16]
        ssq = small[:, 16:22]
        rstd = small[:, 22:28]
        qss = small[:, 32:76]
        qrs = small[:, 76:120]
        nmx = small[:, 120:152]
        rsum = small[:, 152:184]
        rinv = small[:, 184:216]
        ones1 = small[:, 242:243]
        eps1, eps2 = small[:, 240:241], small[:, 241:242]

        vec_in, x_in, ctx_in, tab_in, out_sem = sem("vec_in"), sem("x_in"), sem("ctx_in"), sem("tab_in"), sem("out_sem")
        w_landed = [sem("w_landed0"), sem("w_landed1")]
        m_landed = [sem("m_landed0"), sem("m_landed1")]
        m_first = [sem(f"m_first{i}") for i in range(4)]
        hi_done, lo_done, chunk_done = sem("hi_done"), sem("lo_done"), sem("chunk_done")
        acc_read = [sem("acc_read0"), sem("acc_read1")]
        consts, vecT, cols_rd, cpad_rd = sem("consts"), sem("vecT"), sem("cols_rd"), sem("cpad_rd")
        tick_done, mrow_rd, msum_rd, modT, mod_rd = sem("tick_done"), sem("mrow_rd"), sem("msum_rd"), sem("modT"), sem("mod_rd")
        ssq_rd, rin_rd, rstd_rd, xn_rd, sc_rd = sem("ssq_rd"), sem("rin_rd"), sem("rstd_rd"), sem("xn_rd"), sem("sc_rd")
        xjob, x_read = sem("xjob"), sem("x_read")
        u_tmp, u_hi, u_lo = sem("u_tmp"), sem("u_hi"), sem("u_lo")
        ctx_read, sq_rd, qv_rd, qrs_rd, rope_rd = sem("ctx_read"), sem("sq_rd"), sem("qv_rd"), sem("qrs_rd"), sem("rope_rd")
        qkT, qk_hi, qk_lo, kz_rd = sem("qkT"), sem("qk_hi"), sem("qk_lo"), sem("kz_rd")
        s_rd, mx_rd, p_rd, t_rd, pt_rd, pv_rd, o_rd = [sem(n) for n in ("s_rd", "mx_rd", "p_rd", "t_rd", "pt_rd", "pv_rd", "o_rd")]
        conv_rd, cmean, cd_rd, csq_rd, cvar, crs, ct_rd = [sem(n) for n in (
            "conv_rd", "cmean", "cd_rd", "csq_rd", "cvar", "crs", "ct_rd")]
        oT = sem("oT")
        ax_rd, ang_rd, sin_rd, odd_in = sem("ax_rd"), sem("ang_rd"), sem("sin_rd"), sem("odd_in")
        rp_rd, zero_rd, ixT, ix_hi, ix_lo, ixs_rd, ixr_rd, ix_acc, msk_rd = [sem(n) for n in (
            "rp_rd", "zero_rd", "ixT", "ix_hi", "ix_lo", "ixs_rd", "ixr_rd", "ix_acc", "msk_rd")]
        jobT, job_hi, job_lo = sem("jobT"), sem("job_hi"), sem("job_lo")
        z_rd, zmin_rd, zexp_rd, zln_rd, sp_rd, arg_rd, wgt_rd, sv_rd, so_rd = [sem(n) for n in (
            "z_rd", "zmin_rd", "zexp_rd", "zln_rd", "sp_rd", "arg_rd", "wgt_rd", "sv_rd", "so_rd")]
        ds_rd, dmx_rd, dp_rd, dt_rd, dpv_rd, do_rd = [sem(n) for n in ("ds_rd", "dmx_rd", "dp_rd", "dt_rd", "dpv_rd", "do_rd")]
        dpt_rd = [sem("dpt_rd0"), sem("dpt_rd1")]
        aoT, ao_hi, ao_lo = sem("aoT"), sem("ao_hi"), sem("ao_lo")
        ln_mean, ln_d, ln_sq, ln_var, ln_rs, ln_t = [sem(n) for n in (
            "ln_mean", "ln_d", "ln_sq", "ln_var", "ln_rs", "ln_t")]
        h_hi, h_lo = sem("h_hi"), sem("h_lo")
        lam_rd, fs_rd, fmx_rd, fp_rd, fa_rd, ft_rd, fpv_rd, fo_rd = [sem(n) for n in (
            "lam_rd", "fs_rd", "fmx_rd", "fp_rd", "fa_rd", "ft_rd", "fpv_rd", "fo_rd")]
        dq_rd, dinv_rd, fp2_rd, wsc_rd, kn_rd = sem("dq_rd"), sem("dinv_rd"), sem("fp2_rd"), sem("wsc_rd"), sem("kn_rd")
        fpt_rd = [sem("fpt_rd0"), sem("fpt_rd1")]
        sln_sq, sln_v, sln_rs = sem("sln_sq"), sem("sln_v"), sem("sln_rs")
        fin_T, fin_v, fin_a = sem("fin_T"), sem("fin_v"), sem("fin_a")
        vch, ach, gch = sem("vector_chain"), sem("scalar_chain"), sem("gpsimd_chain")

        b1 = ExitStack()

        def s1(name, shape, dt=F32):
            return b1.enter_context(nc.sbuf_tensor(name, shape, dt))

        def overlay(specs):
            with ExitStack() as o:
                return [o.enter_context(nc.sbuf_tensor(name, shape, dt)) for name, shape, dt in specs]

        xtok, ctok, xn = overlay([("xtok", [P, TT, D], F32), ("ctok", [P, CT, D], F32), ("xn", [P, TT, D], F32)])
        sq, = overlay([("pad_sq", [P, 8192], F32), ("sq", [P, 2816], F32)])[1:]
        sqt, sqk = sq[:, 0:2048], sq[:, 2048:2816]
        kdup, = overlay([("pad_kd", [P, 8192 + 1536], F32), ("kdup", [P, 6, 2, 2, HD], F32)])[1:]
        sgt, = overlay([("pad_sg", [P, 8192], F32), ("sgt", [P, 2, SEQ], F32)])[1:]
        sz = s1("sz", [P, 8, SEQ])
        qH = s1("qH", [P, 4, SEQ], F32R)
        qL = s1("qL", [P, 4, SEQ], F32R)
        ptb = s1("ptb", [P, 2, 768])
        ptT = s1("ptT", [P, 2, 768])
        mfirst, = overlay([("mfirst", [P, 4, 2, GW], F32)])
        gt, = overlay([("gt", [P, 4, 256], F32)])
        ucH = s1("ucH", [P, KT, CTX], F32R)
        ucL = s1("ucL", [P, KT, CTX], F32R)
        flatH, flatL = (w[:, :, :].rearrange("p k n -> p (k n)") for w in (ucH, ucL))
        kH, kL = (w[:, :, :].rearrange("p k n -> p (k n)")[:, 0:3072].rearrange("p (e g n) -> p e g n", e=2, g=2)
                  for w in (uH, uL))
        yH, yL = (w.rearrange("p (k n) -> p k n", k=4) for w in (flatH, flatL))
        utp = s1("utp", [P, 4, SEQ + 2 * PAD])
        vr1, cwr = overlay([("vr1", [P, 3, P], F32), ("cwr", [P, 512], F32)])
        cy = s1("cy", [P, 4, SEQ])
        qtok = s1("qtok", [P, TT, 512])
        kvt = s1("kvt", [P, 6, 256])

        b1.close()

        e2 = ExitStack()

        def s2(name, shape, dt=F32):
            return e2.enter_context(nc.sbuf_tensor(name, shape, dt))

        T0 = s2("T0", [P, TT, EVEN])
        kid = s2("kid", [P, TT, 2, HD])
        kdd = s2("kdd", [P, TT, 2, HD])
        score = s2("score", [P, 3, SEQ])
        work = s2("work", [P, 3, SEQ])
        ptd = s2("ptd", [P, 2, SEQ])
        ge, = overlay([("ge", [P, 4, 256], F32)])
        ptdT = s2("ptdT", [P, 2, SEQ])
        Mk = s2("Mk", [P, 3, SEQ], BF16)
        wsc = s2("wsc", [P, TT, 4])
        smask = s2("smask", [P, P], BF16)
        negtri = s2("negtri", [P, P])
        negone = s2("negone", [P, P])
        m8 = s2("m8", [P, 3, 8])
        cnt = s2("cnt", [P, 3, 2])
        ixr, = overlay([("ixr", [P, 2, SEQ], F32)])
        ixH, ixL, izH, izL = overlay([("pad_iz", [P, 1024], F32)] + [(n, [P, 2, SEQ], F32R) for n in
                                                                     ("ixH", "ixL", "izH", "izL")])[1:]
        zw = s2("zw", [P, 2, 1280])
        spt = s2("spt", [P, 2, 1280])
        e2.close()

        otok, = overlay([("otok", [P, TT, D], F32)])
        sqs, = overlay([("sqs", [P, KT, SEQ], F32)])
        hH, hL = overlay([("hH", [P, 22, SEQ], F32R), ("hL", [P, 22, SEQ], F32R)])

        o2 = ExitStack()

        def s3(name, shape, dt=F32):
            return o2.enter_context(nc.sbuf_tensor(name, shape, dt))

        T1 = s3("T1", [P, TT, 3 * D])
        pdf = s3("pdf", [P, 2, 2, SEQ])
        pdT = s3("pdT", [P, 2, SEQ])
        g1t = s3("g1t", [P, 4, 512])
        g2t = s3("g2t", [P, 4, 512])
        subg = s3("subg", [P, P])
        lv = s3("lv", [P, 4, HD])
        o2.close()

        w_in, w_out, w_pw = t["w_in"][0], t["w_out"][0], t["w_pw"][0]
        k_lo, v_hi, za, glu, zc = 512, 768, 768, 1280, 2304

        def cut(w, c0, n=WCOL):
            return w[:, c0:c0 + n].rearrange("(k p) n -> p k n", p=P)

        sources = []
        for j in range(2):
            sources += [cut(w_in, glu + 512 + WCOL * j), cut(w_in, glu + WCOL * j)]
        sources += [cut(w_in, WCOL * j) for j in range(2)] + [cut(w_in, k_lo)]
        sources += [cut(w_in, za + WCOL * j) for j in range(2)] + [cut(w_in, zc + WCOL * j) for j in range(2)]
        sources += [cut(w_pw, WCOL * j) for j in range(2)]
        sources += [cut(w_out, WCOL * j) for j in range(4)]
        even, odd = t["w_in_even_2"][0], t["w_in_odd_2"][0]
        sources += [cut(even, WCOL * j, min(WCOL, EVEN - WCOL * j)) for j in EORD]
        sources += [cut(t["w_out_even_2"][0], WCOL * j) for j in range(4)]
        N_UP = {0: len(sources), 1: len(sources) + 34 + 16}
        N_DN = {l: N_UP[l] + 22 for l in range(2)}
        N_ODD = N_DN[0] + 12
        A_DN = {0: N_DN[0], 1: N_DN[1] - 8}

        def ffn_sources(l):
            up = []
            for i in range(11):
                up += [cut(t["w_gate_2"][l], WCOL * i), cut(t["w_up_2"][l], WCOL * i)]
            dn = t["w_down_2"][l]
            for j in range(4):
                for c in range(3):
                    k0, k1 = 8 * c, min(8 * c + 8, 22)
                    up.append(dn[k0 * P:k1 * P, WCOL * j:WCOL * j + WCOL].rearrange("(k p) n -> p k n", p=P))
            return up

        sources += ffn_sources(0)
        sources += [cut(odd, WCOL * j) for j in range(12)]
        sources += [cut(t["w_out_odd_2"][0], WCOL * j) for j in range(4)]
        sources += ffn_sources(1)
        assert N_ODD == N_UP[1] - 16 and len(sources) == N_DN[1] + 12
        NC1 = N_WO + 4
        NCH = len(sources)

        def ticks_of(n):
            if n in (N_PW - 1, N_PW):
                return (0, 1, 2, 3) if n == N_PW - 1 else ()
            return (2 * (n % 2), 2 * (n % 2) + 1) if n < NC1 - 1 else ()

        def group_of(n):
            return 4 + n // 2

        def use_of(n):
            if n < N_DN[0]:
                return n
            return N_DN[0] + (n - N_DN[0]) // 3 if n < N_ODD else (n - 8 if n < N_DN[1] else A_DN[1] + (n - N_DN[1]) // 3)

        def acc_tile(eng, a, m):
            counted = a // 2 + 1 - (1 if a > N_PW + 1 else 0)
            eng.wait_ge(acc_read[a % 2], 2 * counted - 1 + m)

        def acc_count(a):
            return 2 * (a // 2 + 1 - (1 if a > N_PW + 1 else 0))

        def slot_full(eng, n):
            eng.wait_ge(w_landed[n % 2], 16 * (n // 2 + 1))

        def acc_gone(eng, a):
            counted = a // 2 + 1 - (1 if a > N_PW + 1 else 0)
            eng.wait_ge(acc_read[a % 2], 2 * counted)

        def key_banks(j):
            return X[:, 0:2, :].rearrange("p a n -> p (a n)")[:, 0:768] if j == 4 else pair[1][:, 0:768]

        def msum_at(g):
            return 11 * (g - G_POOL) - 3 * min(max(g - G_DVE[0], 0), len(G_DVE))

        def msum_after(k):
            g, kp = divmod(k, 4)
            return msum_at(g) + (2 * kp + 2 if g in G_DVE else 3 * kp + 2)

        def tick_slot(k):
            return mfirst[:, k % 4] if k < 16 else mraw[:, k % 2]

        def sums_bank(g):
            return acc[:, g, :] if g < 4 else modp

        block = ctx.enter_context(nc.Block())

        @block.sync
        def _(sp):
            def load_chunk(n):
                if n >= 2:
                    sp.wait_ge(lo_done, n - 1)
                src = sources[n]
                dst = wT4[0] if N_PW <= n < N_WO else wT[0]
                sp.dma_start(dst[n % 2][:, 0:src.shape[1], 0:src.shape[2]], src).then_inc(w_landed[n % 2], 16)

            def load_tick(g, kp):
                k = 4 * g + kp
                ahead = 4 if g < 4 else 2
                if k >= 4 * G_POOL + 2:
                    sp.wait_ge(msum_rd, msum_after(k - 2))
                elif k >= 4 and k not in (16, 17):
                    sp.wait_ge(tick_done, k - ahead + 1)
                src = t["w_mod"][0] if g < 6 else t["w_mod_2"][(g - 6) // 12]
                c0 = GW * (g if g < 6 else (g - 6) % 12)
                sp.dma_start(tick_slot(k), src[256 * kp:256 * kp + 256, c0:c0 + GW]
                             .rearrange("(k p) n -> p k n", p=P)).then_inc(m_first[k % 4] if g < 4 else m_landed[k % 2], 16)

            row = lambda ap: ap.rearrange("(r f) -> r f", f=P)
            for r, ap in ((VC, t["c"][0]), (VCC, t["c_ctx"]), (VC2, t["c_2"][0]), (VBM, t["b_mod"][0]),
                          (VNW, t["norm_w"][0]), (VCB, t["conv_b"][0]), (VLW, t["conv_ln_w"][0]),
                          (VLB, t["conv_ln_b"][0]), (VBP, t["b_pw"][0])):
                v = row(ap)
                sp.dma_start(vr1[r:r + v.shape[0], 0], v).then_inc(vec_in, 16)
            sp.dma_start(vr1[0:NV2, 1], t["b_mod_2"].rearrange("l (r f) -> (l r) f", f=P)).then_inc(vec_in, 16)
            for r, name in ((0, "ln_mix_g_2"), (16, "ln_mix_b_2"), (32, "ln_ffn_g_2"), (48, "ln_ffn_b_2")):
                sp.dma_start(vr1[r:r + 16, 2], t[name].rearrange("l (r f) -> (l r) f", f=P)).then_inc(vec_in, 16)
            sp.dma_start(cwr[0:TAPS, :], t["conv_w"][0]).then_inc(vec_in, 16)
            for kp in range(4):
                load_tick(0, kp)
            for tt in range(TT):
                sp.dma_start(xtok[:, tt], t["x"][0, tt * P:tt * P + P, :]).then_inc(x_in, 16)
            sp.dma_start(ctok[:, :, :], t["ctx"][0].rearrange("(t p) n -> p t n", p=P)).then_inc(ctx_in, 16)
            for g in range(1, 4):
                for kp in range(4):
                    load_tick(g, kp)
                if g == 3:
                    sp.dma_start(ropet[:, 0], t["cos1"].rearrange("(t p) n -> p t n", p=P)).then_inc(tab_in, 16)
                    sp.dma_start(ropet[:, 1], t["sin1"].rearrange("(t p) n -> p t n", p=P)).then_inc(tab_in, 16)
                    sp.dma_start(qkw[:, 0], t["q_norm_w"].to_broadcast([P, HD])).then_inc(tab_in, 16)
                    for tt in range(TT):
                        sp.dma_start(posi[:, tt:tt + 1], t["positions_2"][0, tt * P:tt * P + P]
                                     .rearrange("(p o) -> p o", o=1)).then_inc(tab_in, 16)
                    sp.dma_start(ifr[:, :], t["inv2"].to_broadcast([P, 32])).then_inc(tab_in, 16)
                    sp.dma_start(qkw[:, 1], t["k_norm_w"].to_broadcast([P, HD])).then_inc(tab_in, 16)
                    load_chunk(1)
                if g == 1:
                    load_chunk(0)
            for n in range(N_UP[0]):
                load_chunk(n + 2)
                for g_, kps in TICK_LOADS.get(n - NC1, ()) if n >= NC1 else [(group_of(n), ticks_of(n))]:
                    for kp in kps:
                        load_tick(g_, kp)

            def up_loads(l):
                def tick_load(i, kp):
                    sp.wait_ge(msum_rd, 11 * i + msum_after(4 * 19 + kp - 2))
                    sp.dma_start(mraw[:, kp % 2], t["w_mod_2"][1][256 * kp:256 * kp + 256, bass.ds(i * GW + GW, GW)]
                                 .rearrange("(k p) n -> p k n", p=P)).then_inc(m_landed[kp % 2], 16)

                with sp.Fori(0, 10) as i:
                    for e, w in ((0, "w_gate_2"), (1, "w_up_2")):
                        p = (N_UP[l] + e) % 2
                        sp.wait_ge(lo_done, 2 * i + (N_UP[l] + e + 1))
                        sp.dma_start(wT[0][p], t[w][l][:, bass.ds(i * WCOL + WCOL, WCOL)]
                                     .rearrange("(k p) n -> p k n", p=P)).then_inc(w_landed[p], 16)
                        if l == 0:
                            for kp in (2 * e, 2 * e + 1):
                                tick_load(i, kp)
                for e in range(2):
                    load_chunk(N_DN[l] + e)
                    if l == 0:
                        for kp in (2 * e, 2 * e + 1):
                            load_tick(29, kp)

            up_loads(0)
            for n in range(N_DN[0], N_UP[1]):
                load_chunk(n + 2)
                if n == N_ODD:
                    sp.wait_ge(chunk_done, N_ODD)
                    sp.dma_start(subg[:, :], t["subln_g_2"].to_broadcast([P, P])).then_inc(odd_in, 16)
                    for k, name in enumerate(("lam_q1_2", "lam_k1_2", "lam_q2_2", "lam_k2_2")):
                        sp.dma_start(lv[:, k], t[name].to_broadcast([P, HD])).then_inc(odd_in, 16)
            up_loads(1)
            for n in range(N_DN[1], NCH - 2):
                load_chunk(n + 2)
            for i in range(2 * TT):
                tt, half = i % 4, i // 4
                if i < 6:
                    sp.wait_ge(fin_v, i + 1)
                else:
                    sp.wait_ge(fin_a, i - 5)
                sp.dma_start(out[0, tt * P:tt * P + P, half * 512:half * 512 + 512],
                             otok[:, tt, half * 512:half * 512 + 512]).then_inc(out_sem, 16)
            sp.wait_ge(out_sem, 32 * TT)

        @block.gpsimd
        def _(pool):
            g = nc.gpsimd
            n = [0]

            def link(ins):
                n[0] += 1
                ins.then_inc(gch, 1)
                pool.wait_ge(gch, n[0])

            g.memset(eps1, EPS)
            g.memset(ones1, 1.0)
            g.memset(eps2, LN_EPS)
            g.memset(onesD[:], 1.0 / D)
            g.memset(cpad[:], 0.0)
            g.memset(utp[:], 0.0)
            link(g.memset(ident[:], 0.0))
            g.affine_select(out=ident[:], in_=ident[:], compare_op=ALU.not_equal, fill=1.0, base=0,
                            pattern=[[-1, P]], channel_multiplier=1).then_inc(consts, 1)
            g.memset(identB[:], 0.0)
            link(g.memset(cmask[:], 0.0))
            g.affine_select(out=identB[:], in_=identB[:], compare_op=ALU.not_equal, fill=1.0, base=0,
                            pattern=[[-1, P]], channel_multiplier=1).then_inc(consts, 1)
            g.affine_select(out=cmask[:], in_=cmask[:], compare_op=ALU.is_ge, fill=BIG, base=0,
                            pattern=[[-1, P]], channel_multiplier=1).then_inc(consts, 1)

            pool.wait_ge(tab_in, 144)
            pool.wait_ge(qrs_rd, 1)
            qv = qtok[:, :, :].rearrange("p t (h d) -> p t h d", d=HD)
            kv = kvt[:, :, 0:P].rearrange("p t (h d) -> p t h d", d=HD)
            for tt in range(TT):
                link(g.tensor_tensor(qv[:, tt], qv[:, tt],
                                     qrs[:, tt * NH:tt * NH + NH].unsqueeze(2).to_broadcast([P, NH, HD]), ALU.mult))
                link(g.tensor_tensor(qv[:, tt], qv[:, tt],
                                     qkw[:, 0:1, :].to_broadcast([P, NH, HD]), ALU.mult))
            pool.wait_ge(kn_rd, 1)
            for tt in range(TT):
                for heads, src, dsts in ((2, kvt[:, 2 + tt, 0:P], [0, 1]), (NH, qtok[:, tt], None)):
                    v = src.rearrange("p (h a z f) -> p h a z f", a=2, z=2, f=16)
                    one, two = v[:, :, :, 0, :], v[:, :, :, 1, :]
                    w = heads * 32
                    tm = [gt[:, i, 0:w].rearrange("p (h a f) -> p h a f", a=2, f=16) for i in range(4)]
                    cs, sn = [ropet[:, i, tt].rearrange("p (o a f) -> p o a f", o=1, a=2)
                              .to_broadcast([P, heads, 2, 16]) for i in range(2)]
                    link(g.tensor_tensor(tm[0], one, cs, ALU.mult))
                    link(g.tensor_tensor(tm[1], two, sn, ALU.mult))
                    link(g.tensor_tensor(tm[2], one, sn, ALU.mult))
                    link(g.tensor_tensor(tm[3], two, cs, ALU.mult))
                    if dsts is None:
                        link(g.tensor_tensor(one, tm[0], tm[1], ALU.subtract))
                        link(g.tensor_tensor(two, tm[2], tm[3], ALU.add))
                    else:
                        for e in dsts:
                            d = kdup[:, 2 + tt, :, e, :].rearrange("p h (a z f) -> p h a z f", a=2, z=2)
                            link(g.tensor_tensor(d[:, :, :, 0, :], tm[0], tm[1], ALU.subtract))
                            link(g.tensor_tensor(d[:, :, :, 1, :], tm[2], tm[3], ALU.add))
            for c in range(CT):
                for e in range(2):
                    last = g.tensor_copy(kdup[:, c, :, e, :], kv[:, c])
                    if c < CT - 1 or e == 0:
                        link(last)
            last.then_inc(rope_rd, 1)
            pool.wait_ge(chunk_done, N_PW)
            pool.wait_ge(rope_rd, 1)
            for i in range(4):
                half = slice(HD, P) if i % 2 == 0 else slice(0, HD)
                g.memset((kH, kL)[i // 2][half, i % 2].bitcast(F32), 0.0).then_inc(kz_rd, 1)
                pool.wait_ge(kz_rd, i + 1)

            def turn_heads(src, heads, tm_, tt, out2=None, sem_=None):
                v = src.rearrange("p (h z f) -> p h z f", z=2, f=32)
                one, two = v[:, :, 0, :], v[:, :, 1, :]
                tm = [tm_[:, i, 0:heads * 32].rearrange("p (h f) -> p h f", f=32) for i in range(4)]
                cs, sn = [ropet[:, i, tt:tt + 1].to_broadcast([P, heads, 32]) for i in range(2)]
                link(g.tensor_tensor(tm[0], one, cs, ALU.mult))
                link(g.tensor_tensor(tm[1], two, sn, ALU.mult))
                link(g.tensor_tensor(tm[2], one, sn, ALU.mult))
                link(g.tensor_tensor(tm[3], two, cs, ALU.mult))
                for o1, o2_ in ([(one, two)] if out2 is None else [(out2[:, e, 0:32].unsqueeze(1), out2[:, e, 32:64].unsqueeze(1)) for e in range(2)]):
                    link(g.tensor_tensor(o1, tm[0], tm[1], ALU.subtract))
                    last = g.tensor_tensor(o2_, tm[2], tm[3], ALU.add)
                    if sem_ is None:
                        link(last)
                    else:
                        last.then_inc(sem_, 1)
                        pool.wait_ge(sem_, tt + 1)

            def sum_tick(kp, slot, before, i=None):
                def at(v):
                    return v if i is None else 11 * i + v

                w, v = mraw[:, slot], before + (0, 2, 5, 8)[kp]
                g.tensor_tensor(w, w, cpad[:, 2 * kp:2 * kp + 2, 2:3].to_broadcast([P, 2, GW]), ALU.mult).then_inc(msum_rd, 1)
                pool.wait_ge(msum_rd, at(v + 1))
                if kp == 0:
                    g.tensor_tensor(msum[:], w[:, 0], w[:, 1], ALU.add).then_inc(msum_rd, 1)
                    pool.wait_ge(msum_rd, at(v + 2))
                else:
                    for kk in range(2):
                        g.tensor_tensor(msum[:], msum[:], w[:, kk], ALU.add).then_inc(msum_rd, 1)
                        pool.wait_ge(msum_rd, at(v + 2 + kk))

            def sum_ticks(g_, kps):
                for kp in kps:
                    k = 4 * g_ + kp
                    pool.wait_ge(m_landed[k % 2], 16 * ((k - 16) // 2 + 1))
                    if kp == 0:
                        pool.wait_ge(modT, g_)
                    sum_tick(kp, k % 2, msum_at(g_))

            for g_ in range(G_POOL, G_DVE[0]):
                sum_ticks(g_, range(4))
            pool.wait_ge(sin_rd, 2)
            acc_gone(pool, NC1)
            acc_gone(pool, NC1 + 1)
            for tt in range(TT):
                turn_heads(T0[:, tt, IXQ:IXK], 4, ge, tt)
                turn_heads(T0[:, tt, IXK:IXW], 1, ge, tt, kid[:, tt])
                turn_heads(T0[:, tt, DSK:DSV], 1, ge, tt, kdd[:, tt])
            for i in range(4):
                half, e = (slice(HD, P), 0) if i % 2 == 0 else (slice(0, HD), 1)
                link(g.memset((izH, izL)[i // 2][half, e].bitcast(F32), 0.0))
            link(g.memset(negtri[:], -1.0))
            g.affine_select(out=negtri[:], in_=negtri[:], compare_op=ALU.is_ge, fill=0.0, base=0,
                            pattern=[[-1, P]], channel_multiplier=1)
            g.memset(negone[:], -1.0)
            link(g.memset(smask[:], 0.0))
            g.affine_select(out=smask[:], in_=smask[:], compare_op=ALU.is_gt, fill=BIG, base=0,
                            pattern=[[1, P]], channel_multiplier=-1).then_inc(rp_rd, 1)
            pool.wait_ge(rp_rd, 1)
            for g_ in (16,):
                sum_ticks(g_, range(4))

            def zero_keys(n, count):
                pool.wait_ge(chunk_done, n)
                for i in range(8):
                    w, sl, e = (uH, uL)[i // 4], (i // 2) % 2, i % 2
                    half = slice(HD, P) if e == 0 else slice(0, HD)
                    g.memset(w[half, 4 * sl + 1 + e].bitcast(F32), 0.0).then_inc(zero_rd, 1)
                    pool.wait_ge(zero_rd, count + i + 1)

            acc_gone(pool, NC1 + 2)
            acc_gone(pool, NC1 + 3)
            for tt in range(TT):
                turn_heads(T0[:, tt, DSQ:DSK], NH, ge, tt, sem_=dq_rd)
            zero_keys(NC1 + 10, 0)
            for g_ in (17, 18):
                sum_ticks(g_, range(4))
            with pool.Fori(0, 11) as i:
                for kp in range(4):
                    pool.wait_ge(m_landed[kp % 2], 32 * i + 16 * (2 * (19 - 4) + kp // 2 + 1))
                    if kp == 0:
                        pool.wait_ge(modT, i + 19)
                    sum_tick(kp, kp % 2, msum_at(19), i)
            for part in range(2):
                for c in range(4):
                    acc_gone(pool, use_of(N_ODD + 4 * part + c))
                for tt in range(TT):
                    turn_heads(T1[:, tt, part * D:part * D + D], 16, (g1t, g2t)[part], tt)
            zero_keys(N_ODD + 12, 8)

        @block.tensor
        def _(pe):
            mm, tr = nc.tensor.matmul, nc.tensor.transpose

            pe.wait_ge(vec_in, 16 * 15)
            pe.wait_ge(consts, 1)
            tr(X[:, 0, 0:NV1], vr1[0:NV1, 0], ident[0:NV1, 0:NV1])
            tr(X[:, 0, NV1:NV1 + NV2], vr1[0:NV2, 1], ident[0:NV2, 0:NV2])
            tr(X[:, 0, NV1 + NV2:VCW], vr1[0:NV3, 2], ident[0:NV3, 0:NV3])
            for j in range(4):
                last = tr(X[:, 0, VCW + TAPS * j:VCW + TAPS * j + TAPS], cwr[0:TAPS, j * P:j * P + P],
                          ident[0:TAPS, 0:TAPS])
            last.then_inc(vecT, 1)
            pe.wait_ge(cpad_rd, 1)

            def tick(g, kp):
                if g >= G_POOL:
                    return
                k = 4 * g + kp
                if g < 4:
                    pe.wait_ge(m_first[k % 4], 16 * (g + 1))
                else:
                    pe.wait_ge(m_landed[k % 2], 16 * ((k - 16) // 2 + 1))
                if kp == 0 and g >= 5:
                    pe.wait_ge(mod_rd, g)
                for kk in range(2):
                    for j in range(4):
                        last = mm(sums_bank(g)[32 * j:32 * j + 32, 0:P], cpad[:, 2 * kp + kk, :],
                                  tick_slot(k)[:, kk, j * P:j * P + P],
                                  start=(kp == 0 and kk == 0), stop=(kp == 3 and kk == 1))
                last.then_inc(tick_done, 1)

            def add_partitions():
                for j in range(4):
                    last = mm(modp[:, j:j + 1], msum[:, j * P:j * P + P], ones1, start=True, stop=True)
                last.then_inc(modT, 1)

            def turn_group(g):
                if g < G_POOL:
                    pe.wait_ge(mrow_rd, g + 1)
                    tr(sums_bank(g)[:, P:2 * P], mrow[:], ident[:]).then_inc(modT, 1)
                else:
                    pe.wait_ge(msum_rd, msum_at(g + 1))
                    pe.wait_ge(mod_rd, g)
                    add_partitions()

            def input_tile(f):
                i = f % 8
                if f == 0:
                    pe.wait_ge(x_in, 64)
                    pe.wait_ge(cols_rd, 1)
                if f == 8:
                    pe.wait_ge(xn_rd, 4)
                if f == 16:
                    pe.wait_ge(xn_rd, 6)
                if f >= 11:
                    pe.wait_ge(u_tmp, f - 10)
                elif f >= 3:
                    pe.wait_ge(x_read, f - 2)
                src = xtok if f < 8 else (xn if f < 16 else ctok)
                for tt in range(TT if f < 16 else CT):
                    s = src[:, tt, i * P:i * P + P]
                    last = tr(X[:, f % 3, tt * P:tt * P + P], s, ident[:])
                last.then_inc(xjob, 1)

            first_tiles = (range(0, 8), (), range(8, 11), ())
            for g in range(4):
                for kp in range(4):
                    tick(g, kp)
                if g >= 1:
                    turn_group(g - 1)
                for f in first_tiles[g]:
                    input_tile(f)
            turn_group(3)
            for f in range(11, 16):
                input_tile(f)

            def product(n, a, nk, u0, xh, xl, w_hi, w_lo, turn=None, k0=0, first=True, done=True):
                pe.wait_ge(lo_done, n + 1)
                if a - 2 in (N_PW, N_PW + 1):
                    pe.wait_ge(u_tmp, U_CV + 2 * (a - 2 - N_PW) + 2)
                elif a >= 2 and first:
                    acc_gone(pe, a - 2)
                steps = [(m, k) for m in range(2) for k in range(nk)]
                if u0 is not None:
                    steps = [(m, k) for k in range(nk) for m in range(2)]
                for i, (m, k) in enumerate(steps):
                    o = acc[:, 2 * (a % 2) + m, :]
                    if i == nk and turn is not None:
                        turn_group(turn)
                    if u0 is not None and m == 0:
                        pe.wait_ge(u_lo, u0 + k + 1)
                    h, l = w_hi[n % 2][:, k, m * P:m * P + P], w_lo[n % 2][:, k, m * P:m * P + P]
                    mm(o, h, xh[:, k0 + k], start=(first and k == 0), stop=False)
                    mm(o, h, xl[:, k0 + k], start=False, stop=False)
                    last = mm(o, l, xh[:, k0 + k], start=False, stop=(done and k == nk - 1))
                last.then_inc(chunk_done, 1)

            def by_token(o, n, nt, xh, xl, ncol=WCOL, turn=None, u0=None):
                steps = [(tt, k) for tt in range(nt) for k in range(KT)]
                if u0 is not None:
                    steps = [(tt, k) for k in range(KT) for tt in range(nt)]
                for i, (tt, k) in enumerate(steps):
                    if i == KT and turn is not None:
                        turn_group(turn)
                    if u0 is not None and tt == 0:
                        pe.wait_ge(u_lo, u0 + k + 1)
                    h, l = whi_v[n % 2][:, k, 0:ncol], wlo_v[n % 2][:, k, 0:ncol]
                    oo = o[:, tt * WCOL:tt * WCOL + ncol]
                    xs = slice(tt * P, tt * P + P)
                    mm(oo, xh[:, k, xs], h, start=(k == 0 and (u0 is None or tt % 2 == 0)), stop=False,
                       skip_group_check=u0 is not None)
                    mm(oo, xh[:, k, xs], l, start=False, stop=False, skip_group_check=u0 is not None)
                    last = mm(oo, xl[:, k, xs], h, start=False, stop=(k == KT - 1), skip_group_check=u0 is not None)
                return last

            whi_v, wlo_v = wT[1], wT[2]
            for n in range(N_PW):
                turn = 3 + n // 2 if n and n % 2 == 0 else None
                if N_Q <= n < N_ZA:
                    pe.wait_ge(lo_done, n + 1)
                    acc_gone(pe, n - 2)
                    if n == N_KV:
                        pe.wait_ge(u_lo, U_UC + 8)
                        pe.wait_ge(u_tmp, 16)
                        by_token(X[:, 0, :], n, CT, ucH, ucL)
                    by_token(pair[n % 2], n, TT, uH, uL, turn=turn).then_inc(chunk_done, 1)
                else:
                    product(n, n, KT, U_U if n == 0 else None, uH, uL, wT[1], wT[2], turn)
                for f in CTX_TILES.get(n, ()):
                    input_tile(f)
                for kp in ticks_of(n):
                    tick(group_of(n), kp)

            pe.wait_ge(rope_rd, 1)
            pe.wait_ge(ctx_read, 1)
            for j in range(6):
                if j in (2, 3, 4):
                    pe.wait_ge(qk_lo, j if j == 4 else j - 1)
                if j == 5:
                    acc_gone(pe, N_PW - 2)
                if j < 4:
                    for tt in range(TT):
                        last = tr(X[:, j % 2, tt * P:tt * P + P], qtok[:, tt, j * P:j * P + P], ident[:])
                else:
                    for c in range(6):
                        last = tr(key_banks(j)[:, c * P:c * P + P],
                                  kdup[:, c, j - 4].rearrange("p e d -> p (e d)"), ident[:])
                last.then_inc(qkT, 1)

            pe.wait_ge(qk_lo, 6)
            pe.wait_ge(kz_rd, 4)
            acc_gone(pe, N_PW - 1)
            acc_gone(pe, N_PW - 2)

            def scores(i):
                h, qt = i // 4, i % 4
                if i >= 2:
                    pe.wait_ge(p_rd, i - 1)
                ql = slice(qt * P, qt * P + P)
                for c0, c1 in ((0, 512), (512, 768)):
                    o = pair[i % 2][:, c0:c1]
                    q_h, q_l = qH[:, h // 2, ql], qL[:, h // 2, ql]
                    k_h, k_l = kH[:, h % 2, h // 4, c0:c1], kL[:, h % 2, h // 4, c0:c1]
                    mm(o, q_h, k_h, start=True, stop=False)
                    mm(o, q_h, k_l, start=False, stop=False)
                    last = mm(o, q_l, k_h, start=False, stop=True)
                last.then_inc(s_rd, 1)

            def turn(i):
                pe.wait_ge(p_rd, i + 1)
                if i >= 1:
                    pe.wait_ge(pt_rd, i)
                for c in range(6):
                    last = tr(X[:, c // 4, (c % 4) * P:(c % 4) * P + P], ptb[:, i % 2, c * P:c * P + P], ident[:])
                last.then_inc(t_rd, 1)

            def values(i):
                h, qt = i // 4, i % 4
                o = X[:, 2, :] if h % 2 == 0 else modp[:, :]
                pe.wait_ge(pt_rd, i + 1)
                if qt == 0 and h >= 2:
                    pe.wait_ge(o_rd, h - 1)
                v0 = P + HD * (h // 4)
                for c in range(6):
                    last = mm(o[:, 256 + qt * HD:256 + qt * HD + HD], ptT[:, i % 2, c * P:c * P + P],
                              kvt[:, c, v0:v0 + HD], start=(c == 0), stop=(c == 5))
                last.then_inc(pv_rd, 1)

            NS = 4 * NH
            pe.wait_ge(mrow_rd, 10)
            scores(0)
            scores(1)
            for i in range(NS):
                turn(i)
                if i + 2 < NS:
                    scores(i + 2)
                if i >= 1:
                    values(i - 1)
            values(NS - 1)

            pe.wait_ge(conv_rd, 4)
            for j in range(4):
                last = mm(acc[:, 0, :], onesD[:], cy[:, j], start=(j == 0), stop=(j == 3))
            last.then_inc(cmean, 1)
            pe.wait_ge(o_rd, NH)
            for j in range(4):
                for tt in range(TT):
                    last = tr(oTp[j][:, tt * P:tt * P + P], qtok[:, tt, j * P:j * P + P], ident[:])
                last.then_inc(oT, 1)
            for j in range(4):
                pe.wait_ge(csq_rd, j + 1)
                last = mm(acc[:, 1, :], onesD[:], sgt[:, j % 2], start=(j == 0), stop=(j == 3))
                last.then_inc(cvar, 1)
            for n in range(N_PW, NC1):
                turn = 3 + n // 2 if n % 2 == 0 else None
                if n == N_PW + 1:
                    pe.wait_ge(u_tmp, U_AT + 4)
                if n < N_WO:
                    product(n, n, 4, U_Y if n == N_PW else None, yH, yL, wT4[1], wT4[2], turn)
                else:
                    product(n, n, KT, U_AT if n == N_WO else None, uH, uL, wT[1], wT[2], turn)
                for kp in ticks_of(n):
                    tick(group_of(n), kp)

            for e in range(10):
                n = NC1 + e
                turn = TURNS.get(e)
                pe.wait_ge(lo_done, n + 1)
                acc_gone(pe, n - 2)
                by_token(pair[n % 2], n, TT, uH, uL, min(WCOL, EVEN - WCOL * EORD[e]), turn=turn,
                         u0=U_B2 if e == 0 else None).then_inc(chunk_done, 1)
                if e == 4:
                    pe.wait_ge(rp_rd, 1)
                    for j in range(3):
                        for tt in range(TT):
                            src = T0[:, tt, IXQ + j * P:IXQ + j * P + P] if j < 2 else \
                                kid[:, tt].rearrange("p e d -> p (e d)")
                            last = tr(X[:, j, tt * P:tt * P + P], src, ident[:])
                        last.then_inc(ixT, 1)
                if e == 5:
                    pe.wait_ge(ix_lo, 3)
                    for i in range(12):
                        q, h = i // 4 + 1, i % 4
                        if i >= 3:
                            pe.wait_ge(ixr_rd, i - 2)
                        o, w = X[:, i % 3, 0:(q + 1) * P], slice(0, (q + 1) * P)
                        q_h, q_l = ixH[:, h // 2, q * P:q * P + P], ixL[:, h // 2, q * P:q * P + P]
                        mm(o, q_h, izH[:, h % 2, w], start=True, stop=False)
                        mm(o, q_h, izL[:, h % 2, w], start=False, stop=False)
                        mm(o, q_l, izH[:, h % 2, w], start=False, stop=True).then_inc(ixs_rd, 1)

            def sb_job(j):
                c0 = (SBQ, SBK)[j % 2] + (j // 2) * P
                if j >= 2:
                    pe.wait_ge(job_lo, j)
                for tt in range(TT):
                    last = tr(ps[:, 6 if j == 1 else 7, tt * P:tt * P + P], T0[:, tt, c0:c0 + P], ident[:])
                last.then_inc(jobT, 1)

            def region(h):
                return ps[:, 3 * (h % 2):3 * (h % 2) + 3, :].rearrange("p b n -> p (b n)")

            def sb_scores(h):
                z, sl, e = region(h), 4 * ((h // 2) % 2), h % 2
                pe.wait_ge(job_lo, 2 * (h // 2) + 2)
                if h >= 2:
                    pe.wait_ge(wgt_rd, h - 1)
                for kt in range(4):
                    w = SEQ - kt * P
                    o = z[:, ZOFF[kt]:ZOFF[kt] + w]
                    ks, qs = slice(kt * P, kt * P + P), slice(kt * P, SEQ)
                    mm(o, uH[:, sl + 1 + e, ks], uH[:, sl, qs], start=(kt != 3), stop=False, skip_group_check=True)
                    mm(o, uH[:, sl + 1 + e, ks], uL[:, sl, qs], start=False, stop=False, skip_group_check=True)
                    mm(o, uL[:, sl + 1 + e, ks], uH[:, sl, qs], start=False, stop=False, skip_group_check=True)
                    last = mm(o[:, 0:P], identB[:], smask[:], start=False, stop=True, skip_group_check=True)
                last.then_inc(z_rd, 1)

            def sb_suffix(h):
                z, s_ = region(h), spt[:, h % 2]
                pe.wait_ge(sp_rd, h + 1)
                for kt in range(4):
                    for k2 in range(kt, 4):
                        w = SEQ - k2 * P
                        o0 = ZOFF[kt] + (k2 - kt) * P
                        last = mm(z[:, o0:o0 + w], negtri[:] if k2 == kt else negone[:], s_[:, ZOFF[k2]:ZOFF[k2] + w],
                                  start=False, stop=True, skip_group_check=True)
                last.then_inc(arg_rd, 1)

            def sb_values(h):
                pe.wait_ge(wgt_rd, h + 1)
                if h >= 1:
                    pe.wait_ge(so_rd, h)
                for q in range(TT):
                    for kt in range(q + 1):
                        o0 = ZOFF[kt] + (q - kt) * P
                        last = mm(ps[:, 6, q * HD:q * HD + HD], spt[:, h % 2, o0:o0 + P],
                                  T0[:, kt, SBV + h * HD:SBV + h * HD + HD], start=(kt == 0), stop=(kt == q))
                last.then_inc(sv_rd, 1)

            def dsa_job(j):
                pe.wait_ge(job_lo, j)
                if j == 9:
                    pe.wait_ge(dq_rd, TT)
                for tt in range(TT):
                    src = kdd[:, tt].rearrange("p e d -> p (e d)") if j == 8 else \
                        T0[:, tt, DSQ + (j - 9) * P:DSQ + (j - 9) * P + P]
                    last = tr(ps[:, 7 if j < 10 else 3, tt * P:tt * P + P], src, ident[:])
                last.then_inc(jobT, 1)

            acc_gone(pe, NC1 + 9)
            acc_gone(pe, NC1 + 8)
            pe.wait_ge(mod_rd, TURNS[9] + 1)
            sb_job(0)
            sb_job(1)
            pe.wait_ge(zero_rd, 8)
            sb_scores(0)
            sb_scores(1)
            sb_job(2)
            for h in range(NH):
                sb_suffix(h)
                if h % 2 == 0 and h + 3 < NH:
                    sb_job(h + 3)
                if h >= 1:
                    sb_values(h - 1)
                if h + 2 < NH:
                    sb_scores(h + 2)
                if h % 2 == 1 and h + 3 < NH:
                    sb_job(h + 3)
                if h in (5, 6):
                    dsa_job(h + 3)

            def dsa_scores(i):
                h, q = i // 4, i % 4
                w = (q + 1) * P
                if i % 8 == 0:
                    pe.wait_ge(job_lo, 8 + 2 + h // 2)
                if i >= 3:
                    pe.wait_ge(dp_rd, i - 2)
                o, sl = ps[:, i % 3, 0:w], 4 * ((h // 2) % 2)
                q_h, q_l = uH[:, sl, q * P:q * P + P], uL[:, sl, q * P:q * P + P]
                k_h, k_l = uH[:, 1 + h % 2, 0:w], uL[:, 1 + h % 2, 0:w]
                mm(o, q_h, k_h, start=True, stop=False)
                mm(o, q_h, k_l, start=False, stop=False)
                mm(o, q_l, k_h, start=False, stop=False)
                mm(o, identB[:], cmask[:] if q == 0 else Mk[:, q - 1, 0:w], start=False, stop=True).then_inc(ds_rd, 1)

            def dsa_turn(i):
                q = i % 4
                pe.wait_ge(dp_rd, i + 1)
                if i >= 2:
                    pe.wait_ge(dpt_rd[i % 2], i // 2)
                for c in range(q + 1):
                    last = tr(ps[:, 4 + i % 2, c * P:c * P + P], ptd[:, i % 2, c * P:c * P + P], ident[:])
                last.then_inc(dt_rd, 1)

            def dsa_values(i):
                h, q = i // 4, i % 4
                pe.wait_ge(dpt_rd[i % 2], i // 2 + 1)
                if q == 0 and h >= 2:
                    pe.wait_ge(do_rd, h - 1)
                for c in range(q + 1):
                    last = mm(ps[:, 6 + h % 2, q * HD:q * HD + HD], ptdT[:, i % 2, c * P:c * P + P],
                              T0[:, c, DSV:DSV + HD], start=(c == 0), stop=(c == q))
                last.then_inc(dpv_rd, 1)

            pe.wait_ge(wgt_rd, NH - 1)
            dsa_scores(0)
            pe.wait_ge(msk_rd, 3)
            dsa_scores(1)
            sb_values(NH - 1)
            pe.wait_ge(so_rd, NH)
            for i in range(NS):
                dsa_turn(i)
                if i % 8 == 2 and i // 8 + 1 < 4:
                    dsa_job(10 + i // 8)
                if i + 2 < NS:
                    dsa_scores(i + 2)
                if i >= 1:
                    dsa_values(i - 1)
            dsa_values(NS - 1)

            def mixer_out(l, src):
                for k in range(KT):
                    if k >= 3:
                        pe.wait_ge(ao_lo, 8 * l + k - 2)
                    for tt in range(TT):
                        last = tr(X[:, k % 3, tt * P:tt * P + P], src[:, tt, k * P:k * P + P], ident[:])
                    last.then_inc(aoT, 1)

            def mean(L, a, j):
                for m in range(2):
                    acc_tile(pe, a, m)
                    x = 2 * j + m
                    last = mm(X[:, 0, :], onesD[:], xT[:, x], start=(x == 0), stop=(x == 7))
                return last

            def out_product(L, l, n0):
                for j in range(4):
                    n = n0 + j
                    turn = TURNS.get(10 + j) if l == 0 else None
                    product(n, use_of(n), KT, None, uH, uL, wT[1], wT[2], turn)
                    if j:
                        mean(L, use_of(n) - 1, j - 1)
                mean(L, use_of(n0 + 3), 3).then_inc(ln_mean, 1)

            def variance(L):
                for x in range(8):
                    pe.wait_ge(ln_sq, 8 * L + x + 1)
                    mm(X[:, 1, :], onesD[:], sqs[:, x], start=(x == 0), stop=(x == 7)).then_inc(ln_var, 1)

            pe.wait_ge(do_rd, NH)
            mixer_out(0, T0)
            pe.wait_ge(ao_lo, 8)
            out_product(0, 0, NC1 + 10)
            variance(0)

            def feed_forward(l):
                n0, a0 = N_UP[l], use_of(N_UP[l])
                with pe.Fori(0, 11) as i:
                    for e in range(2):
                        p = (n0 + e) % 2
                        pa = (a0 + e) % 2
                        pe.wait_ge(lo_done, 2 * i + (n0 + e + 1))
                        pe.wait_ge(acc_read[pa], 2 * i + acc_count(a0 + e - 2))
                        for s_ in range(2 * KT):
                            if s_ == KT and e == 0 and l == 0:
                                pe.wait_ge(msum_rd, 11 * i + msum_at(19))
                                pe.wait_ge(mod_rd, i + 18)
                                add_partitions()
                            k, m = (s_ // 2, s_ % 2) if e == 0 else (s_ % KT, s_ // KT)
                            if e == 0 and m == 0:
                                pe.wait_ge(u_lo, U_LN[2 * l] + k + 1)
                            o = acc[:, 2 * pa + m, :]
                            h_, l_ = wT[1][p][:, k, m * P:m * P + P], wT[2][p][:, k, m * P:m * P + P]
                            mm(o, h_, uH[:, k], start=(k == 0), stop=False)
                            mm(o, h_, uL[:, k], start=False, stop=False)
                            last = mm(o, l_, uH[:, k], start=False, stop=(k == KT - 1))
                        last.then_inc(chunk_done, 1)
                if l == 0:
                    turn_group(29)
                for j in range(4):
                    a = A_DN[l] + j
                    for c in range(3):
                        n = N_DN[l] + 3 * j + c
                        if j == 0:
                            pe.wait_ge(h_lo, 11 * l + min(11, 4 * c + 4) + 1)
                        product(n, a, min(8, 22 - 8 * c), None, hH, hL, wT[1], wT[2], None, 8 * c, c == 0, c == 2)
                    if j:
                        mean(2 * l + 1, a - 1, j - 1)
                mean(2 * l + 1, A_DN[l] + 3, 3).then_inc(ln_mean, 1)
                variance(2 * l + 1)

            feed_forward(0)

            for e in range(12):
                n = N_ODD + e
                pe.wait_ge(lo_done, n + 1)
                acc_gone(pe, use_of(n) - 2)
                by_token(pair[use_of(n) % 2], n, TT, uH, uL, u0=U_LN[1] if e == 0 else None).then_inc(chunk_done, 1)

            def diff_job(h, e):
                if (h, e) != (0, 1):
                    pe.wait_ge(job_lo, 13 + 2 * h + e)
                for tt in range(TT):
                    last = tr(ps[:, 6 if (h, e) == (0, 1) else 7, tt * P:tt * P + P], T1[:, tt, e * D + h * P:e * D + h * P + P], ident[:])
                last.then_inc(jobT, 1)

            def diff_scores(i):
                h, q = i // 4, i % 4
                w = (q + 1) * P
                sl = 4 * (h % 2)
                if q == 0:
                    pe.wait_ge(job_lo, 13 + 2 * h + 2)
                if i >= 2:
                    pe.wait_ge(fp_rd, i - 1)
                q_h, q_l = uH[:, sl, q * P:q * P + P], uL[:, sl, q * P:q * P + P]
                for c in range(2):
                    o = ps[:, 2 * (i % 2) + c, 0:w]
                    k_h, k_l = uH[:, sl + 1 + c, 0:w], uL[:, sl + 1 + c, 0:w]
                    mm(o, q_h, k_h, start=True, stop=False)
                    mm(o, q_h, k_l, start=False, stop=False)
                    mm(o, q_l, k_h, start=False, stop=False)
                    last = mm(o[:, q * P:w], identB[:], cmask[:], start=False, stop=True)
                last.then_inc(fs_rd, 1)

            def diff_turn(i):
                pe.wait_ge(fa_rd, i + 1)
                if i >= 1:
                    pe.wait_ge(fpt_rd[(i - 1) % 2], (i - 1) // 2 + 1)
                for c in range(i % 4 + 1):
                    last = tr(ps[:, 4, c * P:c * P + P], pdf[:, i % 2, 0, c * P:c * P + P], ident[:])
                last.then_inc(ft_rd, 1)

            def diff_values(i):
                h, q = i // 4, i % 4
                pe.wait_ge(fpt_rd[i % 2], i // 2 + 1)
                if q == 0 and h >= 2:
                    pe.wait_ge(fo_rd, h - 1)
                for c in range(q + 1):
                    last = mm(ps[:, 5 + h % 2, q * P:q * P + P], pdT[:, i % 2, c * P:c * P + P],
                              T1[:, c, 2 * D + h * P:2 * D + h * P + P], start=(c == 0), stop=(c == q))
                last.then_inc(fpv_rd, 1)

            acc_gone(pe, use_of(N_ODD + 11))
            acc_gone(pe, use_of(N_ODD + 10))
            pe.wait_ge(mod_rd, 30)
            pe.wait_ge(zero_rd, 9)
            diff_job(0, 0)
            diff_job(0, 1)
            diff_job(1, 0)
            pe.wait_ge(zero_rd, 16)
            diff_scores(0)
            diff_scores(1)
            diff_job(1, 1)
            for i in range(NS):
                diff_turn(i)
                if i + 2 < NS:
                    diff_scores(i + 2)
                if i % 4 >= 2 and i // 4 + 2 < NH:
                    diff_job(i // 4 + 2, i % 4 - 2)
                if i >= 1:
                    diff_values(i - 1)
            diff_values(NS - 1)
            pe.wait_ge(fo_rd, NH)
            mixer_out(1, T1)
            pe.wait_ge(ao_lo, 16)
            out_product(2, 1, N_ODD + 12)
            variance(2)
            feed_forward(1)

            for k in range(KT):
                pe.wait_ge(ax_rd, 32 + k + 1)
                for tt in range(TT):
                    last = tr(ps[:, 2 * tt + k // 4, (k % 4) * P:(k % 4) * P + P], xT[:, k, tt * P:tt * P + P], ident[:])
                    if k % 4 == 3:
                        last.then_inc(fin_T, 1)

        @block.scalar
        def _(act):
            A = nc.scalar.activation
            n_ = [0]

            def link(ins):
                n_[0] += 1
                ins.then_inc(ach, 1)
                act.wait_ge(ach, n_[0])

            act.wait_ge(vecT, 1)
            A(cols[:], X[:, 0, 0:NCOL], ACT.Copy).then_inc(cols_rd, 1)
            act.wait_ge(cols_rd, 1)
            act.wait_ge(consts, 1)
            A(cpad[:, :, 0], cols[:, VC:VC + 8], ACT.Silu)
            A(cpad[:, :, 1], cols[:, VCC:VCC + 8], ACT.Silu)
            A(cpad[:, :, 2], cols[:, VC2:VC2 + 8], ACT.Silu).then_inc(cpad_rd, 1)

            def split_high(n):
                slot_full(act, n)
                if n >= 2:
                    act.wait_ge(chunk_done, n - 1)
                A(whi[:, n % 2, :], wraw[:, n % 2, :], ACT.Copy).then_inc(hi_done, 1)

            def copy_group(g):
                if g >= G_POOL:
                    return
                act.wait_ge(tick_done, 4 * g + 4)
                if g >= 1:
                    act.wait_ge(modT, g)
                A(mrow[:], sums_bank(g)[:, 0:P], ACT.Copy).then_inc(mrow_rd, 1)

            def high(i, dst):
                act.wait_ge(u_tmp, i + 1)
                A(dst, tmp[:, i % 2, 0:dst.shape[-1]], ACT.Copy).then_inc(u_hi, 1)

            act.wait_ge(x_in, 64)
            act.wait_ge(ctx_in, 16)
            for tt in range(6):
                src = xtok[:, tt] if tt < 4 else ctok[:, tt - 4]
                if tt >= 4:
                    act.wait_ge(ssq_rd, tt - 3)
                A(xn[:, tt % 4], src, ACT.Square, accum_out=ssq[:, tt:tt + 1]).then_inc(ssq_rd, 1)
            copy_group(0)
            act.wait_ge(ssq_rd, 6)
            act.wait_ge(rin_rd, 1)
            A(rstd, rstd, ACT.Sqrt).then_inc(rstd_rd, 1)
            act.wait_ge(rstd_rd, 1)
            for tt in range(6):
                src = xtok[:, tt] if tt < 4 else ctok[:, tt - 4]
                A(xn[:, tt] if tt < 4 else ctok[:, tt - 4], src, ACT.Copy, scale=rstd[:, tt:tt + 1]).then_inc(xn_rd, 1)
            for g in range(1, 3):
                copy_group(g)
            split_high(0)
            copy_group(3)
            for i in range(8):
                high(U_U + i, uH[:, i])
            split_high(1)

            for n in range(N_PW):
                act.wait_ge(chunk_done, n + 1)
                if n in (0, 2):
                    if n == 2:
                        acc_gone(act, 1)
                    A(sgt[:], acc[:, 2 * (n % 2):2 * (n % 2) + 2, :], ACT.Sigmoid).then_inc(acc_read[n % 2], 2)
                elif N_Q <= n < N_KV:
                    c0 = WCOL * (n - N_Q)
                    A(qtok[:, 0:2, c0:c0 + WCOL], pair[n % 2][:, 0:512].rearrange("p (t n) -> p t n", t=2),
                      ACT.Copy).then_inc(acc_read[n % 2], 1)
                elif n == N_KV:
                    A(kvt[:, 2:4, :], pair[n % 2][:, 0:512].rearrange("p (t n) -> p t n", t=2),
                      ACT.Copy).then_inc(acc_read[n % 2], 1)
                    A(kvt[:, 0:2, :], X[:, 0, :].rearrange("p (t n) -> p t n", t=2), ACT.Copy).then_inc(ctx_read, 1)
                    split_high(n + 2)
                    acc_gone(act, N_KV)
                    acc_gone(act, N_KV - 1)
                    act.wait_ge(ctx_read, 1)
                    A(sqt, qtok[:, :, :].rearrange("p t n -> p (t n)"), ACT.Square).then_inc(sq_rd, 1)
                    A(sqk.rearrange("p (t n) -> p t n", t=6), kvt[:, :, 0:P], ACT.Square).then_inc(sq_rd, 1)
                elif n >= N_ZA:
                    if n == N_ZA:
                        act.wait_ge(qv_rd, 1)
                        A(qrs, qss, ACT.Sqrt).then_inc(qrs_rd, 1)
                    m = 2 * (n - N_ZA)
                    A(sz[:, m:m + 2, :], acc[:, 2 * (n % 2):2 * (n % 2) + 2, :], ACT.Silu)\
                        .then_inc(acc_read[n % 2], 2)
                if n != N_KV:
                    split_high(n + 2)
                for f in CTX_TILES.get(n, ()):
                    high(f - 8, ucH[:, f - 16])
                if 3 in ticks_of(n):
                    copy_group(group_of(n))

            act.wait_ge(chunk_done, N_PW)
            for j in range(6):
                act.wait_ge(qkT, j + 1)
                if j < 4:
                    A(qH[:, j], X[:, j % 2, :], ACT.Copy).then_inc(qk_hi, 1)
                else:
                    src = key_banks(j)
                    A(kH[0:HD, 0, j - 4], src[0:HD], ACT.Copy)
                    A(kH[HD:P, 1, j - 4], src[HD:P], ACT.Copy).then_inc(qk_hi, 1)

            NS = 4 * NH

            def exps(i):
                act.wait_ge(mx_rd, i + 1)
                if i >= 2:
                    act.wait_ge(t_rd, i - 1)
                A(ptb[:, i % 2, :], pair[i % 2][:, 0:768], ACT.Exp, bias=nmx[:, i:i + 1],
                  accum_out=rsum[:, i:i + 1]).then_inc(p_rd, 1)

            def move(i):
                act.wait_ge(t_rd, i + 1)
                if i >= 2:
                    act.wait_ge(pv_rd, i - 1)
                A(ptT[:, i % 2, :], X[:, 0:2, :].rearrange("p a n -> p (a n)")[:, 0:768], ACT.Copy).then_inc(pt_rd, 1)

            exps(0)
            exps(1)
            for i in range(NS):
                move(i)
                if i + 2 < NS:
                    exps(i + 2)

            for j in range(4):
                act.wait_ge(cd_rd, j + 1)
                if j >= 2:
                    act.wait_ge(cvar, j - 1)
                A(sgt[:, j % 2], cy[:, j], ACT.Square).then_inc(csq_rd, 1)
                if j == 0:
                    nc.scalar.preload_act_table_set(LOG_EXP)
            act.wait_ge(cvar, 4)
            A(utp[:, 0, 0:SEQ], acc[:, 1, :], ACT.Ln, scale=2.0, bias=eps1).then_inc(crs, 1)
            act.wait_ge(crs, 1)
            A(utp[:, 0, 0:SEQ], utp[:, 0, 0:SEQ], ACT.Exp, scale=-0.5).then_inc(crs, 1)
            for j in range(4):
                i = U_Y + j
                act.wait_ge(ct_rd, j + 1)
                act.wait_ge(u_lo, i - 1)
                A(tmp[:, i % 2], cy[:, j], ACT.Silu, bias=cols[:, VLB + j:VLB + j + 1],
                  scale=cols[:, VLW + j:VLW + j + 1]).then_inc(u_tmp, 1)
                high(i, yH[:, j])
            for j in range(4):
                high(U_AT + j, uH[:, j])
            for n in range(N_PW, NC1):
                act.wait_ge(chunk_done, n + 1)
                if n < N_WO:
                    for m in range(2):
                        j = 2 * (n - N_PW) + m
                        high(U_CV + j, uH[:, 4 + j])
                split_high(n + 2)
                if 3 in ticks_of(n):
                    copy_group(group_of(n))
                if n == N_WO + 1:
                    act.wait_ge(ang_rd, 1)
                    A(ropet[:, 0].rearrange("p t f -> p (t f)"), ropet[:, 0].rearrange("p t f -> p (t f)"), ACT.Sin).then_inc(sin_rd, 1)
                    A(ropet[:, 1].rearrange("p t f -> p (t f)"), ropet[:, 1].rearrange("p t f -> p (t f)"), ACT.Sin).then_inc(sin_rd, 1)
            for i in range(8):
                high(U_B2 + i, uH[:, i])
                A(xT[:, i], xT[:, i], ACT.Copy, scale=ALPHA).then_inc(ax_rd, 1)
            for e in range(10):
                n = NC1 + e
                c0 = WCOL * EORD[e]
                w = min(WCOL, EVEN - c0)
                act.wait_ge(chunk_done, n + 1)
                A(T0[:, 0:2, c0:c0 + w], pair[n % 2][:, 0:512].rearrange("p (t n) -> p t n", t=2)[:, :, 0:w],
                  ACT.Copy).then_inc(acc_read[n % 2], 1)
                if e < 9:
                    split_high(n + 2)
                if e == 4:
                    for j in range(3):
                        act.wait_ge(ixT, j + 1)
                        if j < 2:
                            A(ixH[:, j], X[:, j, :], ACT.Copy, scale=0.125).then_inc(ix_hi, 1)
                        else:
                            A(izH[0:HD, 0], X[0:HD, j, :], ACT.Copy)
                            A(izH[HD:P, 1], X[HD:P, j, :], ACT.Copy).then_inc(ix_hi, 1)
                if e == 5:
                    for i in range(12):
                        w = (i // 4 + 2) * P
                        act.wait_ge(ixs_rd, i + 1)
                        if i >= 2:
                            act.wait_ge(ix_acc, i - 1)
                        A(ixr[:, i % 2, 0:w], X[:, i % 3, 0:w], ACT.Relu).then_inc(ixr_rd, 1)

            def job_high(j, sl, bank, keys):
                act.wait_ge(jobT, j + 1)
                if keys:
                    A(uH[0:HD, sl + 1], ps[0:HD, bank, :], ACT.Copy)
                    A(uH[HD:P, sl + 2], ps[HD:P, bank, :], ACT.Copy).then_inc(job_hi, 1)
                else:
                    A(uH[:, sl], ps[:, bank, :], ACT.Copy, scale=0.125).then_inc(job_hi, 1)

            def sb_high(j):
                p = j // 2
                if j == 0:
                    act.wait_ge(chunk_done, NC1 + 10)
                if p >= 2:
                    act.wait_ge(z_rd, 2 * p - 2)
                job_high(j, 4 * (p % 2), 6 if j == 1 else 7, j % 2 == 1)

            nc.scalar.preload_act_table_set(LOG_EXP)

            def sb_softplus(h):
                w = zw[:, h % 2]
                act.wait_ge(zmin_rd, h + 1)
                A(w, w, ACT.Exp).then_inc(zexp_rd, 1)
                act.wait_ge(zexp_rd, h + 1)
                A(w, w, ACT.Ln, bias=1.0).then_inc(zln_rd, 1)

            def region(h):
                return ps[:, 3 * (h % 2):3 * (h % 2) + 3, :].rearrange("p b n -> p (b n)")[:, 0:1280]

            sb_high(0)
            sb_high(1)
            split_high(NC1 + 11)
            sb_softplus(0)
            sb_softplus(1)
            sb_high(2)
            for h in range(NH):
                act.wait_ge(arg_rd, h + 1)
                A(spt[:, h % 2], region(h), ACT.Exp).then_inc(wgt_rd, 1)
                if h % 2 == 0 and h + 3 < NH:
                    sb_high(h + 3)
                if h + 2 < NH:
                    sb_softplus(h + 2)
                if h % 2 == 1 and h + 3 < NH:
                    sb_high(h + 3)
                if h in (5, 6):
                    act.wait_ge(z_rd, h + 1)
                    job_high(h + 3, 0, 7, h == 5)

            def dsa_high(p):
                if p >= 2:
                    act.wait_ge(ds_rd, 8 * p - 8)
                job_high(9 + p, 4 * (p % 2), 3, False)

            def dsa_exps(i):
                w = (i % 4 + 1) * P
                act.wait_ge(dmx_rd, i + 1)
                if i >= 2:
                    act.wait_ge(dt_rd, i - 1)
                A(ptd[:, i % 2, 0:w], ps[:, i % 3, 0:w], ACT.Exp, bias=nmx[:, i:i + 1],
                  accum_out=rsum[:, i:i + 1]).then_inc(dp_rd, 1)

            def dsa_move(i):
                w = (i % 4 + 1) * P
                act.wait_ge(dt_rd, i + 1)
                if i >= 2:
                    act.wait_ge(dpv_rd, i - 1)
                A(ptdT[:, i % 2, 0:w], ps[:, 4 + i % 2, 0:w], ACT.Copy).then_inc(dpt_rd[i % 2], 1)

            dsa_exps(0)
            dsa_exps(1)
            for i in range(NS):
                if i % 2:
                    dsa_move(i)
                if i % 8 == 2 and i // 8 + 1 < 4:
                    dsa_high(i // 8 + 1)
                if i + 2 < NS:
                    dsa_exps(i + 2)

            def mixer_high(l):
                for k in range(KT):
                    act.wait_ge(aoT, 8 * l + k + 1)
                    A(uH[:, k], X[:, k % 3, :], ACT.Copy).then_inc(ao_hi, 1)

            def out_steps(l, n0):
                for j in range(4):
                    act.wait_ge(chunk_done, n0 + j + 1)
                    split_high(n0 + j + 2)

            def norm(L):
                nc.scalar.preload_act_table_set(LOG_EXP)
                rs = X[:, 2, :] if L < 3 else tmp[:, 0]
                for x in range(8):
                    act.wait_ge(ln_d, 8 * L + x + 1)
                    A(sqs[:, x], xT[:, x], ACT.Square).then_inc(ln_sq, 1)
                act.wait_ge(ln_var, 8 * L + 8)
                A(rs, X[:, 1, :], ACT.Ln, bias=eps2).then_inc(ln_rs, 1)
                act.wait_ge(ln_rs, 2 * L + 1)
                A(rs, rs, ACT.Exp, scale=-0.5).then_inc(ln_rs, 1)
                for x in range(8):
                    if L < 3:
                        high(U_LN[L] + x, uH[:, x])
                    else:
                        act.wait_ge(ln_t, 8 * L + x + 1)
                    A(xT[:, x], xT[:, x], ACT.Identity, bias=fcol[:, L, 3, x:x + 1],
                      scale=fcol[:, L, 2, x:x + 1]).then_inc(ax_rd, 1)

            act.wait_ge(ds_rd, NS)
            mixer_high(0)
            out_steps(0, NC1 + 10)
            norm(0)

            def feed_forward(l):
                n0, a0 = N_UP[l], use_of(N_UP[l])
                with act.Fori(0, 11) as i:
                    act.wait_ge(chunk_done, 2 * i + (n0 + 1))
                    act.wait_ge(h_lo, i + (11 * l + 1))
                    A(tmp[:, :, :], acc[:, 2 * (a0 % 2):2 * (a0 % 2) + 2, :], ACT.Silu).then_inc(acc_read[a0 % 2], 2)
                    p = n0 % 2
                    act.wait_ge(w_landed[p], 16 * i + 16 * ((n0 + 2) // 2 + 1))
                    A(whi[:, p, :], wraw[:, p, :], ACT.Copy).then_inc(hi_done, 1)
                    act.wait_ge(chunk_done, 2 * i + (n0 + 2))
                    p = 1 - p
                    act.wait_ge(w_landed[p], 16 * i + 16 * ((n0 + 3) // 2 + 1))
                    A(whi[:, p, :], wraw[:, p, :], ACT.Copy).then_inc(hi_done, 1)
                    act.wait_ge(acc_read[(a0 + 1) % 2], 2 * i + acc_count(a0 + 1))
                    A(hH[:, :, :].rearrange("p k n -> p (k n)")[:, bass.ds(i * 1024, 1024)],
                      tmp[:, :, :].rearrange("p k n -> p (k n)"), ACT.Copy).then_inc(h_hi, 1)
                for n in range(N_DN[l], N_DN[l] + 12):
                    act.wait_ge(chunk_done, n + 1)
                    if n + 2 < NCH:
                        split_high(n + 2)
                norm(2 * l + 1)

            feed_forward(0)

            for e in range(12):
                n = N_ODD + e
                a = use_of(n)
                act.wait_ge(chunk_done, n + 1)
                A(T1[:, 0:2, WCOL * e:WCOL * e + WCOL], pair[a % 2][:, 0:512].rearrange("p (t n) -> p t n", t=2),
                  ACT.Copy).then_inc(acc_read[a % 2], 1)
                if e < 11:
                    split_high(n + 2)
                if e == 4:
                    act.wait_ge(lam_rd, 1)
                    nc.scalar.preload_act_table_set(LOG_EXP)
                    A(lam[:, 0:2], lam[:, 0:2], ACT.Exp).then_inc(lam_rd, 1)


            def diff_high(h, e):
                if h >= 2:
                    act.wait_ge(fs_rd, 4 * h - 4)
                job_high(13 + 2 * h + e, 4 * (h % 2), 6 if (h, e) == (0, 1) else 7, e == 1)

            def diff_exps(i):
                w = (i % 4 + 1) * P
                act.wait_ge(fmx_rd, i + 1)
                if i >= 2:
                    act.wait_ge(ft_rd, i - 1)
                for c in range(2):
                    A(pdf[:, i % 2, c, 0:w], ps[:, 2 * (i % 2) + c, 0:w], ACT.Exp, bias=fmx[:, 2 * (i % 4) + c:2 * (i % 4) + c + 1],
                      accum_out=rsum[:, i:i + 1] if c == 0 else fsum[:, i % 4:i % 4 + 1]).then_inc(fp2_rd if c == 0 else fp_rd, 1)

            def diff_move(i):
                w = (i % 4 + 1) * P
                act.wait_ge(ft_rd, i + 1)
                if i >= 2:
                    act.wait_ge(fpv_rd, i - 1)
                A(pdT[:, i % 2, 0:w], ps[:, 4, 0:w], ACT.Copy).then_inc(fpt_rd[i % 2], 1)

            def diff_squares(h):
                act.wait_ge(fpv_rd, 4 * h + 4)
                act.wait_ge(dinv_rd, h + 1)
                for tt in range(TT):
                    A(T1[:, tt, D + h * P:D + h * P + P], ps[:, 5 + h % 2, tt * P:tt * P + P], ACT.Square,
                      scale=rinv[:, 4 * h + tt:4 * h + tt + 1],
                      accum_out=nmx[:, 4 * h + tt:4 * h + tt + 1]).then_inc(sln_sq, 1)
                ms = nmx[:, 4 * h:4 * h + 4]
                act.wait_ge(sln_sq, 4 * h + 4)
                A(ms, ms, ACT.Ln, scale=1.0 / P, bias=eps2).then_inc(sln_v, 1)
                act.wait_ge(sln_v, h + 1)
                A(ms, ms, ACT.Exp, scale=-0.5).then_inc(sln_rs, 1)

            diff_high(0, 0)
            diff_high(0, 1)
            diff_high(1, 0)
            diff_exps(0)
            diff_exps(1)
            diff_high(1, 1)
            split_high(N_ODD + 13)
            for i in range(NS):
                diff_move(i)
                if i + 2 < NS:
                    diff_exps(i + 2)
                if i % 4 >= 2 and i // 4 + 2 < NH:
                    diff_high(i // 4 + 2, i % 4 - 2)
                if i >= 4 and i % 4 == 0:
                    diff_squares(i // 4 - 1)
            diff_squares(NH - 1)
            mixer_high(1)
            out_steps(1, N_ODD + 12)
            norm(2)
            feed_forward(1)

            for tt in range(2, TT):
                act.wait_ge(fin_T, 4 + tt + 1)
                A(otok[:, tt, 512:D], ps[:, 2 * tt + 1, :], ACT.Copy).then_inc(fin_a, 1)

        @block.vector
        def _(dve):
            V = nc.vector
            n_ = [0]

            def link(ins):
                n_[0] += 1
                ins.then_inc(vch, 1)
                dve.wait_ge(vch, n_[0])

            def split_low(n):
                dve.wait_ge(hi_done, n + 1)
                V.tensor_tensor(wlo[:, n % 2, :], wraw[:, n % 2, :], whi[:, n % 2, :].bitcast(F32),
                                ALU.subtract).then_inc(lo_done, 1)

            def group_columns(g):
                dve.wait_ge(modT, g + 1)
                if g < 6:
                    o, b = mod1[:, 4 * g:4 * g + 4, :], cols[:, VBM + 4 * g:VBM + 4 * g + 4]
                    src = sums_bank(g)[:, P:2 * P].rearrange("p (j r) -> p j r", r=32)[:, :, 0:2]
                    V.tensor_tensor(o, src, b.unsqueeze(2).to_broadcast([P, 4, 2]), ALU.add).then_inc(mod_rd, 1)
                else:
                    b = 4 * (g - 6)
                    src = modp[:, P:2 * P].rearrange("p (j r) -> p j r", r=32)[:, :, 2] if g < G_POOL else modp[:, 0:4]
                    V.tensor_tensor(mod2[:, b:b + 4], src, cols[:, VBM2 + b:VBM2 + b + 4], ALU.add).then_inc(mod_rd, 1)

            def low(i, dst, hi):
                dve.wait_ge(u_hi, i + 1)
                V.tensor_tensor(dst, tmp[:, i % 2, 0:dst.shape[-1]], hi.bitcast(F32), ALU.subtract).then_inc(u_lo, 1)

            for f in range(8):
                dve.wait_ge(xjob, f + 1)
                V.tensor_copy(xT[:, f], X[:, f % 3, :]).then_inc(x_read, 1)
            dve.wait_ge(ssq_rd, 6)
            link(V.tensor_scalar(rstd, ssq, 1.0 / D, EPS, ALU.mult, ALU.add))
            V.reciprocal(rstd, rstd).then_inc(rin_rd, 1)
            dve.wait_ge(cols_rd, 1)
            for g in range(2):
                group_columns(g)
            for g in range(2, 4):
                group_columns(g)
            dve.wait_ge(mod_rd, 4)
            for c, dst in ((0, scS), (1, scC)):
                V.scalar_tensor_tensor(dst, mod1[:, 8:16, c], 1.0, cols[:, VNW:VNW + 8], ALU.add, ALU.mult)\
                    .then_inc(sc_rd, 1)
            split_low(0)
            dve.wait_ge(sc_rd, 2)

            def modulate(i):
                f, c, w = i + 8, i // 8, SEQ if i < 8 else CTX
                dve.wait_ge(xjob, f + 1)
                if i >= 2:
                    dve.wait_ge(u_lo, i - 1)
                V.tensor_scalar(tmp[:, i % 2, 0:w], X[:, f % 3, 0:w], (scS, scC)[c][:, i % 8:i % 8 + 1],
                                mod1[:, i % 8, c:c + 1], ALU.mult, ALU.add).then_inc(u_tmp, 1)

            for i in range(8):
                modulate(i)
                if i >= 1:
                    low(i - 1, uL[:, i - 1], uH[:, i - 1])
            low(7, uL[:, 7], uH[:, 7])
            split_low(1)

            def tap(q):
                j, k = q // TAPS, q % TAPS
                w = cols[:, VCW + q:VCW + q + 1]
                if k == 0:
                    link(V.tensor_scalar(cy[:, j], utp[:, j, 0:SEQ], w, cols[:, VCB + j:VCB + j + 1], ALU.mult, ALU.add))
                elif k < TAPS - 1:
                    link(V.scalar_tensor_tensor(cy[:, j], utp[:, j, k:k + SEQ], w, cy[:, j], ALU.mult, ALU.add))
                else:
                    V.scalar_tensor_tensor(cy[:, j], utp[:, j, k:k + SEQ], w, cy[:, j], ALU.mult, ALU.add)\
                        .then_inc(conv_rd, 1)

            TG = 12
            for n in range(N_PW):
                if n in (2, 4):
                    group_columns(3 + n // 2)
                if n in (1, 3):
                    j = n // 2
                    dve.wait_ge(chunk_done, n + 1)
                    acc_gone(dve, n - 1)
                    V.tensor_tensor(utp[:, 2 * j:2 * j + 2, PAD:PAD + SEQ], acc[:, 2 * (n % 2):2 * (n % 2) + 2, :],
                                    sgt[:], ALU.mult).then_inc(acc_read[n % 2], 2)
                elif N_Q <= n < N_KV:
                    c0 = WCOL * (n - N_Q)
                    dve.wait_ge(chunk_done, n + 1)
                    V.tensor_copy(qtok[:, 2:4, c0:c0 + WCOL], pair[n % 2][:, 512:1024].rearrange("p (t n) -> p t n", t=2))\
                        .then_inc(acc_read[n % 2], 1)
                elif n == N_KV:
                    dve.wait_ge(chunk_done, n + 1)
                    V.tensor_copy(kvt[:, 4:6, :], pair[n % 2][:, 512:1024].rearrange("p (t n) -> p t n", t=2))\
                        .then_inc(acc_read[n % 2], 1)
                    split_low(n + 2)
                    dve.wait_ge(sq_rd, 2)
                    V.tensor_reduce(qss[:, 0:32], sqt.rearrange("p (h d) -> p h d", d=HD), AX.X, ALU.add)
                    link(V.tensor_reduce(qss[:, 32:44], sqk.rearrange("p (h d) -> p h d", d=HD), AX.X, ALU.add))
                    dve.wait_ge(tab_in, 144)
                    link(V.tensor_scalar(qss, qss, 1.0 / HD, EPS, ALU.mult, ALU.add))
                    link(V.tensor_scalar(qkw[:, 0], qkw[:, 0], HD ** -0.5, None, ALU.mult))
                    V.reciprocal(qss, qss).then_inc(qv_rd, 1)
                if n != N_KV:
                    split_low(n + 2)
                for f in CTX_TILES.get(n, ()):
                    modulate(f - 8)
                    low(f - 8, ucL[:, f - 16], ucH[:, f - 16])
                if n == N_ZA:
                    dve.wait_ge(qrs_rd, 1)
                    for tt in range(6):
                        last = V.tensor_tensor(kvt[:, tt, 0:P].rearrange("p (h d) -> p h d", d=HD),
                                               kvt[:, tt, 0:P].rearrange("p (h d) -> p h d", d=HD),
                                               qrs[:, 32 + 2 * tt:34 + 2 * tt].unsqueeze(2).to_broadcast([P, 2, HD]), ALU.mult)
                    link(last)
                    for tt in range(6):
                        last = V.tensor_tensor(kvt[:, tt, 0:P].rearrange("p (h d) -> p h d", d=HD),
                                               kvt[:, tt, 0:P].rearrange("p (h d) -> p h d", d=HD),
                                               qkw[:, 1:2, :].to_broadcast([P, 2, HD]), ALU.mult)
                    last.then_inc(kn_rd, 1)
                if N_Q <= n < N_PW - 1:
                    if n == N_Q:
                        acc_gone(dve, 3)
                        acc_gone(dve, 1)
                    for q in range(TG * (n - N_Q), TG * (n - N_Q) + TG):
                        tap(q)
                        if n % 2 and q % TG == TG // 2:
                            group_columns(3 + (n + 1) // 2)

            for j in range(6):
                dve.wait_ge(qk_hi, j + 1)
                if j < 4:
                    V.tensor_tensor(qL[:, j], X[:, j % 2, :], qH[:, j].bitcast(F32), ALU.subtract).then_inc(qk_lo, 1)
                else:
                    src = key_banks(j)
                    V.tensor_tensor(kL[0:HD, 0, j - 4], src[0:HD], kH[0:HD, 0, j - 4].bitcast(F32), ALU.subtract)
                    V.tensor_tensor(kL[HD:P, 1, j - 4], src[HD:P], kH[HD:P, 1, j - 4].bitcast(F32),
                                    ALU.subtract).then_inc(qk_lo, 1)

            NS = 4 * NH

            def maxima(i):
                dve.wait_ge(s_rd, i + 1)
                V.tensor_reduce(nmx[:, i:i + 1], pair[i % 2][:, 0:768], AX.X, ALU.max, negate=True).then_inc(mx_rd, 1)

            def head_out(h):
                dve.wait_ge(pv_rd, 4 * h + 4)
                o = X[:, 2, :] if h % 2 == 0 else modp[:, :]
                link(V.reciprocal(rinv[:, 4 * h:4 * h + 4], rsum[:, 4 * h:4 * h + 4]))
                V.tensor_tensor(qtok[:, :, h * HD:h * HD + HD], o[:, 256:512].rearrange("p (t d) -> p t d", t=4),
                                rinv[:, 4 * h:4 * h + 4].unsqueeze(2).to_broadcast([P, 4, HD]),
                                ALU.mult).then_inc(o_rd, 1)

            q = TG * (N_PW - 1 - N_Q)
            maxima(0)
            maxima(1)
            for i in range(NS):
                if i + 2 < NS:
                    maxima(i + 2)
                if i >= 4 and i % 4 == 1:
                    head_out(i // 4 - 1)
                for _ in range(2 if i % 3 < 2 else 1):
                    if q < 4 * TAPS:
                        tap(q)
                        q += 1
            head_out(NH - 1)

            dve.wait_ge(cmean, 1)
            for j in range(4):
                V.scalar_tensor_tensor(cy[:, j], acc[:, 0, :], -2.0, cy[:, j], ALU.mult, ALU.add).then_inc(cd_rd, 1)
            vr = utp[:, 0, 0:SEQ]
            dve.wait_ge(crs, 2)
            for j in range(4):
                V.tensor_tensor(cy[:, j], cy[:, j], vr, ALU.mult).then_inc(ct_rd, 1)
            for j in range(4):
                low(U_Y + j, yL[:, j], yH[:, j])
            for j in range(4):
                i = U_AT + j
                dve.wait_ge(oT, j + 1)
                dve.wait_ge(u_lo, i - 1)
                V.tensor_tensor(tmp[:, i % 2], oTp[j], sz[:, j], ALU.mult).then_inc(u_tmp, 1)
                low(i, uL[:, j], uH[:, j])
            def rope_angles():
                posf = small[:, 0:4]
                dve.wait_ge(rope_rd, 1)
                link(V.tensor_copy(posf, posi[:, :]))
                ang, kk, red = [tmp[:, 0, i * P:i * P + P] for i in range(3)]
                link(V.tensor_tensor(ang.rearrange("p (t f) -> p t f", f=32), posf.unsqueeze(2).to_broadcast([P, TT, 32]),
                                     ifr[:, :].unsqueeze(1).to_broadcast([P, TT, 32]), ALU.mult))
                ROUND = 12582912.0
                for i, (turn, shift) in enumerate(((0.25, float(np.pi / 2)), (0.0, 0.0))):
                    link(V.tensor_scalar(kk, ang, float(1 / (2 * np.pi)), turn, ALU.mult, ALU.add))
                    link(V.tensor_scalar(kk, kk, ROUND, None, ALU.add))
                    link(V.tensor_scalar(kk, kk, -ROUND, None, ALU.add))
                    link(V.scalar_tensor_tensor(red, kk, -PI2[0], ang, ALU.mult, ALU.add))
                    link(V.scalar_tensor_tensor(red, kk, -PI2[1], red, ALU.mult, ALU.add))
                    link(V.scalar_tensor_tensor(red, kk, -PI2[2], red, ALU.mult, ALU.add))
                    link(V.tensor_scalar(red, red, shift, PI_LOW, ALU.add, ALU.min))
                    last = V.tensor_scalar(ropet[:, i].rearrange("p t f -> p (t f)"), red, -PI_LOW, None, ALU.max)
                    if i == 0:
                        link(last)
                last.then_inc(ang_rd, 1)

            for n in range(N_PW, NC1):
                dve.wait_ge(chunk_done, n + 1)
                if n < N_WO:
                    for m in range(2):
                        j = 2 * (n - N_PW) + m
                        i = U_CV + j
                        dve.wait_ge(u_lo, i - 1)
                        V.scalar_tensor_tensor(tmp[:, i % 2], acc[:, 2 * (n % 2) + m, :], cols[:, VBP + j:VBP + j + 1],
                                               sz[:, 4 + j], ALU.add, ALU.mult).then_inc(u_tmp, 1)
                        low(i, uL[:, 4 + j], uH[:, 4 + j])
                else:
                    for m in range(2):
                        j = 2 * (n - N_WO) + m
                        V.scalar_tensor_tensor(xT[:, j], acc[:, 2 * (n % 2) + m, :], mod1[:, 16 + j, 0:1],
                                               xT[:, j], ALU.mult, ALU.add).then_inc(acc_read[n % 2], 1)
                if n >= 2 and n % 2 == 0:
                    group_columns(3 + n // 2)
                split_low(n + 2)
                if n == N_WO:
                    rope_angles()

            def mod(l, k):
                return mod2[:, 48 * l + 8 * k:48 * l + 8 * k + 8]

            dve.wait_ge(mod_rd, 10)
            link(V.tensor_scalar(scS, mod(0, 1), 1.0, None, ALU.add))
            acc_gone(dve, NC1 - 2)
            acc_gone(dve, NC1 - 1)

            def scaled(i, x, sc, sh):
                dve.wait_ge(u_lo, i - 1)
                V.tensor_scalar(tmp[:, i % 2], xT[:, x], sc[:, x:x + 1], sh[:, x:x + 1], ALU.mult, ALU.add).then_inc(u_tmp, 1)

            for x in range(8):
                scaled(U_B2 + x, x, scS, mod(0, 0))
                if x:
                    low(U_B2 + x - 1, uL[:, x - 1], uH[:, x - 1])
            low(U_B2 + 7, uL[:, 7], uH[:, 7])

            def sum_group(g_):
                dve.wait_ge(modT, g_)
                for kt in range(KT):
                    k = 4 * g_ + kt // 2
                    dve.wait_ge(m_landed[k % 2], 16 * ((k - 16) // 2 + 1))
                    w, c = mraw[:, k % 2, kt % 2, :], cpad[:, kt, 2:3]
                    if kt == 0:
                        V.tensor_scalar(msum[:], w, c, None, ALU.mult).then_inc(msum_rd, 1)
                    else:
                        dve.wait_ge(msum_rd, msum_at(g_) + kt)
                        V.scalar_tensor_tensor(msum[:], w, c, msum[:], ALU.mult, ALU.add).then_inc(msum_rd, 1)

            def topk(r_):
                q, k = r_ // 16, r_ % 16
                w = (q + 2) * P
                src = score if k == 0 else work
                link(V.max(m8[:, q], src[:, q, 0:w]))
                if k < 15:
                    link(V.match_replace(work[:, q, 0:w], m8[:, q], src[:, q, 0:w], LOWEST))
                else:
                    select(q)

            def select(q):
                w = (q + 2) * P
                tau, sc_, gt_, eq, cum = m8[:, q, 7:8], score[:, q, 0:w], work[:, q, 0:w], ptd[:, 0, 0:w], ptd[:, 1, 0:w]
                link(V.tensor_scalar(gt_, sc_, tau, 0.0, ALU.is_gt, ALU.add, accum_out=cnt[:, q, 0:1]))
                link(V.tensor_scalar(cnt[:, q, 1:2], cnt[:, q, 0:1], -1.0, float(TOPK), ALU.mult, ALU.add))
                link(V.tensor_scalar(eq, sc_, tau, None, ALU.is_equal))
                link(V.tensor_tensor_scan(cum, eq, eq, 0.0, ALU.add, ALU.max))
                link(V.scalar_tensor_tensor(cum, cum, cnt[:, q, 1:2], eq, ALU.is_le, ALU.mult))
                link(V.tensor_tensor(gt_, gt_, cum, ALU.add))
                V.tensor_scalar(Mk[:, q, 0:w], gt_, -BIG, BIG, ALU.mult, ALU.add).then_inc(msk_rd, 1)

            for e in range(10):
                n = NC1 + e
                c0 = WCOL * EORD[e]
                w = min(WCOL, EVEN - c0)
                dve.wait_ge(chunk_done, n + 1)
                V.tensor_copy(T0[:, 2:4, c0:c0 + w], pair[n % 2][:, 512:1024].rearrange("p (t n) -> p t n", t=2)[:, :, 0:w])\
                    .then_inc(acc_read[n % 2], 1)
                if e in TURNS:
                    group_columns(TURNS[e])
                if e < 9:
                    split_low(n + 2)
                if 12 + e in G_DVE:
                    sum_group(12 + e)
                if e == 1:
                    acc_gone(dve, n)
                    V.tensor_scalar(wsc[:, :, :], T0[:, :, IXW:IXW + 4], 0.5, None, ALU.mult).then_inc(wsc_rd, 1)
                if e == 4:
                    for j in range(3):
                        dve.wait_ge(ix_hi, j + 1)
                        if j < 2:
                            V.scalar_tensor_tensor(ixL[:, j], X[:, j, :], 0.125, ixH[:, j].bitcast(F32),
                                                   ALU.mult, ALU.subtract).then_inc(ix_lo, 1)
                        else:
                            V.tensor_tensor(izL[0:HD, 0], X[0:HD, j, :], izH[0:HD, 0].bitcast(F32), ALU.subtract)
                            V.tensor_tensor(izL[HD:P, 1], X[HD:P, j, :], izH[HD:P, 1].bitcast(F32),
                                            ALU.subtract).then_inc(ix_lo, 1)
                if e == 5:
                    dve.wait_ge(wsc_rd, 1)
                    for i in range(12):
                        q, h = i // 4, i % 4
                        w = (q + 2) * P
                        dve.wait_ge(ixr_rd, i + 1)
                        if i:
                            dve.wait_ge(ix_acc, i)
                        sc_, wc = score[:, q, 0:w], wsc[:, q + 1, h:h + 1]
                        if h == 0:
                            V.tensor_scalar(sc_, ixr[:, i % 2, 0:w], wc, None, ALU.mult).then_inc(ix_acc, 1)
                        else:
                            V.scalar_tensor_tensor(sc_, ixr[:, i % 2, 0:w], wc, sc_, ALU.mult, ALU.add).then_inc(ix_acc, 1)
                    dve.wait_ge(ix_acc, 12)
                    for q in range(3):
                        d = score[:, q, (q + 1) * P:(q + 2) * P]
                        link(V.tensor_tensor(d, d, cmask[:], ALU.add))
                if 6 <= e < 9:
                    for r_ in range(*((0, 8), (8, 14), (14, 18))[e - 6]):
                        topk(r_)

            def job_low(j, sl, bank, keys):
                dve.wait_ge(job_hi, j + 1)
                if keys:
                    V.tensor_tensor(uL[0:HD, sl + 1], ps[0:HD, bank, :], uH[0:HD, sl + 1].bitcast(F32), ALU.subtract)
                    V.tensor_tensor(uL[HD:P, sl + 2], ps[HD:P, bank, :], uH[HD:P, sl + 2].bitcast(F32),
                                    ALU.subtract).then_inc(job_lo, 1)
                else:
                    V.scalar_tensor_tensor(uL[:, sl], ps[:, bank, :], 0.125, uH[:, sl].bitcast(F32),
                                           ALU.mult, ALU.subtract).then_inc(job_lo, 1)

            def sb_low(j):
                job_low(j, 4 * (j // 2 % 2), 6 if j == 1 else 7, j % 2 == 1)

            def region(h):
                return ps[:, 3 * (h % 2):3 * (h % 2) + 3, :].rearrange("p b n -> p (b n)")[:, 0:1280]

            def sb_min(h):
                dve.wait_ge(z_rd, h + 1)
                if h >= 2:
                    dve.wait_ge(sp_rd, h - 1)
                V.tensor_scalar(zw[:, h % 2], region(h), 40.0, None, ALU.min).then_inc(zmin_rd, 1)

            def sb_max(h):
                dve.wait_ge(zln_rd, h + 1)
                if h >= 2:
                    dve.wait_ge(sv_rd, h - 1)
                V.tensor_tensor(spt[:, h % 2], region(h), zw[:, h % 2], ALU.max).then_inc(sp_rd, 1)

            def sb_out(h):
                dve.wait_ge(sv_rd, h + 1)
                V.tensor_copy(T0[:, :, h * HD:h * HD + HD], ps[:, 6, 0:256].rearrange("p (t d) -> p t d", t=4))\
                    .then_inc(so_rd, 1)

            sb_low(0)
            sb_low(1)
            split_low(NC1 + 11)
            sb_min(0)
            sb_min(1)
            sb_low(2)
            sb_max(0)
            for r_ in range(18, 26):
                topk(r_)
            for h in range(NH):
                if h % 2 == 0 and h + 3 < NH:
                    sb_low(h + 3)
                if h + 1 < NH:
                    sb_max(h + 1)
                if h + 2 < NH:
                    sb_min(h + 2)
                if h % 2 == 1 and h + 3 < NH:
                    sb_low(h + 3)
                if h in (5, 6):
                    job_low(h + 3, 0, 7, h == 5)
                if h >= 1:
                    sb_out(h - 1)
                for r_ in range(26 + 3 * h + (h > 0), min(30 + 3 * h, 48)):
                    topk(r_)

            def dsa_low(p):
                job_low(9 + p, 4 * (p % 2), 3, False)

            def dsa_max(i):
                w = (i % 4 + 1) * P
                dve.wait_ge(ds_rd, i + 1)
                V.tensor_reduce(nmx[:, i:i + 1], ps[:, i % 3, 0:w], AX.X, ALU.max, negate=True).then_inc(dmx_rd, 1)

            def dsa_move(i):
                w = (i % 4 + 1) * P
                dve.wait_ge(dt_rd, i + 1)
                if i >= 2:
                    dve.wait_ge(dpv_rd, i - 1)
                V.tensor_copy(ptdT[:, i % 2, 0:w], ps[:, 4 + i % 2, 0:w]).then_inc(dpt_rd[i % 2], 1)

            def dsa_out(h):
                dve.wait_ge(dpv_rd, 4 * h + 4)
                link(V.reciprocal(rinv[:, 4 * h:4 * h + 4], rsum[:, 4 * h:4 * h + 4]))
                V.tensor_tensor(T0[:, :, 512 + h * HD:512 + h * HD + HD],
                                ps[:, 6 + h % 2, 0:256].rearrange("p (t d) -> p t d", t=4),
                                rinv[:, 4 * h:4 * h + 4].unsqueeze(2).to_broadcast([P, 4, HD]), ALU.mult).then_inc(do_rd, 1)

            dsa_max(0)
            dsa_max(1)
            sb_out(NH - 1)
            for i in range(NS):
                if i % 2 == 0:
                    dsa_move(i)
                if i % 8 == 2 and i // 8 + 1 < 4:
                    dsa_low(i // 8 + 1)
                if i + 2 < NS:
                    dsa_max(i + 2)
                if i >= 4 and i % 4 == 1:
                    dsa_out(i // 4 - 1)
            dsa_out(NH - 1)

            def mixer_low(l):
                for k in range(KT):
                    dve.wait_ge(ao_hi, 8 * l + k + 1)
                    V.tensor_tensor(uL[:, k], X[:, k % 3, :], uH[:, k].bitcast(F32), ALU.subtract).then_inc(ao_lo, 1)

            def fold(L):
                l = L // 2
                gain = cols[:, (VLMG, VLFG)[L % 2] + 8 * l:(VLMG, VLFG)[L % 2] + 8 * l + 8]
                bias = cols[:, (VLMB, VLFB)[L % 2] + 8 * l:(VLMB, VLFB)[L % 2] + 8 * l + 8]
                f = [fcol[:, L, i] for i in range(4)]
                if L < 3:
                    sc_, sh = (mod(l, 4), mod(l, 3)) if L % 2 == 0 else (mod(1, 1), mod(1, 0))
                    link(V.scalar_tensor_tensor(f[0], sc_, 1.0, gain, ALU.add, ALU.mult))
                    link(V.scalar_tensor_tensor(f[1], sc_, 1.0, bias, ALU.add, ALU.mult))
                    link(V.tensor_tensor(f[1], f[1], sh, ALU.add))
                a = ALPHA if L < 3 else 1.0
                link(V.tensor_scalar(f[2], gain, a, None, ALU.mult))
                link(V.tensor_scalar(f[3], bias, a, None, ALU.mult))

            def add_out(L, n, j, a):
                dve.wait_ge(chunk_done, n + 1)
                for m in range(2):
                    x = 2 * j + m
                    V.scalar_tensor_tensor(xT[:, x], acc[:, 2 * (a % 2) + m, :], g1p[:, L, x:x + 1], xT[:, x],
                                           ALU.mult, ALU.add).then_inc(acc_read[a % 2], 1)

            def out_steps(L, l, n0):
                dve.wait_ge(ax_rd, 8 * (L + 1))
                link(V.tensor_scalar(g1p[:, L], mod(l, 2), 1.0, None, ALU.add))
                for j in range(4):
                    n = n0 + j
                    add_out(L, n, j, use_of(n))
                    if l == 0 and 10 + j in TURNS:
                        group_columns(TURNS[10 + j])
                    split_low(n + 2)

            def norm(L, a):
                acc_gone(dve, a)
                acc_gone(dve, a - 1)
                dve.wait_ge(ln_mean, L + 1)
                for x in range(8):
                    V.tensor_tensor(xT[:, x], xT[:, x], X[:, 0, :], ALU.subtract).then_inc(ln_d, 1)
                fold(L)
                dve.wait_ge(ln_rs, 2 * L + 2)
                for x in range(8):
                    V.tensor_tensor(xT[:, x], xT[:, x], X[:, 2, :] if L < 3 else tmp[:, 0], ALU.mult).then_inc(ln_t, 1)
                    if L < 3:
                        dve.wait_ge(ln_t, 8 * L + x + 1)
                        i = U_LN[L] + x
                        scaled(i, x, fcol[:, L, 0], fcol[:, L, 1])
                        if x:
                            low(i - 1, uL[:, x - 1], uH[:, x - 1])
                if L < 3:
                    low(U_LN[L] + 7, uL[:, 7], uH[:, 7])

            mixer_low(0)
            dve.wait_ge(mod_rd, 12)
            out_steps(0, 0, NC1 + 10)
            dve.wait_ge(mod_rd, 16)
            norm(0, use_of(NC1 + 13))

            def feed_forward(l):
                n0, a0 = N_UP[l], use_of(N_UP[l])
                L = 2 * l + 1
                if l == 0:
                    dve.wait_ge(mod_rd, 18)
                    V.tensor_scalar(g1p[:, 1], mod(0, 5), 1.0, None, ALU.add).then_inc(h_lo, 1)
                with dve.Fori(0, 11) as i:
                    if l == 0:
                        dve.wait_ge(modT, i + 19)
                        V.tensor_tensor(mod2[:, bass.ds(4 * i + 48, 4)], modp[:, 0:4],
                                        cols[:, bass.ds(4 * i + (VBM2 + 48), 4)], ALU.add).then_inc(mod_rd, 1)
                    p = n0 % 2
                    dve.wait_ge(hi_done, 2 * i + (n0 + 3))
                    V.tensor_tensor(wlo[:, p, :], wraw[:, p, :], whi[:, p, :].bitcast(F32), ALU.subtract).then_inc(lo_done, 1)
                    p = 1 - p
                    dve.wait_ge(chunk_done, 2 * i + (n0 + 2))
                    dve.wait_ge(acc_read[a0 % 2], 2 * i + acc_count(a0))
                    V.tensor_tensor(tmp[:, :, :], tmp[:, :, :], acc[:, 2 * ((a0 + 1) % 2):2 * ((a0 + 1) % 2) + 2, :],
                                    ALU.mult).then_inc(acc_read[(a0 + 1) % 2], 2)
                    dve.wait_ge(hi_done, 2 * i + (n0 + 4))
                    V.tensor_tensor(wlo[:, p, :], wraw[:, p, :], whi[:, p, :].bitcast(F32), ALU.subtract).then_inc(lo_done, 1)
                    dve.wait_ge(h_hi, i + (11 * l + 1))
                    fl = [w[:, :, :].rearrange("p k n -> p (k n)")[:, bass.ds(i * 1024, 1024)] for w in (hL, hH)]
                    V.tensor_tensor(fl[0], tmp[:, :, :].rearrange("p k n -> p (k n)"), fl[1].bitcast(F32),
                                    ALU.subtract).then_inc(h_lo, 1)
                if l == 0:
                    group_columns(29)
                if l == 0:
                    dve.wait_ge(h_lo, 1)
                else:
                    link(V.tensor_scalar(g1p[:, L], mod(l, 5), 1.0, None, ALU.add))
                dve.wait_ge(ax_rd, 8 * (L + 1))
                for j in range(4):
                    for c in range(3):
                        n = N_DN[l] + 3 * j + c
                        if c == 2:
                            add_out(L, n, j, A_DN[l] + j)
                        if n + 2 < NCH:
                            split_low(n + 2)
                dve.wait_ge(mod_rd, 30)
                norm(L, A_DN[l] + 3)

            feed_forward(0)

            for e in range(12):
                n = N_ODD + e
                a = use_of(n)
                dve.wait_ge(chunk_done, n + 1)
                V.tensor_copy(T1[:, 2:4, WCOL * e:WCOL * e + WCOL], pair[a % 2][:, 512:1024].rearrange("p (t n) -> p t n", t=2))\
                    .then_inc(acc_read[a % 2], 1)
                if e < 11:
                    split_low(n + 2)
                if e == 3:
                    dve.wait_ge(odd_in, 80)
                    pr = lv[:, 0:4:2, :]
                    link(V.tensor_tensor(pr, pr, lv[:, 1:4:2, :], ALU.mult))
                    V.tensor_reduce(lam[:, 0:2], pr, AX.X, ALU.add).then_inc(lam_rd, 1)
                if e == 6:
                    dve.wait_ge(lam_rd, 2)
                    link(V.tensor_tensor(lam[:, 2:3], lam[:, 1:2], lam[:, 0:1], ALU.subtract))
                    link(V.tensor_scalar(lam[:, 3:4], lam[:, 2:3], -LAMBDA_INIT, None, ALU.add))


            def diff_low(h, e):
                job_low(13 + 2 * h + e, 4 * (h % 2), 6 if (h, e) == (0, 1) else 7, e == 1)

            def diff_max(i):
                w = (i % 4 + 1) * P
                dve.wait_ge(fs_rd, i + 1)
                if i >= 4:
                    dve.wait_ge(fp_rd, i - 3)
                V.tensor_reduce(fmx[:, 2 * (i % 4):2 * (i % 4) + 2], ps[:, 2 * (i % 2):2 * (i % 2) + 2, 0:w], AX.X, ALU.max,
                                negate=True).then_inc(fmx_rd, 1)

            def diff_combine(i):
                w = (i % 4 + 1) * P
                f = finv[:, i % 4:i % 4 + 1]
                dve.wait_ge(fp_rd, i + 1)
                dve.wait_ge(fp2_rd, i + 1)
                link(V.reciprocal(f, fsum[:, i % 4:i % 4 + 1]))
                link(V.scalar_tensor_tensor(f, f, lam[:, 3:4], rsum[:, i:i + 1], ALU.mult, ALU.mult))
                p0, p1 = pdf[:, i % 2, 0, 0:w], pdf[:, i % 2, 1, 0:w]
                V.scalar_tensor_tensor(p0, p1, f, p0, ALU.mult, ALU.add).then_inc(fa_rd, 1)

            def diff_out(h):
                dve.wait_ge(sln_rs, h + 1)
                ms = nmx[:, 4 * h:4 * h + 4]
                link(V.tensor_tensor(ms, ms, rinv[:, 4 * h:4 * h + 4], ALU.mult))
                for tt in range(TT):
                    last = V.scalar_tensor_tensor(T1[:, tt, h * P:h * P + P], ps[:, 5 + h % 2, tt * P:tt * P + P], ms[:, tt:tt + 1],
                                                  subg[:, :], ALU.mult, ALU.mult)
                last.then_inc(fo_rd, 1)

            link(V.tensor_scalar(subg[:, :], subg[:, :], 1.0 - LAMBDA_INIT, None, ALU.mult))
            diff_low(0, 0)
            diff_low(0, 1)
            diff_low(1, 0)
            diff_max(0)
            diff_max(1)
            diff_combine(0)
            diff_low(1, 1)
            split_low(N_ODD + 13)
            for i in range(NS):
                if i + 1 < NS:
                    diff_combine(i + 1)
                if i % 4 == 3:
                    V.reciprocal(rinv[:, i - 3:i + 1], rsum[:, i - 3:i + 1]).then_inc(dinv_rd, 1)
                if i + 2 < NS:
                    diff_max(i + 2)
                if i % 4 >= 2 and i // 4 + 2 < NH:
                    diff_low(i // 4 + 2, i % 4 - 2)
                if i >= 4 and i % 4 == 1:
                    diff_out(i // 4 - 1)
            diff_out(NH - 1)

            mixer_low(1)
            out_steps(2, 1, N_ODD + 12)
            norm(2, use_of(N_ODD + 15))
            feed_forward(1)
            for i in range(6):
                tt, half = i % 4, i // 4
                dve.wait_ge(fin_T, i + 1)
                V.tensor_copy(otok[:, tt, half * 512:half * 512 + 512], ps[:, 2 * tt + half, :]).then_inc(fin_v, 1)


_INS = ["x", "c", "ctx", "c_ctx", "w_mod", "b_mod", "norm_w", "w_in", "q_norm_w", "k_norm_w", "conv_w", "conv_b",
        "conv_ln_w", "conv_ln_b", "w_pw", "b_pw", "w_out", "c_2", "positions_2", "w_mod_2", "b_mod_2",
        "w_in_even_2", "w_out_even_2", "w_in_odd_2", "lam_q1_2", "lam_k1_2", "lam_q2_2", "lam_k2_2", "subln_g_2",
        "w_out_odd_2", "ln_mix_g_2", "ln_mix_b_2", "w_gate_2", "w_up_2", "w_down_2", "ln_ffn_g_2", "ln_ffn_b_2"]


def shape_tables():
    tok = np.arange(SEQ, dtype=np.float32)
    freqs = (np.float32(10000.0) ** (-np.arange(0, 32, 2, dtype=np.float32) / np.float32(32))).astype(np.float32)
    r = np.floor(tok / 64).astype(np.float32)[:, None] * freqs[None]
    c = (tok % 64).astype(np.float32)[:, None] * freqs[None]
    ang = np.concatenate([r, c], axis=1)
    inv2 = (np.float32(10000.0) ** (-np.arange(0, 64, 2, dtype=np.float32) / np.float32(64))).astype(np.float32)
    return {"inv2": inv2[None], "cos1": np.cos(ang).astype(np.float32), "sin1": np.sin(ang).astype(np.float32)}


def kernel(**inputs):
    import numpy as _np
    import concourse.bacc as _bacc
    from concourse import mybir as _mybir
    from concourse.bass_utils import run_bass_kernel_spmd as _run

    nc = _bacc.Bacc("TRN2", target_bir_lowering=False, num_devices=1)
    arrays, t = {}, {}
    given = {name: _np.ascontiguousarray(inputs[name]) for name in _INS}
    given.update(shape_tables())
    for name, a in given.items():
        arrays[f"in_{name}_dram"] = a
        t[name] = nc.dram_tensor(f"in_{name}_dram", a.shape, _mybir.dt.from_np(a.dtype), kind="ExternalInput").ap()
    out = nc.dram_tensor("out_0_dram", (1, SEQ, D), _mybir.dt.float32, kind="ExternalOutput").ap()
    program(nc, t, out)
    r = _run(nc, [arrays], core_ids=[0])
    return r.results[0]["out_0_dram"]
```
